# Optimizing a Trainium2 kernel written in Bass

```python
import jax
import jax.numpy as jnp
from jax import lax
import numpy as np

D_MODEL = 1024
BATCH = 1
SEQ = 512
DEPTH = 2
DEC_BATCH = 8
DEC_SEQ = 4
PAST_LEN = 256
PAGE_SIZE = 128

N_A = DEPTH // 2
N_B = DEPTH - N_A
RWKV_HEAD = 64
RWKV_H = D_MODEL // RWKV_HEAD
LORA_DECAY = 64
LORA_A = 64
LORA_V = 32
LORA_G = 160
GN_EPS = 64e-5
N_HEADS = 16
HEAD_DIM = 64
N_KV = 4
GROUP = N_HEADS // N_KV
CMP_STRIDE = 16
CMP_LEN = 2 * CMP_STRIDE
CMP_HID = 2 * HEAD_DIM
SEL_BLOCK = 64
N_SEL = 16
WINDOW = 512
Q_BLOCK = 64
QROW_BUDGET = 256
D_FF = 2816
RMS_EPS = 1e-6
NEG_INF = -1e30
FORCED_SCORE = 1e4

kernel_name = 'yoco_rwkv7_nsa_macaron_step'

RWKV_PARAMS = ('rw_mu', 'rw_w_rkv', 'rw_w0', 'rw_w1', 'rw_w2', 'rw_a0', 'rw_a1', 'rw_a2',
               'rw_g1', 'rw_g2', 'rw_k_k', 'rw_k_a', 'rw_r_k', 'rw_lnx_w', 'rw_lnx_b', 'rw_w_o')

def rms_norm(x, g):
    xf = x.astype(jnp.float32)
    y = xf * lax.rsqrt(jnp.mean(xf * xf, axis=-1, keepdims=True) + RMS_EPS)
    return (y * g.astype(jnp.float32)).astype(x.dtype)

def swiglu(x, w_in, w_out):
    gate, up = jnp.split(x @ w_in, 2, axis=-1)
    return (jax.nn.silu(gate) * up) @ w_out

def alibi_slopes(n):
    return jnp.exp2(-8.0 * jnp.arange(1, n + 1, dtype=jnp.float32) / n)

def query_block(n_rows, tq):
    return max(1, min(Q_BLOCK, tq, QROW_BUDGET // n_rows))

def rwkv7_mix(x, shift0, s0, v_first, ap, vres):
    (mu, w_rkv, w0, w1, w2, a0, a1, a2, g1, g2, k_k, k_a, r_k, lnx_w, lnx_b, w_o) = ap
    B, T, D = x.shape
    x_prev = jnp.concatenate([shift0[:, None, :].astype(x.dtype), x[:, :-1]], axis=1)
    xx = x_prev - x
    xs = x[None] + xx[None] * mu[:, None, None, :]
    r, k, v = jnp.einsum('cbtd,cde->cbte', xs[:3], w_rkv)
    xv, xw, xa, xg = xs[2], xs[3], xs[4], xs[5]
    w = -jax.nn.softplus(-(w0 + jnp.tanh(xw @ w1) @ w2)) - 0.5
    a = jax.nn.sigmoid(a0 + (xa @ a1) @ a2)
    g = jax.nn.sigmoid(xg @ g1) @ g2
    if vres is None:
        v_first = v
    else:
        v0, v1, v2 = vres
        v = v + (v_first - v) * jax.nn.sigmoid(v0 + (xv @ v1) @ v2)

    def heads(t):
        return t.astype(jnp.float32).reshape(B, T, RWKV_H, RWKV_HEAD)

    kk = heads(k * k_k)
    kk = kk * lax.rsqrt(jnp.maximum(jnp.sum(kk * kk, axis=-1, keepdims=True), 1e-24))
    k = k * (1.0 + (a - 1.0) * k_a)
    rh, kh, vh, ah = heads(r), heads(k), heads(v), heads(a)
    decay = jnp.exp(-jnp.exp(heads(w)))

    def tm(t):
        return jnp.swapaxes(t, 0, 1)

    def step(S, inp):
        r_t, w_t, k_t, v_t, a_t, b_t = inp
        sa = jnp.einsum('bhij,bhj->bhi', S, a_t)
        S = S * w_t[:, :, None, :] + sa[..., None] * b_t[:, :, None, :] + v_t[..., None] * k_t[:, :, None, :]
        return S, jnp.einsum('bhij,bhj->bhi', S, r_t)

    S_T, ys = lax.scan(step, s0.astype(jnp.float32),
                       (tm(rh), tm(decay), tm(kh), tm(vh), tm(-kk), tm(kk * ah)))
    y = jnp.swapaxes(ys, 0, 1)
    mean = jnp.mean(y, axis=-1, keepdims=True)
    var = jnp.mean(jnp.square(y - mean), axis=-1, keepdims=True)
    y = ((y - mean) * lax.rsqrt(var + GN_EPS)).reshape(B, T, D) * lnx_w + lnx_b
    bonus = jnp.sum(rh * kh * r_k.astype(jnp.float32), axis=-1, keepdims=True) * vh
    y = y + bonus.reshape(B, T, D)
    out = (y.astype(x.dtype) * g) @ w_o
    return out, x[:, -1], S_T.astype(s0.dtype), v_first

def nsa_compress(k, pos, w1, w2):
    B, tkp = k.shape[:2]
    n = tkp // CMP_STRIDE
    half = CMP_STRIDE * HEAD_DIM
    ch = k.reshape(B, n, CMP_STRIDE, N_KV, HEAD_DIM).transpose(0, 1, 3, 2, 4).reshape(B, n, N_KV, half)
    w1 = w1.astype(jnp.float32)
    h_lo = ch @ w1[:half]
    h_hi = ch @ w1[half:]
    h_hi = jnp.concatenate([h_hi[:, 1:], jnp.zeros_like(h_hi[:, :1])], axis=1)
    h = jax.nn.gelu(h_lo + h_hi + pos.astype(jnp.float32).reshape(-1) @ w1)
    return h @ w2.astype(jnp.float32)

def nsa_prepare(kc, vc, ks, vs, kw, vw, tq, cmp_pos, cmp_w1, cmp_w2):
    B, tk_pad = kc.shape[:2]
    k_cmp = nsa_compress(kc, cmp_pos[0], cmp_w1[0], cmp_w2[0]).transpose(0, 2, 1, 3)
    v_cmp = nsa_compress(vc, cmp_pos[1], cmp_w1[1], cmp_w2[1]).transpose(0, 2, 1, 3)
    n_sel = tk_pad // SEL_BLOCK

    def blocks(t):
        return t.reshape(B, n_sel, SEL_BLOCK, N_KV, HEAD_DIM).transpose(0, 3, 1, 2, 4)

    qb = query_block(B, tq)
    tq_pad = -(-tq // qb) * qb

    def pad_w(t):
        return jnp.pad(t, ((0, 0), (WINDOW, tq_pad - tq), (0, 0), (0, 0)))

    return (k_cmp, v_cmp, blocks(ks), blocks(vs), pad_w(kw), pad_w(vw))

def nsa_attend(q, gates, shared, q_pos0, w_pos0):
    k_cmp, v_cmp, ksb, vsb, kwp, vwp = shared
    B, TQ = q.shape[:2]
    NC, NS = k_cmp.shape[2], ksb.shape[2]
    n_top = min(N_SEL, NS)
    qb = query_block(B, TQ)
    n_qb = -(-TQ // qb)
    TQp = n_qb * qb
    padq = ((0, 0), (0, TQp - TQ), (0, 0), (0, 0))
    qg = jnp.pad(q.astype(jnp.float32) * HEAD_DIM ** -0.5, padq)
    qg = qg.reshape(B, n_qb, qb, N_KV, GROUP, HEAD_DIM).transpose(1, 0, 3, 4, 2, 5)
    gg = jnp.pad(gates, padq).reshape(B, n_qb, qb, N_KV, GROUP, 3).transpose(1, 0, 3, 4, 2, 5)
    slopes = alibi_slopes(N_HEADS).reshape(N_KV, GROUP)[None, :, :, None, None]
    cmp_start = jnp.arange(NC) * CMP_STRIDE
    cmp_end = cmp_start + (CMP_LEN - 1)
    blk = jnp.arange(NS)
    overlap = ((cmp_start[:, None] < (blk[None, :] + 1) * SEL_BLOCK)
               & (cmp_start[:, None] + CMP_LEN > blk[None, :] * SEL_BLOCK)).astype(jnp.float32)
    bi = jnp.arange(B)[:, None, None]
    hi = jnp.arange(N_KV)[None, :, None]
    within = jnp.arange(SEL_BLOCK)
    win_off = jnp.arange(WINDOW + qb)

    def one_block(args):
        i, qi, gi = args
        t0 = q_pos0 + i * qb
        t = t0 + jnp.arange(qb)
        d_c = t[:, None] - cmp_end[None, :]
        ok_c = d_c >= 0
        s = jnp.einsum('bkgqd,bknd->bkgqn', qi, k_cmp) - slopes * d_c.astype(jnp.float32)
        p_c = jnp.where(ok_c, jax.nn.softmax(jnp.where(ok_c, s, NEG_INF), axis=-1), 0.0)
        o_c = jnp.einsum('bkgqn,bknd->bkgqd', p_c, v_cmp)
        cur = t // SEL_BLOCK
        imp = jnp.einsum('bkgqn,ns->bkqs', p_c, overlap)
        forced = (blk[None, :] == 0) | (blk[None, :] == cur[:, None]) | (blk[None, :] == cur[:, None] - 1)
        imp = jnp.where(blk[None, :] <= cur[:, None], jnp.where(forced, FORCED_SCORE, imp), -1.0)
        _, idx = lax.top_k(imp, n_top)
        flat = idx.reshape(B, N_KV, qb * n_top)
        kg = ksb[bi, hi, flat].reshape(B, N_KV, qb, n_top * SEL_BLOCK, HEAD_DIM)
        vg = vsb[bi, hi, flat].reshape(B, N_KV, qb, n_top * SEL_BLOCK, HEAD_DIM)
        spos = (idx[..., None] * SEL_BLOCK + within).reshape(B, N_KV, qb, n_top * SEL_BLOCK)
        d_s = (t[:, None] - spos)[:, :, None]
        s = jnp.einsum('bkgqd,bkqsd->bkgqs', qi, kg) - slopes * d_s.astype(jnp.float32)
        p_s = jax.nn.softmax(jnp.where(d_s >= 0, s, NEG_INF), axis=-1)
        o_s = jnp.einsum('bkgqs,bkqsd->bkgqd', p_s, vg)
        start = t0 - w_pos0
        kw = lax.dynamic_slice_in_dim(kwp, start, WINDOW + qb, axis=1)
        vw = lax.dynamic_slice_in_dim(vwp, start, WINDOW + qb, axis=1)
        wpos = t0 - WINDOW + win_off
        d_w = t[:, None] - wpos[None, :]
        ok_w = (d_w >= 0) & (d_w <= WINDOW) & (wpos[None, :] >= w_pos0)
        s = jnp.einsum('bkgqd,bskd->bkgqs', qi, kw) - slopes * d_w.astype(jnp.float32)
        p_w = jax.nn.softmax(jnp.where(ok_w, s, NEG_INF), axis=-1)
        o_w = jnp.einsum('bkgqs,bskd->bkgqd', p_w, vw)
        return gi[..., 0:1] * o_c + gi[..., 1:2] * o_s + gi[..., 2:3] * o_w

    o = lax.map(one_block, (jnp.arange(n_qb), qg, gg))
    return o.transpose(1, 0, 4, 2, 3, 5).reshape(B, TQp, N_HEADS * HEAD_DIM)[:, :TQ]

def nsa_layer(xn, w_in, w_o, shared, q_pos0, w_pos0):
    B, T, _ = xn.shape
    nq = N_HEADS * HEAD_DIM
    z = xn @ w_in
    q = z[..., :nq].reshape(B, T, N_HEADS, HEAD_DIM)
    gates = jax.nn.sigmoid(z[..., nq:].astype(jnp.float32)).reshape(B, T, N_HEADS, 3)
    o = nsa_attend(q, gates, shared, q_pos0, w_pos0)
    return o.astype(xn.dtype) @ w_o

def trunk(x, shift_in, wkv_in, past_cs, win_buf, win_keep, q_pos0, P):
    B, T, _ = x.shape
    h = x
    shifts, states = [], []
    v_first = None
    shared = None
    w_pos0 = 0
    cs_new = None
    win_state = None
    for l in range(DEPTH):
        g = P['norm_g'][l]
        h = h + 0.5 * swiglu(rms_norm(h, g[0]), P['ffn_w_in'][l, 0], P['ffn_w_out'][l, 0])
        xn = rms_norm(h, g[1])
        if l < N_A:
            ap = tuple(P[n][l] for n in RWKV_PARAMS)
            vres = None if l == 0 else (P['rw_v0'][l - 1], P['rw_v1'][l - 1], P['rw_v2'][l - 1])
            mix, sh, st, v_first = rwkv7_mix(xn, shift_in[l], wkv_in[l], v_first, ap, vres)
            shifts.append(sh)
            states.append(st)
        else:
            mix = nsa_layer(xn, P['b_w_in'][l - N_A], P['b_w_o'][l - N_A], shared, q_pos0, w_pos0)
        h = h + mix
        h = h + 0.5 * swiglu(rms_norm(h, g[2]), P['ffn_w_in'][l, 1], P['ffn_w_out'][l, 1])
        if l == N_A - 1:
            kv = (rms_norm(h, P['kv_norm_g']) @ P['kv_w']).reshape(B, T, 6, N_KV, HEAD_DIM)
            cs_new = kv[:, :, :4]
            win_new = kv[:, :, 4:]
            tk = q_pos0 + T
            tk_pad = -(-tk // SEL_BLOCK) * SEL_BLOCK
            zpad = jnp.zeros((B, tk_pad - tk, N_KV, HEAD_DIM), jnp.float32)
            rows = []
            for c in range(4):
                past = [] if past_cs is None else [past_cs[:, :, c].astype(jnp.float32)]
                rows.append(jnp.concatenate(past + [cs_new[:, :, c].astype(jnp.float32), zpad], axis=1))
            win_all = win_new if win_buf is None else jnp.concatenate(
                [win_buf.astype(win_new.dtype), win_new], axis=1)
            w_pos0 = tk - win_all.shape[1]
            win_state = win_all[:, win_all.shape[1] - win_keep:]
            wf = win_all.astype(jnp.float32)
            shared = nsa_prepare(rows[0], rows[1], rows[2], rows[3], wf[:, :, 0], wf[:, :, 1], T,
                                 P['cmp_pos'], P['cmp_w1'], P['cmp_w2'])
    y = rms_norm(h, P['final_g'])
    return y, jnp.stack(shifts), jnp.stack(states), cs_new, win_state

def setup_inputs(seed: int = 0) -> dict:
    key = jax.random.key(seed)
    keys = jax.random.split(key, 64)
    counter = iter(range(64))

    def nk():
        return keys[next(counter)]

    def nrm(shape, scale=1.0):
        return scale * jax.random.normal(nk(), shape, jnp.float32)

    D = D_MODEL
    n_pages = PAST_LEN // PAGE_SIZE
    n_used = DEC_BATCH * n_pages
    n_pool = (5 * n_used + 3) // 4
    perm = jax.random.permutation(nk(), n_pool)
    page_table = perm[:n_used].reshape(DEC_BATCH, n_pages).astype(jnp.int32)
    ramp = (jnp.arange(D, dtype=jnp.float32) / (D - 1)) ** 1.2
    n_q = N_HEADS * HEAD_DIM
    return {
        'x_prompt': nrm((BATCH, SEQ, D)),
        'x_sample': nrm((DEC_BATCH, DEC_SEQ, D)),
        'cache_cs': nrm((n_pool, PAGE_SIZE, 4, N_KV, HEAD_DIM)),
        'cache_win': nrm((DEC_BATCH, min(WINDOW, PAST_LEN), 2, N_KV, HEAD_DIM)),
        'state_shift': nrm((N_A, DEC_BATCH, D)),
        'state_wkv': nrm((N_A, DEC_BATCH, RWKV_H, RWKV_HEAD, RWKV_HEAD), 0.5),
        'page_table': page_table,
        'norm_g': 1.0 + nrm((DEPTH, 3, D), 0.02),
        'ffn_w_in': nrm((DEPTH, 2, D, 2 * D_FF), D ** -0.5),
        'ffn_w_out': nrm((DEPTH, 2, D_FF, D), D_FF ** -0.5),
        'rw_mu': jax.random.uniform(nk(), (N_A, 6, D), jnp.float32),
        'rw_w_rkv': nrm((N_A, 3, D, D), D ** -0.5),
        'rw_w0': -6.5 + 5.0 * ramp + nrm((N_A, D), 0.1),
        'rw_w1': nrm((N_A, D, LORA_DECAY), D ** -0.5),
        'rw_w2': nrm((N_A, LORA_DECAY, D), 0.05),
        'rw_a0': nrm((N_A, D), 0.1),
        'rw_a1': nrm((N_A, D, LORA_A), D ** -0.5),
        'rw_a2': nrm((N_A, LORA_A, D), 0.1 * LORA_A ** -0.5),
        'rw_g1': nrm((N_A, D, LORA_G), D ** -0.5),
        'rw_g2': nrm((N_A, LORA_G, D), LORA_G ** -0.5),
        'rw_k_k': 0.85 + nrm((N_A, D), 0.05),
        'rw_k_a': 1.0 + nrm((N_A, D), 0.05),
        'rw_r_k': nrm((N_A, RWKV_H, RWKV_HEAD), 0.1),
        'rw_lnx_w': 1.0 + nrm((N_A, D), 0.02),
        'rw_lnx_b': nrm((N_A, D), 0.02),
        'rw_w_o': nrm((N_A, D, D), D ** -0.5),
        'rw_v0': 1.0 + nrm((N_A - 1, D), 0.1),
        'rw_v1': nrm((N_A - 1, D, LORA_V), D ** -0.5),
        'rw_v2': nrm((N_A - 1, LORA_V, D), 0.1 * LORA_V ** -0.5),
        'kv_norm_g': 1.0 + nrm((D,), 0.02),
        'kv_w': nrm((D, 6 * N_KV * HEAD_DIM), D ** -0.5),
        'cmp_pos': nrm((2, CMP_LEN, HEAD_DIM), 0.1),
        'cmp_w1': nrm((2, CMP_LEN * HEAD_DIM, CMP_HID), (CMP_LEN * HEAD_DIM) ** -0.5),
        'cmp_w2': nrm((2, CMP_HID, HEAD_DIM), CMP_HID ** -0.5),
        'b_w_in': nrm((N_B, D, n_q + 3 * N_HEADS), D ** -0.5),
        'b_w_o': nrm((N_B, n_q, D), n_q ** -0.5),
        'final_g': 1.0 + nrm((D,), 0.02),
    }

def reference(x_prompt, x_sample, cache_cs, cache_win, state_shift, state_wkv, page_table,
              norm_g, ffn_w_in, ffn_w_out, rw_mu, rw_w_rkv, rw_w0, rw_w1, rw_w2, rw_a0, rw_a1,
              rw_a2, rw_g1, rw_g2, rw_k_k, rw_k_a, rw_r_k, rw_lnx_w, rw_lnx_b, rw_w_o, rw_v0,
              rw_v1, rw_v2, kv_norm_g, kv_w, cmp_pos, cmp_w1, cmp_w2, b_w_in, b_w_o, final_g):
    P = dict(norm_g=norm_g, ffn_w_in=ffn_w_in, ffn_w_out=ffn_w_out, rw_mu=rw_mu,
             rw_w_rkv=rw_w_rkv, rw_w0=rw_w0, rw_w1=rw_w1, rw_w2=rw_w2, rw_a0=rw_a0,
             rw_a1=rw_a1, rw_a2=rw_a2, rw_g1=rw_g1, rw_g2=rw_g2, rw_k_k=rw_k_k, rw_k_a=rw_k_a,
             rw_r_k=rw_r_k, rw_lnx_w=rw_lnx_w, rw_lnx_b=rw_lnx_b, rw_w_o=rw_w_o, rw_v0=rw_v0,
             rw_v1=rw_v1, rw_v2=rw_v2, kv_norm_g=kv_norm_g, kv_w=kv_w, cmp_pos=cmp_pos,
             cmp_w1=cmp_w1, cmp_w2=cmp_w2, b_w_in=b_w_in, b_w_o=b_w_o, final_g=final_g)
    bp, tp = x_prompt.shape[:2]
    zero_shift = jnp.zeros((N_A, bp, D_MODEL), x_prompt.dtype)
    zero_wkv = jnp.zeros((N_A, bp, RWKV_H, RWKV_HEAD, RWKV_HEAD), jnp.float32)
    y_prompt, p_shift, p_wkv, p_cs, p_win = trunk(
        x_prompt, zero_shift, zero_wkv, None, None, min(WINDOW, tp), 0, P)
    n_seq, n_pages = page_table.shape
    past_len = n_pages * cache_cs.shape[1]
    past_cs = cache_cs[page_table].reshape(n_seq, past_len, 4, N_KV, HEAD_DIM)
    y_sample, s_shift, s_wkv, s_cs, s_win = trunk(
        x_sample, state_shift, state_wkv, past_cs, cache_win, cache_win.shape[1], past_len, P)
    return (y_prompt, y_sample, p_shift, p_wkv, p_cs, p_win, s_shift, s_wkv, s_cs, s_win)


_drawn_inputs = setup_inputs


def setup_inputs(seed=0):
    import zlib

    import numpy as np

    out = dict(_drawn_inputs(seed))
    spreads = {}
    factors = {'rw_w1': 4.582,
     'rw_w2': 4.652,
     'rw_lnx_w': 5.725,
     'rw_lnx_b': 13.202,
     'kv_norm_g': 8.531,
     'final_g': 7.223,
     'cmp_pos': 5.845}
    for name, (base, spread) in spreads.items():
        noise = np.random.default_rng([zlib.crc32(name.encode()), seed]).standard_normal(out[name].shape)
        drawn = base * np.exp(spread * noise) if base else spread * noise
        out[name] = jnp.asarray(drawn.astype(out[name].dtype))
    for name, factor in factors.items():
        out[name] = (out[name] * factor).astype(out[name].dtype)
    return out
```

```python
import math
from contextlib import ExitStack

import numpy as np

import concourse.bass as bass
from concourse import mybir

F32 = mybir.dt.float32
F32R = mybir.dt.float32r
I32 = mybir.dt.int32
ALU = mybir.AluOpType
ACT = mybir.ActivationFunctionType
AX = mybir.AxisListType.X

P = 128
D = 1024
DT = D // P
SEQ, DEC_B, DEC_T = 512, 8, 4
TOK = SEQ + DEC_B * DEC_T
HALF = TOK // 2
DFF = 2816
FT = DFF // P
FTA = 12
FTB = FT - FTA
NH, HD, NKV = 16, 64, 4
PAST, PAGE = 256, 128
NPG = PAST // PAGE
CH = 64
NCMP = SEQ // 16
CMPTOK = SEQ + DEC_B * PAST
NBLK = CMPTOK // 16 - 1
RMS_EPS, GN_EPS = 1e-6, 64e-5
DECAY = math.exp(-0.5)
NEG = -1e30
SLOT = DT * TOK
RAW = 2 * D
EV = DT + 1

H0 = 0
XN = SLOT
XH, XL = SLOT, 2 * SLOT
HH = 3 * SLOT
HL = HH + FTA * TOK
WH = HL + FTA * TOK
WL = WH + 2 * RAW
FFN_END = WL + 2 * RAW
XR = HH
S_A, S_R, S_B, S_K, S_V, S_XR, S_XK = (i * SLOT for i in (1, 2, 3, 4, 5, 6, 7))
LORA = 8 * SLOT
GS = LORA + 4352
SHIFT0 = GS + 2 * TOK
G2 = LORA + 5632
BC = G2 + 2048
CHB = S_XR
CMPT = 2 * SLOT
KV = CMPT + 4 * CMPTOK
CSM = WH
ARENA = 10 * SLOT
CW1 = ARENA - 64 * P
TAIL = FFN_END
KEYS = CW1
VTOK = KEYS + 4 * TOK
ATAB = VTOK + 2560
KSLC_C, VSLC_C, VWIN_C = XH, XH + 4096, XR
QT = XR + SLOT
ATT = QT + SLOT
SBUF = ATT
KWIN_C = WH
PTB = KWIN_C + 4096

STAGES, _k, _ks = {}, 0, 0


def _stages(*stages):
    global _k, _ks
    for name, pairs, split in stages:
        STAGES[name] = (_k, pairs, _ks if split else None)
        _k += pairs
        _ks += pairs if split else 0


def _ffn_stages(f):
    return ((f"inA{f}", FTA // 2, True), (f"outA{f}", DT // 2, True),
            (f"inB{f}", FTB // 2, True), (f"outB{f}", DT // 2, True))


_stages(*_ffn_stages(0), ("v", 2, False), ("rk", 4, False), ("wo", 2, False), *_ffn_stages(1),
        ("kv", 3, False), *_ffn_stages(2), ("q", 2, True), ("bo", 2, True), *_ffn_stages(3))
COLS = {"inA": 2 * D, "inB": 2 * D, "outA": FTA * P, "outB": FTB * P, "q": 2 * D, "bo": 2 * D}


def cols_of(name):
    return COLS[name.rstrip("0123")]


def end_of(name):
    return STAGES[name][0] + STAGES[name][1]


C_ID, C_ONE, C_BLK, C_HSEL, C_RESET = 0, 128, 256, 384, 512
C_MP = C_RESET + TOK
C_MD = C_MP + 9 * 64
C_I = C_MD + 5 * 32
C_SEQ = C_I + 64
C_PAR = C_SEQ + 8
(Q_G00, Q_G01, Q_G02, Q_G10, Q_G11, Q_G12, Q_KVN, Q_FIN, Q_MU, Q_W0, Q_A0, Q_KK, Q_KA, Q_RK, Q_LNW,
 Q_LNB) = (0, 1, 2, 3, 4, 5, 6, 7, 8, 14, 15, 16, 17, 18, 19, 20)
NPAR = 22
C_ALL = C_PAR + NPAR * 8
M_STRICT, M_INCL, M_LOW, M_UP = 0, 1, 2, 3

T_D0, T_DC, T_DH, T_DD = 0, 512, 640, 640 + 1280
T_PT2 = T_DD + 1024
LEVELS_P, LEVELS_D = (2, 4, 8, 16, 32), (2,)


def head_of(i, par):
    return (2 * (i // 4) + par) * 4 + i % 4


SLOPES = [float(np.exp2(np.float32(-8.0 * (h + 1) / NH))) for h in range(NH)]


def constants():
    c = np.zeros((P, C_ALL), np.float32)
    c[:, C_ID:C_ID + P] = np.eye(P)
    c[:, C_ONE:C_ONE + P] = 1.0
    same = (np.arange(P)[:, None] // HD) == (np.arange(P)[None, :] // HD)
    c[:, C_BLK:C_BLK + P] = same
    hs = np.zeros((P, DT, NH), np.float32)
    for ft in range(DT):
        hs[np.arange(P), ft, 2 * ft + np.arange(P) // HD] = 1.0
    c[:, C_HSEL:C_HSEL + DT * NH] = hs.reshape(P, -1)
    reset = np.ones(TOK, np.float32)
    reset[0:SEQ:CH] = 0.0
    reset[SEQ::DEC_T] = 0.0
    c[:, C_RESET:C_RESET + TOK] = reset
    t, s = np.arange(CH)[:, None], np.arange(CH)[None, :]

    def level(m, t, s):
        return ((t // m) % 2 == 1) & (s // m == t // m - 1)

    mp = [(t < s), (t <= s), level(1, t, s)] + [level(m, s, t) for m in (1,) + LEVELS_P]
    for n, m in enumerate(mp):
        c[:, C_MP + n * CH:C_MP + (n + 1) * CH] = np.tile(m, (2, 1))
    n32 = np.arange(32)
    t, s = n32[:, None], n32[None, :]
    own = t // DEC_T == s // DEC_T
    md = [own & (t < s), own & (t <= s), level(1, t, s)] + [level(m, s, t) for m in (1,) + LEVELS_D]
    for n, m in enumerate(md):
        c[0:32, C_MD + n * 32:C_MD + (n + 1) * 32] = m
    c[:, C_I:C_I + CH] = np.tile(np.eye(CH), (2, 1))
    c[0:32, C_SEQ:C_SEQ + DEC_B] = n32[:, None] // DEC_T == np.arange(DEC_B)[None, :]
    expand = np.zeros((NH, DT, P), np.float32)
    for h in range(NH):
        expand[h, h // 2, (h % 2) * HD:(h % 2) * HD + HD] = 1.0
    p = np.arange(P)[:, None]
    d0 = np.arange(SEQ)[None, :] - 384 - p
    att = np.zeros((P, T_PT2), np.float32)
    att[:, T_D0:T_D0 + SEQ] = np.where(d0 <= 0, d0, NEG)
    dc = (16 * np.arange(NCMP)[None, None, :] + 31) - (P * np.arange(4)[None, :, None] + p[:, :, None])
    att[:, T_DC:T_DC + P] = np.where(dc <= 0, dc, NEG).reshape(P, P)
    j, h, tt = np.arange(P) // 64, (np.arange(P) % 64) // DEC_T, np.arange(P) % DEC_T
    slope = np.array(SLOPES, np.float32)[h][:, None]
    pos = (PAST + tt)[:, None]
    dd = np.zeros((P, 4, 192), np.float32)
    for u in range(4):
        b = (2 * u + j)[:, None]
        kb, kn = np.arange(P)[None, :] // 16, np.arange(P)[None, :] % 16
        dist = 16 * kn + 31 - pos
        dd[:, u, 0:P] = np.where((kb == b) & (dist <= 0), dist * slope, NEG)
        nb, nt = np.arange(32)[None, :] // DEC_T, np.arange(32)[None, :] % DEC_T
        dist = nt - tt[:, None]
        new = np.where((nb == b) & (dist <= 0), dist * slope, NEG)
        dd[:, u, 128:160] = new
        dd[:, u, 160:192] = new
    att[:, T_DD:T_DD + 768] = dd.reshape(P, 768)
    att[:, T_DD + 768:T_DD + 1024] = (np.arange(PAST)[None, :] - pos) * slope
    valid = (np.arange(P) >= 31).astype(np.float32)[:, None]
    return c, expand.reshape(NH, D), att, valid


class Steps:

    def __init__(self, engine, sem):
        self.engine, self.sem, self.n = engine, sem, 0

    def do(self, instruction):
        instruction.then_inc(self.sem, 1)
        self.n += 1
        return self.n

    def wait(self, n=None):
        self.engine.wait_ge(self.sem, self.n if n is None else n)


def program(nc, I, O):
    with ExitStack() as ctx:
        def sb(name, shape, dt=F32):
            return ctx.enter_context(nc.sbuf_tensor(name, shape, dt))

        def sem(name):
            return ctx.enter_context(nc.semaphore(name))

        base = -(-nc.sbuf_base // 32) * 32
        arena = sb("arena", [P, ARENA])
        raw = sb("raw", [P, 2, RAW])
        acc = sb("acc", [P, TOK])
        eps = sb("eps", [P, 1])

        def split_at(name, off, *shape):
            return nc.alloc_sbuf_tensor_at(name, [P, *shape], F32R, offset=base + 4 * off)

        xh, xl = split_at("xh", XH, DT, TOK), split_at("xl", XL, DT, TOK)
        hh, hl = split_at("hh", HH, FTA, TOK), split_at("hl", HL, FTA, TOK)
        wh, wl = split_at("wh", WH, 2, RAW), split_at("wl", WL, 2, RAW)
        const = sb("const", [P, C_ALL])
        sg = sb("sg", [P, 2, TOK])
        wc = sb("wc", [P, DT, 16])
        st = sb("st", [P, DT, HD])
        sm = sb("sm", [P, 2, 16])
        cbias = sb("cbias", [P, 4])
        ptab = sb("ptab", [1, DEC_B * NPG], I32)
        pst = ctx.enter_context(nc.psum_tensor("banks", [P, 8, 512], F32))

        def ar(off, *shape, p0=0, p1=P):
            n = 1
            for x in shape:
                n *= x
            v = arena[p0:p1, off:off + n]
            if len(shape) == 2:
                v = v.rearrange("p (a b) -> p a b", a=shape[0])
            elif len(shape) == 3:
                v = v.rearrange("p (a b c) -> p a b c", a=shape[0], b=shape[1])
            elif len(shape) == 4:
                v = v.rearrange("p (a b c d) -> p a b c d", a=shape[0], b=shape[1], c=shape[2])
            return v

        hT, xn = ar(H0, DT, TOK), ar(XN, DT, TOK)
        xr = ar(XR, DT, TOK)
        ident = const[:, C_ID:C_ID + P]
        ones = const[:, C_ONE:C_ONE + P]
        blk = const[:, C_BLK:C_BLK + P]
        hsel = const[:, C_HSEL:C_HSEL + DT * NH].rearrange("p (f h) -> p f h", f=DT)
        reset = const[:, C_RESET:C_RESET + TOK]

        def par(q, ft):
            return const[:, C_PAR + q * 8 + ft:C_PAR + q * 8 + ft + 1]

        def halves(ap):
            return ap.rearrange("p (h c) -> p h c", h=2)

        def bank2(b):
            return pst[:, b:b + 2, 0:HALF]

        xx, xs_w, xs_a, xs_g = ar(S_R, DT, TOK), ar(S_B, DT, TOK), ar(S_K, DT, TOK), ar(S_V, DT, TOK)
        xs_r, xs_k, xs_v = ar(S_XR, DT, TOK), ar(S_XK, DT, TOK), xx
        cumw, sigw, a_t = ar(S_A, DT, TOK), ar(S_B, DT, TOK), ar(S_K, DT, TOK)
        t_a, t_r, t_b, t_k, t_v = (ar(x, DT, TOK) for x in (S_A, S_R, S_B, S_K, S_V))
        t_ar = ar(S_A, 2, DT, TOK)
        w_w1, w_a1, w_g1 = ar(LORA, DT, 64), ar(LORA + 512, DT, 64), ar(LORA + 1024, DT, 160)
        w_w2, w_a2 = ar(LORA + 2304, D, p1=64), ar(LORA + 3328, D, p1=64)
        gs = ar(GS, 2, TOK)
        shift0 = ar(SHIFT0, DT, DEC_B)
        w_g2a, w_g2b = ar(G2, D), ar(G2 + 1024, D, p1=32)
        expand = ar(G2 + 1024, D, p0=32, p1=48)
        bc = ar(BC, TOK, p0=32, p1=48)
        shifts = ar(BC + TOK, DT, 9)
        tmp = [ar(LORA + n * TOK, TOK) for n in range(8)]
        EP, EN, EX, KR, KK_, SQ, KP, RR = tmp

        cb = [ar(CHB + n * 1024, 1024) for n in range(12)]
        V_, B_, K_, ABT, AKT, RBT, RKT, X_, XT, PP, AL, UU = cb
        um = ar(CHB + 7 * 1024, 2, 2, 512, p1=32)
        s0T = ar(S_B, DT, DEC_B, HD)
        y0 = ar(S_K, DT, 2, 32)

        kslc, kwin = ar(KEYS, 2, TOK), ar(KEYS + 2 * TOK, 2, TOK)
        kvT = ar(KV, 12, TOK)
        cmpT = ar(CMPT, 2, 2, CMPTOK)
        cw1 = ar(CW1, 2, 32, P)
        chid = ar(CSM, 4, 2, 160)
        cpos = ar(CSM + 1280, 2, 32, p1=64)
        cw2 = ar(CSM + 1344, 2, HD)
        cred = ar(CSM + 1472, 2, P, p1=64)
        ctmp = ar(CSM + 1728, 32, P, p1=64)
        kcmp = ar(TAIL, 2, 160)
        vcmp_p, vcmp_d = ar(TAIL + 320, 256, p1=32), ar(TAIL + 576, 256)
        v_slc, v_win, v_new = ar(VTOK, 4, 256), ar(VTOK + 1024, 4, 256), ar(VTOK + 2048, 2, 256, p1=32)
        kwin_c, kslc_c = ar(KWIN_C, DEC_B, 2, PAST), ar(KSLC_C, DEC_B * NPG, 2, PAGE)
        vslc_c, vwin_c = ar(VSLC_C, DEC_B * NPG, 256), ar(VWIN_C, DEC_B * NPG, 256)
        qT = oT = ar(QT, DT, TOK)
        sbuf = [ar(SBUF + n * 1056, 1056) for n in range(4)]
        ptb = [ar(PTB + n * 9 * P, 9, P) for n in range(2)]
        att = ar(ATAB, T_PT2)
        wgt = ar(ATT, DT, 48)
        gT = ar(ATT + 384, TOK, p1=48)
        gS = ar(ATAB + T_PT2, 48, p1=32)
        qbd = sg[:].rearrange("p a b -> p (a b)")[:, 0:1024]\
            .rearrange("p (x b r) -> p x b r", x=2, b=DEC_B)

        landed = [sem("slot0_landed"), sem("slot1_landed")]
        multiplied = [sem("slot0_multiplied"), sem("slot1_multiplied")]
        taken = [sem("set0_taken"), sem("set1_taken")]
        w_hi = [sem("slot0_high"), sem("slot1_high")]
        w_split = [sem("slot0_split"), sem("slot1_split")]
        gate_done = [sem("gate0_done"), sem("gate1_done")]
        hid_hi = [sem("hidden0_high"), sem("hidden1_high")]
        hid_done = [sem("hidden0_done"), sem("hidden1_done")]
        acc_step, xr_done, xh_done, xn_split = sem("acc_step"), sem("xr_done"), sem("xh_done"), sem("xn_split")
        oh_done, o_split, keys_kept, eps_set = sem("oh_done"), sem("o_split"), sem("keys_kept"), sem("eps_set")
        x_in = [sem("x0_in"), sem("x1_in")]
        const_in, lora_in = sem("const_in"), sem("lora_in")
        sq_done, sum_done, root_done, xn_done = (
            sem("sq_done"), sem("sum_done"), sem("root_done"), sem("xn_done"))
        xs_done, lora_mm, lora_act, lw_mm, lw_sig, lw_taken, cum_done = (
            sem("xs_done"), sem("lora_mm"), sem("lora_act"), sem("lw_mm"), sem("lw_sig"), sem("lw_taken"),
            sem("cum_done"))
        diff_done, exps_done, rk_copied, kksq_done, kksum_done, kkmax_done, kkroot_done, rk_done, bonus_mm = (
            sem("diff_done"), sem("exps_done"), sem("rk_copied"), sem("kksq_done"), sem("kksum_done"),
            sem("kkmax_done"), sem("kkroot_done"), sem("rk_done"), sem("bonus_mm"))
        temps_free, bonus_done, shifts_done, shift_out = (
            sem("temps_free"), sem("bonus_done"), sem("shifts_done"), sem("shift_out"))
        filled = [sem(f"buf{b}_filled") for b in range(4)]
        emptied = [sem(f"buf{b}_emptied") for b in range(4)]
        pe_order = sem("pe_order")
        al_ready, xt_ready, st_ready = sem("al_ready"), sem("xt_ready"), sem("st_ready")
        s0_in, um_ready, um_used, wkv_ready, wkv_out = (
            sem("s0_in"), sem("um_ready"), sem("um_used"), sem("wkv_ready"), sem("wkv_out"))
        dve_step, act_step, pool_step = sem("dve_step"), sem("act_step"), sem("pool_step")
        gn_sq, gn_root = sem("gn_sq"), sem("gn_root")
        expand_in, chid_zero = sem("expand_in"), sem("chid_zero")
        kv_done, kv_out, cache_cmp_in, cw_in, cprod, cred_done = (
            sem("kv_done"), sem("kv_out"), sem("cache_cmp_in"), sem("cw_in"), sem("cprod"), sem("cred_done"))
        cmp_mm, cmp_ev, win_out = sem("cmp_mm"), sem("cmp_ev"), sem("win_out")
        table_in, caches_in, vwin_in, att_in = sem("table_in"), sem("caches_in"), sem("vwin_in"), sem("att_in")
        vt_mm, vt_ev = sem("vt_mm"), sem("vt_ev")
        gate_w_in, gate_mm, gate_sig, gate_tr, gates_done, gates_d_out, gates_d_in = (
            sem("gate_w_in"), sem("gate_mm"), sem("gate_sig"), sem("gate_tr"), sem("gates_done"),
            sem("gates_d_out"), sem("gates_d_in"))
        bias_ready, gates_s = sem("bias_ready"), sem("gates_s")
        score_mm, score_taken, negmax, exp_done, p_ready = (
            sem("score_mm"), sem("score_taken"), sem("negmax"), sem("exp_done"), sem("p_ready"))
        turned, turn_taken, o_mm, o_taken = sem("turned"), sem("turn_taken"), sem("o_mm"), sem("o_taken")
        qbd_zero, qbd_done = sem("qbd_zero"), sem("qbd_done")
        y_done, y_out = sem("y_done"), sem("y_out")

        g_p = sb("g_p", [P, 4, 48])
        g_d = sb("g_d", [P, 4, 3])
        block = ctx.enter_context(nc.Block())

        @block.sync
        def _(sp):
            def stream(name, src):
                k0, n, _ = STAGES[name]
                with sp.Fori(0, n) as i:
                    for s in range(2):
                        sp.wait_ge(multiplied[s], i + k0)
                        sp.dma_start(raw[:, s, :], src[bass.ds(2 * i + s, 1)].rearrange("o p c -> p (o c)"))\
                            .then_inc(landed[s], 16)

            def stream_split(name, src, c0=0):
                k0, n, ks = STAGES[name]
                cols = cols_of(name)
                with sp.Fori(0, n) as i:
                    for s in range(2):
                        sp.wait_ge(w_split[s], i + ks)
                        sp.dma_start(raw[:, s, 0:cols],
                                     src[bass.ds(2 * i + s, 1)].rearrange("o p c -> p (o c)")[:, c0:c0 + cols])\
                            .then_inc(landed[s], 16)

            def stream_ffn(f):
                stream_split(f"inA{f}", I["w_in"][f, 0:FTA])
                stream_split(f"outA{f}", I["w_out"][f])
                stream_split(f"inB{f}", I["w_in"][f, FTA:FT])
                stream_split(f"outB{f}", I["w_out"][f], FTA * P)

            def plain_done(name):
                for s in range(2):
                    sp.wait_ge(multiplied[s], end_of(name))

            for half in range(2):
                sp.dma_start(hT[:, 4 * half:4 * half + 4], I["x"][:, 4 * half:4 * half + 4])\
                    .then_inc(x_in[half], 16)
            stream_ffn(0)
            stream("v", I["w_v"])
            stream("rk", I["w_rk"])
            stream("wo", I["w_o"])
            plain_done("wo")
            stream_ffn(1)
            stream("kv", I["w_kv"])
            plain_done("kv")
            stream_ffn(2)
            stream_split("q", I["w_q"])
            stream_split("bo", I["w_bo"])
            stream_ffn(3)
            for ft in range(DT):
                sp.wait_ge(y_done, ft + 1)
                sp.dma_start(O["y"][:, ft], xn[:, ft]).then_inc(y_out, 16)
            sp.wait_ge(y_out, 16 * DT)
            sp.wait_ge(shift_out, 16)
            sp.wait_ge(wkv_out, 32)
            sp.wait_ge(kv_out, 16)
            sp.wait_ge(win_out, 16 * (4 + DEC_B))

        @block.tensor
        def _(pe):
            mm = pe.matmul

            def take(s, k):
                pe.wait_ge(landed[s], (k + 1) * 16)
                pe.wait_ge(taken[s], k)

            def take_split(s, k, ks):
                pe.wait_ge(w_split[s], ks + 1)
                pe.wait_ge(taken[s], k)

            def norm(n):
                pe.wait_ge(acc_step, EV * (n + 1))
                for half in range(2):
                    last = mm(pst[:, half, 0:HALF], ones, acc[:, half * HALF:(half + 1) * HALF],
                              start=True, stop=True)
                last.then_inc(sum_done, 1)

            def times(bank, s, tile, ah, al, start, stop):
                w = slice(tile * P, (tile + 1) * P)
                for wt, a, first, last in ((wh, ah, start, False), (wh, al, False, False), (wl, ah, False, stop)):
                    for half in range(2):
                        ins = mm(pst[:, bank + half, 0:HALF], wt[:, s, w], a[:, half * HALF:(half + 1) * HALF],
                                 start=first, stop=last)
                return ins

            def outputs2(s, ah, al, ready=None):
                for m in range(2):
                    for ft in range(DT):
                        if ready and m == 0:
                            ready(ft)
                        last = times(4 * s + 2 * m, s, m * DT + ft, ah[:, ft, :], al[:, ft, :],
                                     ft == 0, ft == DT - 1)
                last.then_inc(multiplied[s], 1)

            def split_stage(name, ready=None):
                k0, pairs, ks = STAGES[name]
                if ready:
                    for s in range(2):
                        take_split(s, k0, ks)
                        outputs2(s, xh, xl, ready if s == 0 else None)
                a = 1 if ready else 0
                with pe.Fori(a, pairs) as i:
                    for s in range(2):
                        take_split(s, i + k0, i + ks)
                        outputs2(s, xh, xl)

            def out_stage(name, tiles, hidden):
                k0, pairs, ks = STAGES[name]
                with pe.Fori(0, pairs) as i:
                    for s in range(2):
                        take_split(s, i + k0, i + ks)
                        for x in range(2):
                            pe.wait_ge(hid_done[x], hidden + tiles // 2 - 1)
                        for ft in range(tiles):
                            if ft >= tiles - 2:
                                pe.wait_ge(hid_done[ft % 2], hidden + tiles // 2)
                            last = times(4 * s, s, ft, hh[:, ft, :], hl[:, ft, :], ft == 0, ft == tiles - 1)
                        last.then_inc(multiplied[s], 1)

            def xn_ready(n):
                return lambda ft: pe.wait_ge(xn_split, DT * n + ft + 1)

            def ffn(f, n):
                split_stage(f"inA{f}", xn_ready(n))
                out_stage(f"outA{f}", FTA, f * FT // 2)
                split_stage(f"inB{f}")
                out_stage(f"outB{f}", FTB, f * FT // 2 + FTA // 2)

            def project(name, src):
                k0, pairs, _ = STAGES[name]
                with pe.Fori(k0, k0 + pairs) as k:
                    for s in range(2):
                        take(s, k)
                        for m in range(2):
                            for ft in range(DT):
                                w = raw[:, s, (m * DT + ft) * P:(m * DT + ft + 1) * P]
                                for half in range(2):
                                    last = mm(pst[:, 4 * s + 2 * m + half, 0:HALF], w,
                                              src[:, ft, half * HALF:(half + 1) * HALF],
                                              start=(ft == 0), stop=(ft == DT - 1))
                        last.then_inc(multiplied[s], 1)

            fills = [0, 0, 0, 0]

            def fill(b):
                if fills[b]:
                    pe.wait_ge(emptied[b], fills[b])
                fills[b] += 1
                return pst[:, 2 * b:2 * b + 2, :]

            def got(b):
                pe.wait_ge(emptied[b], fills[b])

            pe.wait_ge(const_in, 32)
            norm(0)
            ffn(0, 0)
            norm(1)

            pe.wait_ge(lora_in, 16 * 8)
            for n, (x, w, m0, m) in enumerate(((xs_w, w_w1, 0, 64), (xs_a, w_a1, 0, 64), (xs_g, w_g1, 0, 128),
                                               (xs_g, w_g1, 128, 32))):
                pe.wait_ge(xs_done, min(n, 2) + 1)
                for half in range(2):
                    for ft in range(DT):
                        last = mm(pst[0:m, 2 * n + half, 0:HALF], w[:, ft, m0:m0 + m],
                                  x[:, ft, half * HALF:(half + 1) * HALF],
                                  start=(ft == 0), stop=(ft == DT - 1))
                last.then_inc(lora_mm, 1)
            pe.wait_ge(lora_act, 4)
            for ft in range(DT):
                e = ft % 2
                if ft >= 2:
                    pe.wait_ge(lw_sig, 2 * (ft - 1))
                for half in range(2):
                    mm(pst[:, 4 * e + half, 0:HALF], w_w2[:, ft * P:(ft + 1) * P],
                       sg[0:64, 0, half * HALF:(half + 1) * HALF], start=True, stop=True)
                for half in range(2):
                    last = mm(pst[:, 4 * e + 2 + half, 0:HALF], w_a2[:, ft * P:(ft + 1) * P],
                              sg[0:64, 1, half * HALF:(half + 1) * HALF], start=True, stop=True)
                last.then_inc(lw_mm, 1)
            pe.wait_ge(lw_sig, 2 * DT)
            pe.wait_ge(xs_done, 6)
            project("v", xs_v)
            k0 = STAGES["rk"][0]

            def rk_squares(m):
                pe.wait_ge(kksq_done, m + 1)
                if m:
                    pe.wait_ge(kkmax_done, m)
                for half in range(2):
                    last = mm(pst[:, 4 + half, 0:HALF], blk, SQ[:, half * HALF:(half + 1) * HALF],
                              start=True, stop=True)
                last.then_inc(kksum_done, 1)

            def rk_bonus(m):
                pe.wait_ge(rk_done, m + 1)
                for half in range(2):
                    last = mm(pst[32:48, 6 + half, 0:HALF], hsel[:, m, :], SQ[:, half * HALF:(half + 1) * HALF],
                              start=(m == 0), stop=(m == DT - 1))
                last.then_inc(bonus_mm, 1)

            for m in range(DT):
                s, k = m % 2, k0 + m // 2
                pe.wait_ge(landed[s], (k + 1) * 16)
                pe.wait_ge(taken[1 - s], k + s)
                pe.wait_ge(taken[s], k)
                for w0, src in ((0, xs_r), (1, xs_k)):
                    for ft in range(DT):
                        w = raw[:, s, (w0 * DT + ft) * P:(w0 * DT + ft + 1) * P]
                        for half in range(2):
                            last = mm(pst[:, 2 * w0 + half, 0:HALF], w,
                                      src[:, ft, half * HALF:(half + 1) * HALF],
                                      start=(ft == 0), stop=(ft == DT - 1))
                    if m and w0 == 0:
                        rk_squares(m - 1)
                last.then_inc(multiplied[s], 1)
                if m:
                    rk_bonus(m - 1)
            rk_squares(DT - 1)
            rk_bonus(DT - 1)
            pe.wait_ge(bonus_done, 1)
            pe.wait_ge(taken[0], k0 + 4)
            pe.wait_ge(taken[1], k0 + 4)
            pe.wait_ge(temps_free, DT)

            def cols(h, q, c):
                o = (h % 2) * 512 + (h // 2) * 64
                return slice(64 * q, 64 * q + c), slice(o, o + c)

            def wide(ap):
                return ap.rearrange("p b c -> p (b c)")

            def turn(src, u, b):
                buf = wide(fill(b))
                n = P if u < 4 else 32
                for ft in range(DT):
                    last = pe.transpose(buf[0:n, ft * P:(ft + 1) * P], src[:, ft, u * P:u * P + n], ident)
                last.then_inc(filled[b], 1)

            def gram(b, lhs, rhs, u, c, nq):
                buf = wide(fill(b))
                for q in range(nq):
                    t0 = u * P + 64 * q
                    for h in range(NH):
                        f = slice(64 * (h % 2), 64 * (h % 2) + 64)
                        r, co = cols(h, q, c)
                        last = mm(buf[r, co], lhs[f, h // 2, t0:t0 + c], rhs[f, h // 2, t0:t0 + c],
                                  start=True, stop=True)
                last.then_inc(filled[b], 1)

            def product(b, lhs, rhs, c, nq):
                buf = wide(fill(b))
                for q in range(nq):
                    for h in range(NH):
                        r, co = cols(h, q, c)
                        last = mm(buf[r, co], lhs[r, co], rhs[r, co], start=True, stop=True)
                last.then_inc(filled[b], 1)

            for u in range(5):
                c, nq, levels = (64, 2, LEVELS_P) if u < 4 else (32, 1, LEVELS_D)
                turn(t_v, u, 0)
                turn(t_b, u, 1)
                turn(t_k, u, 2)
                gram(3, t_b, t_a, u, c, nq)
                gram(0, t_a, t_b, u, c, nq)
                gram(1, t_k, t_a, u, c, nq)
                gram(2, t_b, t_r, u, c, nq)
                gram(3, t_k, t_r, u, c, nq)
                got(0)
                for n, _m in enumerate(levels):
                    lev = u * 5 + n
                    pe.wait_ge(al_ready, lev + 1)
                    product(0, AL, X_, c, nq)
                    got(0)
                    pe.wait_ge(xt_ready, u + 1)
                    if n:
                        got(2)
                    if n < len(levels) - 1:
                        product(1, XT, PP, c, nq)
                    product(2, PP, XT, c, nq)
                    if n < len(levels) - 1:
                        got(1)
                got(1)
                got(2)
                got(3)
                if u < 4:
                    for q in range(2):
                        t0 = u * P + 64 * q
                        turns = 2 * u + q
                        pe.wait_ge(st_ready, turns + 1)
                        buf = wide(fill(3))
                        for h in range(0, NH, 2):
                            for p in range(2):
                                f = slice(64 * p, 64 * p + 64)
                                r, co = cols(h + p, q, 64)
                                last = mm(buf[r, co], t_a[f, h // 2, t0:t0 + 64], st[f, h // 2, :],
                                          start=(h == 0), stop=False, skip_group_check=True)
                        last.then_inc(pe_order, 1)
                        pe.wait_ge(pe_order, turns + 1)
                        for p in range(2):
                            for h in range(p, NH, 2):
                                r, co = cols(h, q, 64)
                                last = mm(buf[r, co], AKT[r, co], V_[r, h * 64:h * 64 + 64],
                                          start=False, stop=True, skip_group_check=True)
                        last.then_inc(filled[3], 1)
                        ybuf = wide(fill(1))
                        for h in range(0, NH, 2):
                            for p in range(2):
                                f = slice(64 * p, 64 * p + 64)
                                o = p * 512 + (h // 2) * 64
                                mm(ybuf[f, o:o + 64], st[f, h // 2, :], t_r[f, h // 2, t0:t0 + 64],
                                   start=(h == 0), stop=False, skip_group_check=True)
                        got(3)
                        buf = wide(fill(0))
                        for h in range(NH):
                            r, co = cols(h, q, 64)
                            last = mm(buf[r, co], XT[r, co], PP[r, co], start=True, stop=True)
                        last.then_inc(filled[0], 1)
                        got(0)
                        for p in range(2):
                            for h in range(p, NH, 2):
                                r, co = cols(h, q, 64)
                                f = slice(64 * p, 64 * p + 64)
                                o = p * 512 + (h // 2) * 64
                                mm(ybuf[f, o:o + 64], UU[r, co], RBT[r, co],
                                   start=False, stop=False, skip_group_check=True)
                                last = mm(ybuf[f, o:o + 64], V_[r, h * 64:h * 64 + 64], RKT[r, co],
                                          start=False, stop=True, skip_group_check=True)
                        last.then_inc(filled[1], 1)
                        buf = wide(fill(2))
                        for h in range(NH):
                            r, co = cols(h, q, 64)
                            f = slice(64 * (h % 2), 64 * (h % 2) + 64)
                            o = (h // 2) * 64
                            mm(buf[f, o:o + 64], B_[r, h * 64:h * 64 + 64], UU[r, co], start=True, stop=False)
                            last = mm(buf[f, o:o + 64], K_[r, h * 64:h * 64 + 64], V_[r, h * 64:h * 64 + 64],
                                      start=False, stop=True)
                        last.then_inc(filled[2], 1)
                else:
                    pe.wait_ge(s0_in, 16)
                    buf = wide(fill(3))
                    for h in range(NH):
                        r, co = cols(h, 0, 32)
                        o = (h % 2) * 512 + (h // 2) * 64
                        last = mm(buf[r, o:o + 64], AKT[r, co], V_[r, h * 64:h * 64 + 64], start=True, stop=True)
                    last.then_inc(filled[3], 1)
                    buf = fill(1).rearrange("p k (f x t) -> p k f x t", f=DT, x=2)
                    for b in range(DEC_B):
                        t0 = SEQ + DEC_T * b
                        for h in range(NH):
                            f = slice(64 * (h % 2), 64 * (h % 2) + 64)
                            last = mm(buf[f, h % 2, h // 2, :, 4 * b:4 * b + 4], s0T[f, h // 2, b, :],
                                      t_ar[f, :, h // 2, t0:t0 + DEC_T], start=True, stop=True)
                    last.then_inc(filled[1], 1)
                    got(1)
                    buf = wide(fill(0))
                    for ft in range(DT):
                        last = pe.transpose(buf[0:32, ft * P:(ft + 1) * P], y0[:, ft, 0, :], ident)
                    last.then_inc(filled[0], 1)
                    got(0)
                    buf = wide(fill(2))
                    for h in range(NH):
                        r, co = cols(h, 0, 32)
                        o = (h % 2) * 512 + (h // 2) * 64
                        last = mm(buf[r, o:o + 64], XT[r, co], PP[r, o:o + 64], start=True, stop=True)
                    last.then_inc(filled[2], 1)
                    got(2)
                    buf = wide(fill(1))
                    for h in range(NH):
                        r, co = cols(h, 0, 32)
                        o = (h % 2) * 512 + (h // 2) * 64
                        f = slice(64 * (h % 2), 64 * (h % 2) + 64)
                        mm(buf[f, o:o + 32], UU[r, o:o + 64], RBT[r, co], start=True, stop=False)
                        last = mm(buf[f, o:o + 32], V_[r, h * 64:h * 64 + 64], RKT[r, co], start=False, stop=True)
                    last.then_inc(filled[1], 1)
                    for ft in range(DT):
                        b = 2 + ft % 2
                        pe.wait_ge(um_ready, ft + 1)
                        buf = fill(b)
                        for p in range(2):
                            h = 2 * ft + p
                            f = slice(64 * p, 64 * p + 64)
                            mm(buf[f, 0, :], B_[0:32, h * 64:h * 64 + 64], um[:, p, 0, :], start=True, stop=False)
                            last = mm(buf[f, 0, :], K_[0:32, h * 64:h * 64 + 64], um[:, p, 1, :],
                                      start=False, stop=True)
                        last.then_inc(filled[b], 1)
            pe.wait_ge(expand_in, 16)
            for step in range(4):
                for ft in range(DT):
                    b = ft % 4
                    if step == 0 and ft == 0:
                        for x in range(4):
                            got(x)
                    if step == 1:
                        pe.wait_ge(gn_sq, ft + 1)
                    buf = fill(b)
                    for half in range(2):
                        t = slice(half * HALF, (half + 1) * HALF)
                        if step == 0:
                            last = mm(buf[:, half, 0:HALF], blk, t_r[:, ft, t], start=True, stop=True)
                        elif step == 1:
                            last = mm(buf[:, half, 0:HALF], blk, t_a[:, ft, t], start=True, stop=True)
                        elif step == 2:
                            last = mm(buf[:, half, 0:HALF], expand[:, ft * P:(ft + 1) * P], bc[:, t],
                                      start=True, stop=True)
                        else:
                            mm(buf[:, half, 0:HALF], w_g2a[:, ft * P:(ft + 1) * P], gs[:, 0, t],
                               start=True, stop=False)
                            last = mm(buf[:, half, 0:HALF], w_g2b[:, ft * P:(ft + 1) * P], gs[0:32, 1, t],
                                      start=False, stop=True)
                    last.then_inc(filled[b], 1)
            for x in range(4):
                got(x)
            project("wo", t_r)

            norm(2)
            ffn(1, 1)
            norm(3)
            pe.wait_ge(xn_done, 2)
            project("kv", xn)

            for b in (0, 1):
                pe.wait_ge(taken[b], STAGES["kv"][0] + 3)
            pe.wait_ge(kv_done, 1)
            pe.wait_ge(cache_cmp_in, 16 * DEC_B * NPG)
            pe.wait_ge(cw_in, 16 * 4)
            pe.wait_ge(cred_done, 2)
            for kv in range(2):
                last = mm(pst[:, 4, kv:kv + 1], cred[:, kv, :], ones[0:64, 0:1], start=True, stop=True)
            last.then_inc(cmp_mm, 1)
            for kv in range(2):
                for s in range(32):
                    for p in range(2):
                        f = slice(64 * p, 64 * p + 64)
                        last = mm(pst[:, 2 * kv + p, 0:2 * NBLK], cw1[f, kv, s, :],
                                  cmpT[f, kv, :, s:s + 16 * (NBLK - 1) + 1:16],
                                  start=(s == 0), stop=(s == 31))
                last.then_inc(cmp_mm, 1)
            pe.wait_ge(cmp_ev, 1 + 4)
            for p in range(2):
                f = slice(64 * p, 64 * p + 64)
                mm(pst[f, 5, 0:320], cw2[:, 0, :], chid[:, p, :, :], start=True, stop=True)
            for kvh in range(NKV):
                mm(pst[0:32, 6, kvh * 64:kvh * 64 + 64], chid[:, 2 + kvh % 2, kvh // 2, 0:32], cw2[:, 1, :],
                   start=True, stop=True)
                last = mm(pst[:, 7, kvh * 64:kvh * 64 + 64], chid[:, 2 + kvh % 2, kvh // 2, 32:160],
                          cw2[:, 1, :], start=True, stop=True)
            last.then_inc(cmp_mm, 1)
            for n, (src, tl) in enumerate([(8, t) for t in range(4)] + [(10, t) for t in range(4)]
                                          + [(8, 4), (10, 4)]):
                b = n % 4
                m = P if tl < 4 else 32
                if n >= 4:
                    pe.wait_ge(vt_ev, n - 3)
                for p in range(2):
                    last = pe.transpose(pst[0:m, b, p * P:(p + 1) * P], kvT[:, src + p, tl * P:tl * P + m],
                                        ident)
                last.then_inc(vt_mm, 1)
            pe.wait_ge(vt_ev, 10)
            pe.wait_ge(cmp_ev, 8)

            norm(4)
            ffn(2, 2)
            norm(5)
            split_stage("q", xn_ready(3))
            pe.wait_ge(taken[0], STAGES["q"][0] + 2)
            pe.wait_ge(taken[1], STAGES["q"][0] + 2)
            pe.wait_ge(gate_w_in, 16)
            for half in range(2):
                for ft in range(DT):
                    last = mm(pst[0:48, half, 0:HALF], wgt[:, ft, :], xr[:, ft, half * HALF:(half + 1) * HALF],
                              start=(ft == 0), stop=(ft == DT - 1))
            last.then_inc(gate_mm, 1)
            pe.wait_ge(gate_sig, 1)
            for tl in range(5):
                m = P if tl < 4 else 32
                last = pe.transpose(pst[0:m, 2, tl * 48:tl * 48 + 48], gT[:, tl * P:tl * P + m],
                                    ident[0:48, 0:48])
            last.then_inc(gate_tr, 1)
            pe.wait_ge(gates_done, 1)

            n_turn = [0]

            def scores(e):
                i, p, qt = e // 8, e // 4 % 2, e % 4
                f = slice(64 * p, 64 * p + 64)
                nk = P * (qt + 1)
                q = qT[f, i, qt * P:(qt + 1) * P]
                if e >= 2:
                    pe.wait_ge(score_taken, 3 * (e - 1))
                mm(pst[:, 2 * (e % 2), 0:nk], q, kslc[f, i // 4, 0:nk], start=True, stop=True)
                mm(pst[:, 2 * (e % 2) + 1, 0:nk], q, kwin[f, i // 4, 0:nk], start=True, stop=True)
                if e >= 1:
                    pe.wait_ge(score_taken, 3 * e - 2)
                mm(pst[:, 4, 0:NCMP], q, kcmp[f, i // 4, 0:NCMP], start=True, stop=True).then_inc(score_mm, 1)

            def turn_group(blocks, bank, c0, free):
                if free > 0:
                    pe.wait_ge(turn_taken, free)
                for x, (src, m) in enumerate(blocks):
                    last = pe.transpose(pst[0:m, bank, c0 + x * P:c0 + (x + 1) * P], src, ident)
                last.then_inc(turned, 1)

            def turn_probs(e):
                qt = e % 4
                s = sbuf[e % 4]
                pe.wait_ge(p_ready, e + 1)
                turn_group([(s[:, x * P:(x + 1) * P], P) for x in range(qt + 1)], 6, 0, 3 * e)
                turn_group([(s[:, 512 + x * P:512 + (x + 1) * P], P) for x in range(qt + 1)], 7, 0, 3 * e - 1)

            def turn_cmp(e):
                turn_group([(sbuf[e % 4][:, 1024:1024 + NCMP], NCMP)], 6, 0, 3 * e + 1)

            def values(e):
                i, p, qt = e // 8, e // 4 % 2, e % 4
                f = slice(64 * p, 64 * p + 64)
                kvh = 2 * (i // 4) + p
                pt = ptb[e % 2]
                pe.wait_ge(turn_taken, 3 * e + 3)
                if qt == 0 and e >= 8:
                    pe.wait_ge(o_taken, e // 4 - 1)
                out = pst[f, 5, qt * P:(qt + 1) * P]
                c = slice(kvh * 64, kvh * 64 + 64)
                for x in range(qt + 1):
                    mm(out, v_slc[:, x, c], pt[:, x, :], start=(x == 0), stop=False)
                for x in range(qt + 1):
                    mm(out, v_win[:, x, c], pt[:, 4 + x, :], start=False, stop=False)
                mm(out, vcmp_p[:, c], pt[0:NCMP, 8, :], start=False, stop=True).then_inc(o_mm, 1)

            E = 2 * DT * 4
            def sample_scores(u):
                if u == 0:
                    pe.wait_ge(qbd_done, 4)
                    pe.wait_ge(caches_in, 16 * (2 * DEC_B * NPG + 1))
                    pe.wait_ge(score_taken, 3 * (E - 1))
                else:
                    pe.wait_ge(score_taken, 3 * E + 2 * (u - 1))
                bank = 2 * (u % 2)
                for j in range(2):
                    b = 2 * u + j
                    r = slice(64 * j, 64 * j + 64)
                    for out, src in ((pst[r, bank, 0:128], lambda x: kcmp[:, x, 32:160]),
                                     (pst[r, bank, 128:160], lambda x: kslc[:, x, SEQ:TOK]),
                                     (pst[r, bank, 160:192], lambda x: kwin[:, x, SEQ:TOK]),
                                     (pst[r, bank + 1, 0:256].rearrange("p (g t) -> p g t", g=NPG),
                                      lambda x: kslc_c[:, 2 * b:2 * b + 2, x, :]),
                                     (pst[r, bank + 1, 256:512], lambda x: kwin_c[:, b, x, :])):
                        for x in range(2):
                            last = mm(out, qbd[:, x, b, :], src(x), start=(x == 0), stop=(x == 1))
                last.then_inc(score_mm, 1)

            def sample_turns(u):
                pe.wait_ge(p_ready, E + u + 1)
                s = sbuf[u]
                turn_group([(s[:, x * P:(x + 1) * P], P) for x in range(3)]
                           + [(s[:, 416:544], P)], 6, 0, 3 * E if u == 0 else 3 * E + 2 * u - 1)
                turn_group([(s[:, 544:672], P), (s[:, 384:416], 32), (s[:, 672:704], 32)], 7, 0, 3 * E + 2 * u)

            def sample_values(u):
                pe.wait_ge(turn_taken, 3 * E + 2 * u + 2)
                if u == 0:
                    pe.wait_ge(vwin_in, 16)
                    pe.wait_ge(score_taken, 3 * E)
                pt = ptb[u % 2]
                for x in range(2):
                    c = slice(x * P, (x + 1) * P)

                    def both(ap, x=x):
                        return ap.rearrange("p (j x r) -> p x j r", j=2, x=2)[:, x]

                    out = pst[:, 4, P * u:P * (u + 1)]
                    mm(both(out), vcmp_d[:, c], both(pt[:, 0, :]), start=True, stop=False, skip_group_check=True)
                    for j in range(2):
                        b, rows = 2 * u + j, slice(64 * j + 32 * x, 64 * j + 32 * x + 32)
                        for pg in range(NPG):
                            mm(out[:, rows], vslc_c[:, 2 * b + pg, c], pt[:, 1 + pg, rows],
                               start=False, stop=False, skip_group_check=True)
                            mm(out[:, rows], vwin_c[:, 2 * b + pg, c], pt[:, 3 + pg, rows],
                               start=False, stop=False, skip_group_check=True)
                    mm(both(out), v_new[:, 0, c], both(pt[0:32, 5, :]), start=False, stop=False,
                       skip_group_check=True)
                    last = mm(both(out), v_new[:, 1, c], both(pt[0:32, 6, :]), start=False, stop=True,
                              skip_group_check=True)
                last.then_inc(o_mm, 1)

            for e in range(E + 4):
                if 3 <= e <= E + 2:
                    turn_probs(e - 3)
                if e < E:
                    scores(e)
                if e == E:
                    sample_scores(0)
                if 3 <= e <= E + 2:
                    turn_cmp(e - 3)
                if e >= 4:
                    values(e - 4)
            for u in range(4):
                sample_turns(u)
                if u < 3:
                    sample_scores(u + 1)
                sample_values(u)
            split_stage("bo", lambda ft: pe.wait_ge(o_split, ft + 1))
            norm(6)
            ffn(3, 4)
            norm(7)

        @block.scalar
        def _(act):
            def split(name, i, s):
                k0, _, ks = STAGES[name]
                cols = cols_of(name)
                act.wait_ge(landed[s], (i + k0) * 16 + 16)
                act.wait_ge(multiplied[s], i + k0)
                act.activation(wh[:, s, 0:cols], raw[:, s, 0:cols], ACT.Copy).then_inc(w_hi[s], 1)

            def pipeline(name, finish, following):
                pairs = STAGES[name][1]
                with act.Fori(0, pairs - 1) as i:
                    split(name, i, 1)
                    finish(i, 0)
                    split(name, i + 1, 0)
                    finish(i, 1)
                split(name, pairs - 1, 1)
                finish(pairs - 1, 0)
                if following:
                    split(following, 0, 0)
                finish(pairs - 1, 1)

            def squares(name, n, tiles):
                k0 = STAGES[name][0]

                def finish(i, s):
                    act.wait_ge(taken[s], i + k0 + 1)
                    for m in range(tiles):
                        t = (2 * i + s) * tiles + m
                        x = m if tiles == 2 else s
                        act.wait_ge(acc_step, t + EV * n)
                        act.activation(sg[:, x, :], hT[:, bass.ds(t, 1), :].rearrange("p o c -> p (o c)"),
                                       ACT.Square).then_inc(sq_done, 1)
                return finish

            def norm(n, splits):
                act.wait_ge(sum_done, n + 1)
                act.activation(halves(sg[:, 0, :]), bank2(0), ACT.Sqrt, bias=eps[:], scale=1.0 / D)\
                   .then_inc(root_done, 1)
                if splits is not None:
                    for ft in range(DT):
                        act.wait_ge(xr_done, splits * DT + ft + 1)
                        act.activation(xh[:, ft, :], xr[:, ft, :], ACT.Copy).then_inc(xh_done, 1)

            def ffn(f, n, following=None):
                def hidden(name, before):
                    k0 = STAGES[name][0]

                    def finish(i, s):
                        act.wait_ge(multiplied[s], i + k0 + 1)
                        act.wait_ge(hid_done[s], i + before)
                        act.activation(halves(sg[:, s, :]), bank2(4 * s), ACT.Silu).then_inc(gate_done[s], 1)
                        act.wait_ge(taken[s], i + k0 + 1)
                        act.activation(hh[:, bass.ds(2 * i + s, 1), :].rearrange("p o c -> p (o c)"),
                                       sg[:, s, :], ACT.Copy).then_inc(hid_hi[s], 1)
                    return finish

                pipeline(f"inA{f}", hidden(f"inA{f}", f * FT // 2), f"outA{f}")
                pipeline(f"outA{f}", lambda i, s: None, f"inB{f}")
                pipeline(f"inB{f}", hidden(f"inB{f}", f * FT // 2 + FTA // 2), f"outB{f}")
                pipeline(f"outB{f}", squares(f"outB{f}", n, 1), following)

            def plain(name, finish):
                pairs = STAGES[name][1]
                with act.Fori(0, pairs) as i:
                    for s in range(2):
                        finish(i, s)

            seen = [0, 0, 0, 0]

            def empty(b):
                seen[b] += 1
                act.wait_ge(filled[b], seen[b])
                return pst[:, 2 * b:2 * b + 2, :]

            def skip(*bs):
                for b in bs:
                    seen[b] += 1

            act.wait_ge(const_in, 32)
            act.wait_ge(eps_set, 1)
            for ft in range(DT):
                if ft % 4 == 0:
                    act.wait_ge(x_in[ft // 4], 16)
                act.wait_ge(acc_step, ft)
                act.activation(sg[:, ft % 2, :], hT[:, ft, :], ACT.Square).then_inc(sq_done, 1)
            split("inA0", 0, 0)
            norm(0, 0)
            ffn(0, 1)
            norm(1, None)

            for n, (fn, out) in enumerate(((ACT.Tanh, sg[0:64, 0, :]), (ACT.Copy, sg[0:64, 1, :]),
                                           (ACT.Sigmoid, gs[:, 0, :]), (ACT.Sigmoid, gs[0:32, 1, :]))):
                m = out.shape[0]
                act.wait_ge(lora_mm, n + 1)
                if n == 0:
                    act.wait_ge(xn_done, 1)
                act.activation(halves(out), pst[0:m, 2 * n:2 * n + 2, 0:HALF], fn).then_inc(lora_act, 1)
            act.wait_ge(xs_done, 6)
            for ft in range(DT):
                e = ft % 2
                act.wait_ge(lw_mm, ft + 1)
                act.activation(halves(sigw[:, ft, :]), bank2(4 * e), ACT.Sigmoid, bias=par(Q_W0, ft))\
                   .then_inc(lw_sig, 1)
                act.activation(halves(a_t[:, ft, :]), bank2(4 * e + 2), ACT.Sigmoid, bias=par(Q_A0, ft))\
                   .then_inc(lw_sig, 1)
            k0, pairs, _ = STAGES["v"]
            for n in range(2 * pairs):
                s = n % 2
                act.wait_ge(multiplied[s], k0 + n // 2 + 1)
                for m in range(2):
                    ins = act.activation(halves(t_v[:, 2 * n + m, :]), bank2(4 * s + 2 * m), ACT.Copy)
                ins.then_inc(taken[s], 1)
            k0 = STAGES["rk"][0]
            for m in range(DT):
                s = m % 2
                if m:
                    act.wait_ge(temps_free, m)
                act.wait_ge(cum_done, m + 1)
                act.activation(EP, cumw[:, m, :], ACT.Exp, scale=-DECAY)
                act.activation(EN, cumw[:, m, :], ACT.Exp, scale=DECAY)
                act.wait_ge(diff_done, m + 1)
                act.activation(EX, KP, ACT.Exp, scale=-DECAY).then_inc(exps_done, 1)
                act.wait_ge(multiplied[s], k0 + m // 2 + 1)
                act.activation(halves(KR), bank2(2), ACT.Copy)
                act.activation(halves(RR), bank2(0), ACT.Copy).then_inc(taken[s], 1)
                act.wait_ge(kkmax_done, m + 1)
                act.activation(SQ, SQ, ACT.Sqrt).then_inc(kkroot_done, 1)
            act.wait_ge(bonus_mm, DT)
            act.activation(halves(bc), pst[32:48, 6:8, 0:HALF], ACT.Copy).then_inc(bonus_done, 1)
            act.wait_ge(temps_free, DT)

            def flat(ap):
                return ap.rearrange("p b c -> p (b c)")

            for u in range(5):
                n = P if u < 4 else 32
                levels = LEVELS_P if u < 4 else LEVELS_D
                for b, dst in ((0, V_), (1, B_), (2, K_)):
                    act.activation(dst[0:n], flat(empty(b)[0:n]), ACT.Copy).then_inc(emptied[b], 1)
                skip(3, 0, 1, 2, 3)
                for x in range(len(levels)):
                    if u < 4:
                        act.activation(PP, flat(empty(0)), ACT.Copy).then_inc(emptied[0], 1)
                    else:
                        src = flat(empty(0)[0:32]).rearrange("p (a c) -> p a c", a=NH)[:, :, 0:32]
                        act.activation(PP[0:32].rearrange("p (a c) -> p a c", a=NH)[:, :, 0:32], src, ACT.Copy)\
                           .then_inc(emptied[0], 1)
                    skip(*((1, 2) if x < len(levels) - 1 else (2,)))
                if u < 4:
                    for q in range(2):
                        r = slice(64 * q, 64 * q + 64)
                        act.activation(PP[r], flat(empty(3)[r]), ACT.Copy).then_inc(emptied[3], 1)
                        act.activation(UU[r], flat(empty(0)[r]), ACT.Copy).then_inc(emptied[0], 1)
                        t0 = u * P + 64 * q
                        buf = empty(1)
                        for p in range(2):
                            f = slice(64 * p, 64 * p + 64)
                            ins = act.activation(t_r[f, :, t0:t0 + 64],
                                                 buf[f, p, :].rearrange("p (f t) -> p f t", f=DT), ACT.Copy)
                        ins.then_inc(emptied[1], 1)
                        skip(2)
                else:
                    act.activation(PP[0:32], flat(empty(3)[0:32]), ACT.Copy).then_inc(emptied[3], 1)
                    buf = empty(1)
                    for p in range(2):
                        f = slice(64 * p, 64 * p + 64)
                        ins = act.activation(y0[f].rearrange("p f x t -> p (f x t)"), buf[f, p, :], ACT.Copy)
                    ins.then_inc(emptied[1], 1)
                    skip(0)
                    act.activation(UU[0:32], flat(empty(2)[0:32]), ACT.Copy).then_inc(emptied[2], 1)
                    skip(1)
                    for ft in range(DT):
                        skip(2 + ft % 2)
            for ft in range(DT):
                skip(ft % 4)
                act.wait_ge(emptied[ft % 4], seen[ft % 4])
                act.activation(t_a[:, ft, :], t_r[:, ft, :], ACT.Square).then_inc(gn_sq, 1)
            for ft in range(DT):
                skip(ft % 4)
                act.wait_ge(emptied[ft % 4], seen[ft % 4])
                act.activation(t_k[:, ft, :], t_k[:, ft, :], ACT.Sqrt).then_inc(gn_root, 1)

            plain("wo", squares("wo", 2, 2))
            split("inA1", 0, 0)
            norm(2, 1)
            ffn(1, 3)
            norm(3, None)

            k0, pairs, _ = STAGES["kv"]
            for n in range(2 * pairs):
                s = n % 2
                act.wait_ge(multiplied[s], k0 + n // 2 + 1)
                for m in range(2):
                    ins = act.activation(halves(kvT[:, 2 * n + m, :]), bank2(4 * s + 2 * m), ACT.Copy)
                ins.then_inc(taken[s], 1)
            act.wait_ge(taken[0], k0 + 3)
            act.wait_ge(taken[1], k0 + 3)
            act.activation(cmpT[:, :, :, 0:SEQ].rearrange("p a b c -> p (a b) c"), kvT[:, 4:8, 0:SEQ], ACT.Copy)\
               .then_inc(kv_done, 1)
            act.wait_ge(cmp_mm, 1)
            act.activation(cbias[:, 0:2], pst[:, 4, 0:2], ACT.Copy).then_inc(cmp_ev, 1)
            act.wait_ge(cmp_ev, 1)
            act.wait_ge(chid_zero, 1)
            for kv in range(2):
                act.wait_ge(cmp_mm, 2 + kv)
                for p in range(2):
                    act.activation(chid[:, 2 * kv + p, :, 0:NBLK],
                                   pst[:, 2 * kv + p, 0:2 * NBLK].rearrange("p (x n) -> p x n", x=2),
                                   ACT.Gelu_apprx_tanh, bias=cbias[:, kv:kv + 1]).then_inc(cmp_ev, 1)
            act.wait_ge(cmp_mm, 4)
            act.activation(kcmp, pst[:, 5, 0:320].rearrange("p (x n) -> p x n", x=2), ACT.Copy).then_inc(cmp_ev, 1)
            act.activation(vcmp_p, pst[0:32, 6, 0:256], ACT.Copy).then_inc(cmp_ev, 1)
            act.activation(vcmp_d, pst[:, 7, 0:256], ACT.Copy).then_inc(cmp_ev, 1)
            act.wait_ge(cmp_mm, 4)
            for n in range(10):
                act.wait_ge(vt_mm, n + 1)
                b = n % 4
                if n < 8:
                    dst, m = (v_slc, v_win)[n // 4][:, n % 4, :], P
                else:
                    dst, m = v_new[:, n - 8, :], 32
                act.activation(dst, pst[0:m, b, 0:256], ACT.Copy).then_inc(vt_ev, 1)

            act.wait_ge(kv_out, 16)
            split("inA2", 0, 0)
            for ft in range(DT):
                act.wait_ge(acc_step, EV * 4 + ft)
                act.activation(sg[:, ft % 2, :], hT[:, ft, :], ACT.Square).then_inc(sq_done, 1)
            norm(4, 2)
            ffn(2, 5, "q")
            norm(5, 3)
            k0, pairs, _ = STAGES["q"]
            for n in range(2 * pairs):
                s = n % 2
                if n + 1 < 2 * pairs:
                    split("q", (n + 1) // 2, (n + 1) % 2)
                act.wait_ge(multiplied[s], k0 + n // 2 + 1)
                for m in range(2):
                    ins = act.activation(halves(qT[:, 2 * n + m, :]), bank2(4 * s + 2 * m), ACT.Copy,
                                         scale=HD ** -0.5)
                ins.then_inc(taken[s], 1)
            act.wait_ge(gate_mm, 1)
            act.activation(halves(gT), pst[0:48, 0:2, 0:HALF], ACT.Sigmoid).then_inc(gate_sig, 1)

            E = 2 * DT * 4
            turns = [0]

            def copy_turned(dst, m, n, b, c0=0):
                act.wait_ge(turned, turns[0] + 1)
                turns[0] += 1
                act.activation(dst, pst[0:m, b, c0:c0 + n * P].rearrange("p (x c) -> p x c", x=n), ACT.Copy)\
                   .then_inc(turn_taken, 1)

            def exps(e):
                qt, s, x = e % 4, sbuf[e % 4], e % 2
                nk = P * (qt + 1)
                act.wait_ge(negmax, e + 1)
                for n, c in enumerate((slice(1024, 1024 + NCMP), slice(0, nk), slice(512, 512 + nk))):
                    ins = act.activation(s[:, c], s[:, c], ACT.Exp, bias=sm[:, x, 4 + n:5 + n],
                                         accum_out=sm[:, x, 8 + n:9 + n])
                ins.then_inc(exp_done, 1)

            def copies(e):
                qt, pt = e % 4, ptb[e % 2]
                if e >= 2:
                    act.wait_ge(o_mm, e - 1)
                copy_turned(pt[:, 0:qt + 1, :], P, qt + 1, 6)
                copy_turned(pt[:, 4:4 + qt + 1, :], P, qt + 1, 7)
                copy_turned(pt[0:NCMP, 8:9, :], NCMP, 1, 6)

            for e in range(1, E + 3):
                if e <= E:
                    exps(e - 1)
                if e >= 3:
                    copies(e - 3)
            for u in range(4):
                e = E + u
                s, x = sbuf[u], u % 2
                act.wait_ge(negmax, e + 1)
                for n, c in enumerate((slice(0, 128), slice(128, 416), slice(416, 704))):
                    ins = act.activation(s[:, c], s[:, c], ACT.Exp, bias=sm[:, x, 4 + n:5 + n],
                                         accum_out=sm[:, x, 8 + n:9 + n])
                ins.then_inc(exp_done, 1)
                pt = ptb[u % 2]
                act.wait_ge(o_mm, e - 1)
                copy_turned(pt[:, 0:4, :], P, 4, 6)
                act.wait_ge(turned, turns[0] + 1)
                turns[0] += 1
                act.activation(pt[:, 4, :], pst[:, 7, 0:P], ACT.Copy)
                act.activation(pt[0:32, 5:7, :], pst[0:32, 7, P:3 * P].rearrange("p (x c) -> p x c", x=2),
                               ACT.Copy).then_inc(turn_taken, 1)
            act.wait_ge(o_mm, E + 4)
            split("bo", 0, 0)
            act.wait_ge(o_taken, 20)
            for ft in range(DT):
                act.activation(xh[:, ft, :], oT[:, ft, :], ACT.Copy).then_inc(oh_done, 1)
            pipeline("bo", squares("bo", 6, 2), "inA3")
            norm(6, 4)
            ffn(3, 7)
            norm(7, None)

        @block.vector
        def _(dve):
            own = Steps(dve, dve_step)
            do = own.do

            def split(name, i, s):
                ks = STAGES[name][2]
                cols = cols_of(name)
                dve.wait_ge(w_hi[s], i + ks + 1)
                dve.tensor_tensor(wl[:, s, 0:cols], raw[:, s, 0:cols], wh[:, s, 0:cols].bitcast(F32), ALU.subtract)\
                   .then_inc(w_split[s], 1)

            def pipeline(name, finish, following):
                pairs = STAGES[name][1]
                with dve.Fori(0, pairs - 1) as i:
                    split(name, i, 1)
                    finish(i, 0)
                    split(name, i + 1, 0)
                    finish(i, 1)
                split(name, pairs - 1, 1)
                finish(pairs - 1, 0)
                if following:
                    split(following, 0, 0)
                finish(pairs - 1, 1)

            def clear(n):
                if n:
                    dve.wait_ge(sum_done, n)
                dve.memset(acc[:], 0.0).then_inc(acc_step, 1)

            def sum_square(n, t, x):
                dve.wait_ge(sq_done, t + (DT * n + 1))
                dve.wait_ge(acc_step, t + (EV * n + 1))
                dve.tensor_tensor(acc[:], acc[:], sg[:, x, :], ALU.add).then_inc(acc_step, 1)

            def norm(n, q, splits=None, last=False):
                dve.wait_ge(root_done, n + 1)
                do(dve.reciprocal(sg[:, 1, :], sg[:, 0, :]))
                own.wait()

                def low(ft):
                    dve.wait_ge(xh_done, splits * DT + ft + 1)
                    dve.tensor_tensor(xl[:, ft, :], xr[:, ft, :], xh[:, ft, :].bitcast(F32), ALU.subtract)\
                       .then_inc(xn_split, 1)

                dst = xn if splits is None else xr
                for ft in range(DT):
                    ins = dve.scalar_tensor_tensor(out=dst[:, ft, :], in0=hT[:, ft, :], scalar=par(q, ft),
                                                   in1=sg[:, 1, :], op0=ALU.mult, op1=ALU.mult)
                    if last:
                        ins.then_inc(y_done, 1)
                    elif splits is not None:
                        ins.then_inc(xr_done, 1)
                        if ft:
                            low(ft - 1)
                if splits is not None:
                    low(DT - 1)
                elif not last:
                    ins.then_inc(xn_done, 1)

            def ffn(f, n, following=None):
                def hidden(name, before):
                    def finish(i, s):
                        dve.wait_ge(gate_done[s], i + (before + 1))
                        dve.tensor_tensor(halves(sg[:, s, :]), halves(sg[:, s, :]), bank2(4 * s + 2), ALU.mult)\
                           .then_inc(taken[s], 1)
                        dve.wait_ge(hid_hi[s], i + (before + 1))
                        t = bass.ds(2 * i + s, 1)
                        dve.tensor_tensor(hl[:, t, :].rearrange("p o c -> p (o c)"), sg[:, s, :],
                                          hh[:, t, :].rearrange("p o c -> p (o c)").bitcast(F32), ALU.subtract)\
                           .then_inc(hid_done[s], 1)
                    return finish

                pipeline(f"inA{f}", hidden(f"inA{f}", f * FT // 2), f"outA{f}")
                pipeline(f"outA{f}", add(f"outA{f}", 1, 0.5), f"inB{f}")
                pipeline(f"inB{f}", hidden(f"inB{f}", f * FT // 2 + FTA // 2), f"outB{f}")
                clear(n)
                pipeline(f"outB{f}", add(f"outB{f}", 1, 0.5, n), following)

            def add(name, tiles, factor, n=None):
                k0 = STAGES[name][0]

                def finish(i, s):
                    dve.wait_ge(multiplied[s], i + (k0 + 1))
                    for m in range(tiles):
                        dst = hT[:, bass.ds((2 * i + s) * tiles + m, 1), :]\
                            .rearrange("p o (h c) -> p (o h) c", h=2)
                        ins = dve.scalar_tensor_tensor(out=dst, in0=bank2(4 * s + 2 * m), scalar=factor,
                                                       in1=dst, op0=ALU.mult, op1=ALU.add)
                    ins.then_inc(taken[s], 1)
                    if n is not None:
                        for m in range(tiles):
                            sum_square(n, (2 * i + s) * tiles + m, m if tiles == 2 else s)
                return finish

            seen = [0, 0, 0, 0]

            def empty(b):
                seen[b] += 1
                dve.wait_ge(filled[b], seen[b])
                return pst[:, 2 * b:2 * b + 2, :]

            def skip(*bs):
                for b in bs:
                    seen[b] += 1

            dve.wait_ge(const_in, 32)
            dve.memset(eps[:], RMS_EPS).then_inc(eps_set, 1)
            clear(0)
            do(dve.tensor_scalar(const[:, C_PAR + 21 * 8:C_PAR + 22 * 8],
                                 const[:, C_PAR + Q_KA * 8:C_PAR + Q_KA * 8 + 8], -1.0, 1.0, ALU.mult, ALU.add))
            for ft in range(DT):
                sum_square(0, ft, ft % 2)
            split("inA0", 0, 0)
            norm(0, Q_G00, 0)
            ffn(0, 1)
            norm(1, Q_G01)
            dve.wait_ge(xn_done, 1)

            dve.wait_ge(lora_in, 16 * 8)
            dv = xn[:, :, SEQ:].rearrange("p f (b t) -> p f b t", t=DEC_T)
            dx = xx[:, :, SEQ:].rearrange("p f (b t) -> p f b t", t=DEC_T)
            do(dve.tensor_tensor(xx[:, :, 1:SEQ], xn[:, :, 0:SEQ - 1], xn[:, :, 1:SEQ], ALU.subtract))
            do(dve.tensor_scalar(xx[:, :, 0:1], xn[:, :, 0:1], -1.0, None, ALU.mult))
            do(dve.tensor_tensor(dx[:, :, :, 1:DEC_T], dv[:, :, :, 0:DEC_T - 1], dv[:, :, :, 1:DEC_T], ALU.subtract))
            do(dve.tensor_tensor(dx[:, :, :, 0], shift0, dv[:, :, :, 0], ALU.subtract))
            do(dve.tensor_copy(shifts[:, :, 0:1], xn[:, :, SEQ - 1:SEQ]))
            dve.tensor_copy(shifts[:, :, 1:9], dv[:, :, :, DEC_T - 1]).then_inc(shifts_done, 1)
            own.wait()
            for c, dst in ((3, xs_w), (4, xs_a), (5, xs_g), (0, xs_r), (1, xs_k), (2, xs_v)):
                for ft in range(DT):
                    ins = dve.scalar_tensor_tensor(out=dst[:, ft, :], in0=xx[:, ft, :], scalar=par(Q_MU + c, ft),
                                                   in1=xn[:, ft, :], op0=ALU.mult, op1=ALU.add)
                ins.then_inc(xs_done, 1)
            for ft in range(DT):
                dve.wait_ge(lw_sig, 2 * ft + 1)
                if ft == 0:
                    dve.wait_ge(xs_done, 6)
                dve.tensor_tensor_scan(cumw[:, ft, :], reset, sigw[:, ft, :], 0.0, ALU.mult, ALU.add)\
                   .then_inc(cum_done, 1)
            dve.wait_ge(lora_act, 4)
            for m in range(DT):
                if m:
                    dve.wait_ge(bonus_mm, m)
                dve.wait_ge(cum_done, m + 1)
                dve.wait_ge(lw_sig, 2 * m + 2)
                if m:
                    dve.wait_ge(temps_free, m)
                if m == 0:
                    dve.wait_ge(lw_sig, 2 * DT)
                dve.tensor_tensor(KP, cumw[:, m, :], sigw[:, m, :], ALU.subtract).then_inc(diff_done, 1)
                dve.wait_ge(taken[m % 2], STAGES["rk"][0] + m // 2 + 1)
                do(dve.tensor_scalar(KK_, KR, par(Q_KK, m), None, ALU.mult))
                own.wait()
                dve.tensor_tensor(SQ, KK_, KK_, ALU.mult).then_inc(kksq_done, 1)
                dve.wait_ge(kksum_done, m + 1)
                dve.tensor_scalar(halves(SQ), bank2(4), 1e-24, None, ALU.max).then_inc(kkmax_done, 1)
                dve.wait_ge(exps_done, m + 1)
                do(dve.tensor_scalar(KP, a_t[:, m, :], par(Q_KA, m), par(21, m), ALU.mult, ALU.add))
                do(dve.tensor_tensor(t_r[:, m, :], RR, EP, ALU.mult))
                own.wait()
                do(dve.tensor_tensor(KP, KP, KR, ALU.mult))
                do(dve.tensor_copy(wc[:, m, 0:8], EP[:, CH - 1:SEQ:CH]))
                do(dve.tensor_copy(wc[:, m, 8:16], EP[:, SEQ + DEC_T - 1:TOK:DEC_T]))
                dve.wait_ge(kkroot_done, m + 1)
                do(dve.reciprocal(SQ, SQ))
                own.wait()
                do(dve.tensor_tensor(KK_, KK_, SQ, ALU.mult))
                own.wait()
                do(dve.scalar_tensor_tensor(out=t_a[:, m, :], in0=KK_, scalar=-1.0, in1=EX,
                                            op0=ALU.mult, op1=ALU.mult))
                do(dve.tensor_tensor(KR, KK_, a_t[:, m, :], ALU.mult))
                dve.scalar_tensor_tensor(out=SQ, in0=RR, scalar=par(Q_RK, m), in1=KP,
                                         op0=ALU.mult, op1=ALU.mult).then_inc(rk_done, 1)
                own.wait()
                do(dve.tensor_tensor(t_b[:, m, :], KR, EN, ALU.mult))
                dve.tensor_tensor(t_k[:, m, :], KP, EN, ALU.mult).then_inc(temps_free, 1)
            dve.wait_ge(bonus_mm, DT)
            dve.wait_ge(temps_free, DT)

            def flat(ap):
                return ap.rearrange("p b c -> p (b c)")

            def by_head(ap, c):
                return ap.rearrange("p (a c) -> p a c", a=NH)[:, :, 0:c]

            st_ready_n = [1]
            dve.memset(st[:], 0.0).then_inc(st_ready, 1)
            for u in range(5):
                c, n, levels = (64, P, LEVELS_P) if u < 4 else (32, 32, LEVELS_D)

                def mask(x, n=n, c=c, u=u):
                    o = (C_MP if u < 4 else C_MD) + x * c
                    return const[0:n, o:o + c].unsqueeze(1).to_broadcast([n, NH, c])

                eye = const[0:n, C_I:C_I + c].unsqueeze(1).to_broadcast([n, NH, c])
                skip(0, 1, 2)

                def masked(dst, b, x, n=n, c=c):
                    return dve.tensor_tensor(by_head(dst[0:n], c), by_head(flat(empty(b)[0:n]), c), mask(x), ALU.mult)

                masked(ABT, 3, M_STRICT).then_inc(emptied[3], 1)
                do(masked(X_, 0, M_LOW))
                dve.wait_ge(emptied[3], seen[3])
                do(dve.tensor_tensor(by_head(XT[0:n], c), by_head(ABT[0:n], c), mask(M_UP), ALU.mult))
                own.wait()
                dve.tensor_tensor(by_head(X_[0:n], c), by_head(X_[0:n], c), eye, ALU.add).then_inc(emptied[0], 1)
                dve.tensor_tensor(by_head(XT[0:n], c), by_head(XT[0:n], c), eye, ALU.add).then_inc(xt_ready, 1)
                masked(AKT, 1, M_STRICT).then_inc(emptied[1], 1)
                masked(RBT, 2, M_INCL).then_inc(emptied[2], 1)
                masked(RKT, 3, M_INCL).then_inc(emptied[3], 1)
                dve.wait_ge(emptied[0], seen[0])
                dve.wait_ge(xt_ready, u + 1)
                for x in range(len(levels)):
                    skip(0)
                    if x < len(levels) - 1:
                        buf = by_head(flat(empty(1)[0:n]), c)
                        dve.tensor_tensor(by_head(X_[0:n], c), by_head(X_[0:n], c), buf, ALU.add)\
                           .then_inc(emptied[1], 1)
                    buf = by_head(flat(empty(2)[0:n]), c)
                    dve.tensor_tensor(by_head(XT[0:n], c), by_head(XT[0:n], c), buf, ALU.add)\
                       .then_inc(emptied[2], 1)
                    if x < len(levels) - 1:
                        dve.wait_ge(emptied[1], seen[1])
                        dve.wait_ge(emptied[2], seen[2])
                if u < 4:
                    for q in range(2):
                        skip(3, 1, 0)
                        buf = flat(empty(2))[:, 0:512].rearrange("p (f i) -> p f i", f=DT)
                        dve.wait_ge(st_ready, st_ready_n[0])
                        dve.tensor_tensor(st[:], st[:], buf, ALU.add).then_inc(emptied[2], 1)
                        dve.wait_ge(emptied[2], seen[2])
                        w = wc[:, :, 2 * u + q:2 * u + q + 1].to_broadcast([P, DT, HD])
                        dve.tensor_tensor(st[:], st[:], w, ALU.mult).then_inc(st_ready, 1)
                        st_ready_n[0] += 1
                else:
                    skip(3)
                    dve.wait_ge(emptied[3], seen[3])
                    skip(1)
                    buf = flat(empty(0)[0:32]).rearrange("p (f k i) -> p k f i", f=DT, k=2)
                    pp = PP[0:32].rearrange("p (k f i) -> p k f i", k=2, f=DT)
                    for k in range(2):
                        ins = dve.tensor_tensor(pp[:, k], pp[:, k], buf[:, k], ALU.add)
                    ins.then_inc(emptied[0], 1)
                    skip(2)
                    dve.wait_ge(emptied[1], seen[1])
                    buf = empty(1)
                    for p in range(2):
                        f = slice(64 * p, 64 * p + 64)
                        src = buf[f, p, :].rearrange("p (f t) -> p f t", f=DT)[:, :, 0:32]
                        ins = dve.tensor_tensor(t_r[f, :, SEQ:TOK], src, y0[f, :, 1, :], ALU.add)
                    ins.then_inc(emptied[1], 1)
                    for ft in range(DT):
                        b = 2 + ft % 2
                        buf = empty(b)[:, 0, :].rearrange("p (b i) -> p b i", b=DEC_B)
                        dve.tensor_tensor(s0T[:, ft], s0T[:, ft], buf, ALU.add).then_inc(emptied[b], 1)
                        dve.wait_ge(emptied[b], seen[b])
                        w = wc[:, ft, 8:16].unsqueeze(2).to_broadcast([P, DEC_B, HD])
                        dve.tensor_tensor(s0T[:, ft], s0T[:, ft], w, ALU.mult).then_inc(wkv_ready, 1)
            first_seen = list(seen)
            for ft in range(DT):
                buf = empty(ft % 4)[:, :, 0:HALF]
                dve.scalar_tensor_tensor(out=halves(t_r[:, ft, :]), in0=buf, scalar=-1.0 / HD,
                                         in1=halves(t_r[:, ft, :]), op0=ALU.mult, op1=ALU.add)\
                   .then_inc(emptied[ft % 4], 1)
            for ft in range(DT):
                buf = empty(ft % 4)[:, :, 0:HALF]
                dve.tensor_scalar(halves(t_k[:, ft, :]), buf, 1.0 / HD, GN_EPS, ALU.mult, ALU.add)\
                   .then_inc(emptied[ft % 4], 1)
            for ft in range(DT):
                dve.wait_ge(gn_root, ft + 1)
                do(dve.reciprocal(t_k[:, ft, :], t_k[:, ft, :]))
                dve.wait_ge(emptied[ft % 4], first_seen[ft % 4] + 1 + ft // 4)
                own.wait()
                do(dve.tensor_tensor(t_r[:, ft, :], t_r[:, ft, :], t_k[:, ft, :], ALU.mult))
                own.wait()
                do(dve.tensor_scalar(t_r[:, ft, :], t_r[:, ft, :], par(Q_LNW, ft), par(Q_LNB, ft),
                                     ALU.mult, ALU.add))
            for ft in range(DT):
                buf = empty(ft % 4)[:, :, 0:HALF]
                do(dve.tensor_tensor(halves(t_a[:, ft, :]), halves(t_v[:, ft, :]), buf, ALU.mult))
                own.wait()
                dve.tensor_tensor(t_r[:, ft, :], t_r[:, ft, :], t_a[:, ft, :], ALU.add)\
                   .then_inc(emptied[ft % 4], 1)
            for ft in range(DT):
                buf = empty(ft % 4)[:, :, 0:HALF]
                dve.wait_ge(emptied[ft % 4], first_seen[ft % 4] + 5 + ft // 4)
                dve.tensor_tensor(halves(t_r[:, ft, :]), halves(t_r[:, ft, :]), buf, ALU.mult)\
                   .then_inc(emptied[ft % 4], 1)
            clear(2)
            finish = add("wo", 2, 1.0, 2)
            with dve.Fori(0, STAGES["wo"][1]) as i:
                for s in range(2):
                    finish(i, s)
            split("inA1", 0, 0)
            dve.wait_ge(wkv_out, 32)
            norm(2, Q_G02, 1)
            ffn(1, 3)
            norm(3, Q_KVN)

            for kv in range(2):
                dve.wait_ge(cprod, kv + 1)
                dve.tensor_reduce(cred[:, kv, :], ctmp.rearrange("p s c -> p c s"), AX, ALU.add)\
                   .then_inc(cred_done, 1)
            dve.wait_ge(cmp_mm, 3)
            dve.tensor_copy(ar(KEYS, 4, TOK), kvT[:, 0:4, :]).then_inc(keys_kept, 1)
            split("inA2", 0, 0)
            clear(4)
            for ft in range(DT):
                sum_square(4, ft, ft % 2)
            norm(4, Q_G10, 2)
            ffn(2, 5, "q")
            norm(5, Q_G11, 3)
            pairs = STAGES["q"][1]
            for n in range(1, 2 * pairs):
                split("q", n // 2, n % 2)

            dve.wait_ge(gate_tr, 1)
            dve.tensor_copy(gS, pst[0:32, 2, 192:240]).then_inc(gates_s, 1)
            do(dve.tensor_copy(g_p[:], pst[:, 2, 0:192].rearrange("p (t c) -> p t c", t=4)))
            own.wait()
            g0 = g_p[:, 0, :].rearrange("p (h c) -> p h c", c=3)[:, :, 0]
            dve.wait_ge(att_in, 16)
            dve.tensor_scalar(g0, g0, cbias[:, 2:3], None, ALU.mult).then_inc(gates_done, 1)
            dve.wait_ge(gates_done, 1)
            dve.wait_ge(taken[0], STAGES["q"][0] + 2)
            dve.wait_ge(taken[1], STAGES["q"][0] + 2)
            dve.wait_ge(qbd_zero, 1)
            for x in range(2):
                for p in range(2):
                    f = slice(64 * p, 64 * p + 64)
                    src = qT[f, 4 * x:4 * x + 4, SEQ:TOK].rearrange("p g (b t) -> p g b t", t=DEC_T)
                    dst = qbd[f, x].rearrange("p b (x k g t) -> p x k g b t", x=2, k=2, g=4)[:, x, p]
                    for g in range(4):
                        ins = dve.tensor_copy(dst[:, g], src[:, g])
                    ins.then_inc(qbd_done, 1)

            E = 2 * DT * 4

            def bias_max(e):
                hh, qt, s, x = e // 4, e % 4, sbuf[e % 4], e % 2
                nk = P * (qt + 1)
                if qt == 0:
                    dve.wait_ge(bias_ready, hh + 1)
                dh = ar(ATAB + T_DH + 640 * (hh % 2), 640)
                dve.wait_ge(score_mm, e + 1)
                if e >= 4:
                    dve.wait_ge(turned, 3 * (e - 3))
                for n, (c, bank, c0, w, t) in enumerate((
                        (1024, 4, 0, NCMP, 512 + qt * NCMP), (0, 2 * (e % 2), 0, nk, (3 - qt) * P),
                        (512, 2 * (e % 2) + 1, 0, nk, (3 - qt) * P))):
                    dve.tensor_tensor_reduce(s[:, c:c + w], pst[:, bank, c0:c0 + w], dh[:, t:t + w], 1.0, -3e38,
                                             ALU.add, ALU.max, sm[:, x, n:n + 1]).then_inc(score_taken, 1)
                dve.wait_ge(score_taken, 3 * e + 3)
                dve.tensor_scalar(sm[:, x, 4:7], sm[:, x, 0:3], -1.0, None, ALU.mult).then_inc(negmax, 1)

            def scale(e):
                hh, qt, s, x = e // 4, e % 4, sbuf[e % 4], e % 2
                nk = P * (qt + 1)
                h = head_of(hh // 2, hh % 2)
                dve.wait_ge(exp_done, e + 1)
                do(dve.reciprocal(sm[:, x, 12:15], sm[:, x, 8:11]))
                own.wait()
                do(dve.tensor_tensor(sm[:, x, 8:11], sm[:, x, 12:15],
                                     g_p[:, qt, 3 * h:3 * h + 3], ALU.mult))
                own.wait()
                for n, c in ((1, slice(0, nk)), (2, slice(512, 512 + nk)), (0, slice(1024, 1024 + NCMP))):
                    ins = dve.tensor_scalar(s[:, c], s[:, c], sm[:, x, 8 + n:9 + n], None, ALU.mult)
                ins.then_inc(p_ready, 1)

            def take_out(hh):
                i, p = hh // 2, hh % 2
                f = slice(64 * p, 64 * p + 64)
                dve.wait_ge(o_mm, 4 * hh + 4)
                dve.tensor_copy(oT[f, i, 0:SEQ], pst[f, 5, :]).then_inc(o_taken, 1)

            for e in range(E + 1):
                if e < E:
                    bias_max(e)
                if e >= 1:
                    scale(e - 1)
                if e >= 8 and e % 4 == 0 and e < E:
                    take_out(e // 4 - 2)

            dve.wait_ge(gates_d_in, 16 * DEC_B)
            for u in range(4):
                e = E + u
                s, x, bank = sbuf[u], u % 2, 2 * (u % 2)
                dve.wait_ge(score_mm, e + 1)
                dve.wait_ge(turned, 3 * (e - 3))
                dve.wait_ge(p_ready, e)
                dd = att[:, T_DD + 192 * u:T_DD + 192 * u + 192]
                dc = att[:, T_DD + 768:T_DD + 1024]
                do(dve.tensor_tensor(s[:, 0:128], pst[:, bank, 0:128], dd[:, 0:128], ALU.add))
                do(dve.tensor_tensor(s[:, 384:416], pst[:, bank, 128:160], dd[:, 128:160], ALU.add))
                dve.tensor_tensor(s[:, 672:704], pst[:, bank, 160:192], dd[:, 160:192], ALU.add)\
                   .then_inc(score_taken, 1)
                do(dve.tensor_tensor(s[:, 128:384], pst[:, bank + 1, 0:256], dc, ALU.add))
                dve.tensor_tensor(s[:, 416:672], pst[:, bank + 1, 256:512], dc, ALU.add).then_inc(score_taken, 1)
                own.wait()
                dve.wait_ge(score_taken, 3 * E + 2 * u + 2)
                for n, c in enumerate((slice(0, 128), slice(128, 416), slice(416, 704))):
                    do(dve.tensor_reduce(sm[:, x, n:n + 1], s[:, c], AX, ALU.max))
                own.wait()
                dve.tensor_scalar(sm[:, x, 4:7], sm[:, x, 0:3], -1.0, None, ALU.mult).then_inc(negmax, 1)
                dve.wait_ge(exp_done, e + 1)
                do(dve.reciprocal(sm[:, x, 12:15], sm[:, x, 8:11]))
                own.wait()
                do(dve.tensor_tensor(sm[:, x, 8:11], sm[:, x, 12:15], g_d[:, u, :], ALU.mult))
                own.wait()
                for n, c in enumerate((slice(0, 128), slice(128, 416), slice(416, 704))):
                    ins = dve.tensor_scalar(s[:, c], s[:, c], sm[:, x, 8 + n:9 + n], None, ALU.mult)
                ins.then_inc(p_ready, 1)
                if u == 0:
                    take_out(NH - 2)
                    take_out(NH - 1)
            dve.wait_ge(o_mm, E + 4)
            for x in range(2):
                for p in range(2):
                    f = slice(64 * p, 64 * p + 64)
                    src = pst[f, 4, :].rearrange("p (b x k g t) -> p x k g b t", b=DEC_B, x=2, k=2, g=4)[:, x, p]
                    dst = oT[f, 4 * x:4 * x + 4, SEQ:TOK].rearrange("p g (b t) -> p g b t", t=DEC_T)
                    for g in range(4):
                        ins = dve.tensor_copy(dst[:, g], src[:, g])
                    ins.then_inc(o_taken, 1)
            split("bo", 0, 0)
            for ft in range(DT):
                dve.wait_ge(oh_done, ft + 1)
                dve.tensor_tensor(xl[:, ft, :], oT[:, ft, :], xh[:, ft, :].bitcast(F32), ALU.subtract)\
                   .then_inc(o_split, 1)
            clear(6)
            pipeline("bo", add("bo", 2, 1.0, 6), "inA3")
            norm(6, Q_G12, 4)
            ffn(3, 7)
            norm(7, Q_FIN, last=True)

        @block.gpsimd
        def _(pool):
            own = Steps(pool, pool_step)
            pool.dma_start(const[:, 0:C_PAR], I["const"]).then_inc(const_in, 16)
            pool.dma_start(const[:, C_PAR:C_PAR + 21 * 8], I["params"]).then_inc(const_in, 16)
            for dst, src in ((w_w1, "w1"), (w_a1, "a1"), (w_g1, "g1"), (w_w2, "w2"), (w_a2, "a2"),
                             (shift0, "shift0")):
                pool.dma_start(dst, I[src]).then_inc(lora_in, 16)
            pool.dma_start(w_g2a, I["g2"][0:P]).then_inc(lora_in, 16)
            pool.dma_start(w_g2b, I["g2"][P:160]).then_inc(lora_in, 16)
            pool.dma_start(expand, I["expand"]).then_inc(expand_in, 16)
            pool.dma_start(ptab[:], I["page_table"]).then_inc(table_in, 16)
            pool.dma_start(cbias[:, 2:3], I["valid"]).then_inc(att_in, 16)
            pool.dma_start(O["s_wink"][:, :, :, 0:PAST - DEC_T], I["win_k"][:, :, :, DEC_T:PAST])\
                .then_inc(win_out, 16)
            pool.dma_start(O["s_winv"][:, 0:PAST - DEC_T, :], I["win_v"][:, DEC_T:PAST, :]).then_inc(win_out, 16)
            pool.wait_ge(shifts_done, 1)
            pool.dma_start(O["shifts"], shifts).then_inc(shift_out, 16)

            for u in range(5):
                c, n, levels = (64, P, LEVELS_P) if u < 4 else (32, 32, LEVELS_D)
                if u == 4:
                    pool.wait_ge(filled[3], 4 * u + 2)
                    pool.dma_start(s0T, I["s_wkv"]).then_inc(s0_in, 16)
                for x in range(len(levels)):
                    pool.wait_ge(emptied[3], 4 * u + 1)
                    if u or x:
                        pool.wait_ge(filled[0], 9 * u + 2 + x if x else 9 * u - 2)
                    o = (C_MP if u < 4 else C_MD) + (M_UP + 1 + x) * c
                    m = const[0:n, o:o + c].unsqueeze(1).to_broadcast([n, NH, c])
                    al = AL[0:n].rearrange("p (a c) -> p a c", a=NH)[:, :, 0:c]
                    ab = ABT[0:n].rearrange("p (a c) -> p a c", a=NH)[:, :, 0:c]
                    pool.tensor_tensor(al, ab, m, ALU.mult).then_inc(al_ready, 1)
            pool.wait_ge(st_ready, 9)
            pool.dma_start(O["p_wkv"], st[:]).then_inc(wkv_out, 16)
            pool.wait_ge(emptied[2], 40)
            for ft in range(DT):
                if ft:
                    f = ft - 1
                    pool.wait_ge(filled[2 + f % 2], (20 if f % 2 else 41) + f // 2)
                for p in range(2):
                    h, o = 2 * ft + p, p * 512 + ft * 64
                    seq = const[0:32, C_SEQ:C_SEQ + DEC_B].unsqueeze(2).to_broadcast([32, DEC_B, HD])
                    for n, src in enumerate((UU[0:32, o:o + 64], V_[0:32, h * 64:h * 64 + 64])):
                        dst = um[:, p, n, :].rearrange("p (b i) -> p b i", b=DEC_B)
                        own.do(pool.tensor_tensor(dst, src.unsqueeze(1).to_broadcast([32, DEC_B, HD]), seq, ALU.mult))
                own.wait()
                pool.sem_inc(um_ready, 1)
            pool.wait_ge(wkv_ready, DT)
            pool.dma_start(O["s_wkv"], s0T).then_inc(wkv_out, 16)

            k = end_of("wo")
            pool.wait_ge(multiplied[0], k)
            pool.wait_ge(multiplied[1], k)
            pool.wait_ge(shift_out, 16)
            for p in range(2):
                pool.dma_start(cw1[64 * p:64 * p + 64], I["cw1"]).then_inc(cw_in, 16)
            k = end_of("outB1")
            pool.wait_ge(multiplied[0], k)
            pool.wait_ge(multiplied[1], k)
            pool.dma_start(cw2, I["cw2"]).then_inc(cw_in, 16)
            pool.dma_start(cpos, I["cpos"]).then_inc(cw_in, 16)
            pool.wait_ge(table_in, 16)
            with pool.Fori(0, DEC_B * NPG) as i:
                page = pool.value_load(ptab[0:1, bass.ds(i, 1)], min_val=0, max_val=I["pages"].shape[0] - 1)
                src = I["pages"][bass.ds(page, 1), :, 0:512].rearrange("o p (a t) -> p (o a) t", a=4)
                dst = cmpT.rearrange("p a b c -> p (a b) c")[:, :, bass.ds(SEQ + i * PAGE, PAGE)]
                pool.dma_start(dst, src).then_inc(cache_cmp_in, 16)
            pool.memset(chid[:, :, :, NBLK:NBLK + 1], 0.0).then_inc(chid_zero, 1)
            pool.wait_ge(cw_in, 64)
            for kv in range(2):
                if kv:
                    pool.wait_ge(cred_done, kv)
                pool.tensor_tensor(ctmp, cw1[0:64, kv], cpos[:, kv, :].unsqueeze(2).to_broadcast([64, 32, P]),
                                   ALU.mult).then_inc(cprod, 1)
            k = end_of("kv")
            pool.wait_ge(taken[0], k)
            pool.wait_ge(taken[1], k)
            pool.dma_start(O["kv"], kvT).then_inc(kv_out, 16)
            pool.wait_ge(keys_kept, 1)
            for x in range(2):
                pool.dma_start(O["s_wink"][:, :, x, PAST - DEC_T:PAST].rearrange("b p t -> p b t"),
                               kwin[:, x, SEQ:TOK].rearrange("p (b t) -> p b t", t=DEC_T)).then_inc(win_out, 16)
            pool.wait_ge(vt_ev, 10)
            for b in range(DEC_B):
                pool.dma_start(O["s_winv"][b, PAST - DEC_T:PAST, :], v_new[DEC_T * b:DEC_T * b + DEC_T, 1, :])\
                    .then_inc(win_out, 16)
            pool.dma_start(att, I["att"]).then_inc(att_in, 16)
            k = end_of("outB2")
            pool.wait_ge(multiplied[0], k)
            pool.wait_ge(multiplied[1], k)
            pool.dma_start(wgt, I["w_gate"]).then_inc(gate_w_in, 16)
            pool.wait_ge(xn_split, DT * 4)
            pool.memset(sg[:].rearrange("p a b -> p (a b)")[:, 0:1024], 0.0).then_inc(qbd_zero, 1)
            pool.wait_ge(att_in, 32)

            def bias(hh):
                if hh >= 2:
                    pool.wait_ge(score_taken, 12 * (hh - 1))
                dst = ar(ATAB + T_DH + 640 * (hh % 2), 640)
                pool.tensor_scalar(dst, att[:, 0:640], SLOPES[head_of(hh // 2, hh % 2)], None, ALU.mult)\
                    .then_inc(bias_ready, 1)

            bias(0)
            bias(1)
            pool.wait_ge(gate_mm, 1)
            pool.dma_start(kwin_c, I["win_k"].rearrange("b p x t -> p b x t")).then_inc(caches_in, 16)
            for part in range(4):
                with pool.Fori(4 * part, 4 * part + 4) as i:
                    page = pool.value_load(ptab[0:1, bass.ds(i, 1)], min_val=0, max_val=I["pages"].shape[0] - 1)
                    pool.dma_start(kslc_c[:, bass.ds(i, 1)].rearrange("p o x t -> p (o x t)"),
                                   I["pages"][bass.ds(page, 1), :, 512:768].rearrange("o p c -> p (o c)"))\
                        .then_inc(caches_in, 16)
                    pool.dma_start(vslc_c[:, bass.ds(i, 1), :].rearrange("p o c -> p (o c)"),
                                   I["pages"][bass.ds(page, 1), :, 768:1024].rearrange("o p c -> p (o c)"))\
                        .then_inc(caches_in, 16)
                bias(2 + part)
            pool.dma_start(vwin_c, I["win_v"].rearrange("b (g p) c -> p (b g) c", g=NPG)).then_inc(vwin_in, 16)
            pool.wait_ge(gates_s, 1)
            pool.dma_start(I["scratch"], gS).then_inc(gates_d_out, 16)
            pool.wait_ge(gates_d_out, 16)
            for b in range(DEC_B):
                pool.dma_start(g_d[64 * (b % 2):64 * (b % 2) + 64, b // 2, :],
                               I["scratch"].rearrange("(b t) (h c) -> b h t c", c=3, t=DEC_T)[b])\
                    .then_inc(gates_d_in, 16)
            for hh in range(6, NH):
                bias(hh)


def tiles_of(w, group):
    k, n = w.shape[-2:]
    lead = w.shape[:-2]
    x = w.reshape(*lead, k // P, P, n // P // group, group, P)
    d = len(lead)
    x = x.transpose(*range(d), d + 2, d + 1, d + 3, d + 0, d + 4)
    return np.ascontiguousarray(x).reshape(*lead, n // P // group, P, group * k)


def by_feature(v):
    return np.moveaxis(v.reshape(*v.shape[:-1], DT, P), -1, 0)


_OUTS = {"y": (P, DT, TOK), "shifts": (P, DT, 9), "p_wkv": (P, DT, HD), "s_wkv": (P, DT, DEC_B, HD),
         "kv": (P, 12, TOK), "s_wink": (DEC_B, P, 2, PAST), "s_winv": (DEC_B, PAST, 256)}


def kernel(**inputs):
    import concourse.bacc as bacc
    from concourse.bass_utils import run_bass_kernel_spmd

    a = {k: np.asarray(v) for k, v in inputs.items()}
    n_pool = a["cache_cs"].shape[0]
    head_order = [head_of(i, p) for i in range(DT) for p in range(2)]
    cols = np.concatenate([np.arange(h * HD, h * HD + HD) for h in head_order])
    const, expand, att, valid = constants()

    x = np.concatenate([a["x_prompt"].reshape(SEQ, D), a["x_sample"].reshape(DEC_B * DEC_T, D)])
    w_in = a["ffn_w_in"].reshape(4, DT, P, 2, FT, P).transpose(0, 4, 2, 3, 1, 5).reshape(4, FT, P, 2048)
    w_out = a["ffn_w_out"].reshape(4, FT, P, DT, P).transpose(0, 3, 2, 1, 4).reshape(4, DT, P, DFF)
    rkv = a["rw_w_rkv"][0]
    w_rk = rkv[:2].reshape(2, DT, P, DT, P).transpose(3, 2, 0, 1, 4).reshape(DT, P, 2048)
    kv_w = a["kv_w"].reshape(D, 6, 256)[:, [2, 4, 0, 1, 3, 5]].reshape(D, 1536)
    b_in = a["b_w_in"][0]
    cache = a["cache_cs"].reshape(n_pool, PAGE, 4, 2, P)
    pages = np.concatenate([
        cache[:, :, 0:3].transpose(0, 4, 2, 3, 1).reshape(n_pool, P, 6 * PAGE),
        cache[:, :, 3].reshape(n_pool, PAGE, 256)], axis=2)
    win = a["cache_win"].reshape(DEC_B, PAST, 2, 256)
    params = np.concatenate([a["norm_g"].reshape(6, D), a["kv_norm_g"][None], a["final_g"][None], a["rw_mu"][0],
                             a["rw_w0"], a["rw_a0"], a["rw_k_k"], a["rw_k_a"], a["rw_r_k"].reshape(1, D),
                             a["rw_lnx_w"], a["rw_lnx_b"]])
    arrays = {
        "x": by_feature(x).transpose(0, 2, 1),
        "w_in": w_in, "w_out": w_out, "w_rk": w_rk,
        "w_v": tiles_of(rkv[2], 2), "w_o": tiles_of(a["rw_w_o"][0], 2),
        "w_kv": tiles_of(kv_w, 2), "w_q": tiles_of(b_in[:, :D][:, cols], 2),
        "w_bo": tiles_of(a["b_w_o"][0][cols], 2),
        "w_gate": b_in[:, D:].reshape(DT, P, 48).transpose(1, 0, 2),
        "w1": a["rw_w1"][0].reshape(DT, P, 64).transpose(1, 0, 2),
        "a1": a["rw_a1"][0].reshape(DT, P, 64).transpose(1, 0, 2),
        "g1": a["rw_g1"][0].reshape(DT, P, 160).transpose(1, 0, 2),
        "w2": a["rw_w2"][0], "a2": a["rw_a2"][0], "g2": a["rw_g2"][0],
        "shift0": by_feature(a["state_shift"][0]).transpose(0, 2, 1),
        "s_wkv": a["state_wkv"][0].reshape(DEC_B, DT, 2, HD, HD).transpose(2, 4, 1, 0, 3).reshape(P, DT, DEC_B, HD),
        "const": const[:, :C_PAR], "params": by_feature(params).reshape(P, 21 * 8),
        "expand": expand, "att": att, "valid": valid,
        "pages": pages, "page_table": a["page_table"].reshape(1, DEC_B * NPG),
        "win_k": win[:, :, 0].reshape(DEC_B, PAST, 2, P).transpose(0, 3, 2, 1), "win_v": win[:, :, 1],
        "cw1": a["cmp_w1"].reshape(2, 32, HD, P).transpose(2, 0, 1, 3),
        "cw2": a["cmp_w2"].transpose(1, 0, 2), "cpos": a["cmp_pos"].transpose(2, 0, 1),
    }
    nc = bacc.Bacc("TRN2", target_bir_lowering=False, num_devices=1)
    in_map, I, O = {}, {}, {}
    for name, v in arrays.items():
        v = np.ascontiguousarray(v)
        in_map[f"in_{name}"] = v
        I[name] = nc.dram_tensor(f"in_{name}", v.shape, mybir.dt.from_np(v.dtype), kind="ExternalInput").ap()
    I["scratch"] = nc.dram_tensor("scratch", (DEC_B * DEC_T, 48), F32, kind="Internal").ap()
    for name, shape in _OUTS.items():
        O[name] = nc.dram_tensor(f"out_{name}", shape, F32, kind="ExternalOutput").ap()
    program(nc, I, O)
    r = run_bass_kernel_spmd(nc, [in_map], core_ids=[0]).results[0]
    r = {name: np.asarray(r[f"out_{name}"]) for name in _OUTS}

    y = r["y"].transpose(2, 1, 0).reshape(TOK, D)
    shifts = r["shifts"].transpose(2, 1, 0).reshape(9, D)
    p_wkv = r["p_wkv"].reshape(2, HD, DT, HD).transpose(2, 0, 3, 1).reshape(1, 1, NH, HD, HD)
    s_wkv = r["s_wkv"].reshape(2, HD, DT, DEC_B, HD).transpose(3, 2, 0, 4, 1).reshape(1, DEC_B, NH, HD, HD)
    kv = r["kv"].transpose(2, 1, 0).reshape(TOK, 6, NKV, HD)
    cs, win_new = kv[:, [2, 3, 0, 4]], kv[:, [1, 5]]
    s_win = np.stack([r["s_wink"].transpose(0, 3, 2, 1).reshape(DEC_B, PAST, NKV, HD),
                      r["s_winv"].reshape(DEC_B, PAST, NKV, HD)], axis=2)
    return (np.ascontiguousarray(y[:SEQ]).reshape(1, SEQ, D), np.ascontiguousarray(y[SEQ:]).reshape(DEC_B, DEC_T, D),
            shifts[0:1].reshape(1, 1, D), p_wkv, np.ascontiguousarray(cs[:SEQ])[None],
            np.ascontiguousarray(win_new[:SEQ])[None], shifts[1:].reshape(1, DEC_B, D), s_wkv,
            np.ascontiguousarray(cs[SEQ:]).reshape(DEC_B, DEC_T, 4, NKV, HD), s_win)
```

```python
import math
from contextlib import ExitStack

import numpy as np

import concourse.bass as bass
from concourse import mybir

F32 = mybir.dt.float32
F32R = mybir.dt.float32r
I32 = mybir.dt.int32
ALU = mybir.AluOpType
ACT = mybir.ActivationFunctionType
AX = mybir.AxisListType.X

P = 128
D = 1024
DT = D // P
SEQ, DEC_B, DEC_T = 512, 8, 4
TOK = SEQ + DEC_B * DEC_T
HALF = TOK // 2
DFF = 2816
FT = DFF // P
FTA = 12
FTB = FT - FTA
NH, HD, NKV = 16, 64, 4
PAST, PAGE = 256, 128
NPG = PAST // PAGE
CH = 64
NCMP = SEQ // 16
CMPTOK = SEQ + DEC_B * PAST
NBLK = CMPTOK // 16 - 1
RMS_EPS, GN_EPS = 1e-6, 64e-5
DECAY = math.exp(-0.5)
NEG = -1e30
SLOT = DT * TOK
RAW = 2 * D
EV = DT + 1

H0 = 0
XN = SLOT
XH, XL = SLOT, 2 * SLOT
HH = 3 * SLOT
HL = HH + FTA * TOK
WH = HL + FTA * TOK
WL = WH + 2 * RAW
FFN_END = WL + 2 * RAW
XR = HH
S_A, S_R, S_B, S_K, S_V, S_XR, S_XK = (i * SLOT for i in (1, 2, 3, 4, 5, 6, 7))
LORA = 8 * SLOT
GS = LORA + 4352
SHIFT0 = GS + 2 * TOK
G2 = LORA + 5632
BC = G2 + 2048
CHB = S_XR
ARENA = 10 * SLOT
CHID = XN
CMPT = 2 * SLOT
KV = CMPT + 8 * CMPTOK
CW1 = ARENA - 32 * P
KEYS = FFN_END
VTOK = KEYS + 4 * TOK
CSM = VTOK
TAIL = CW1
ATAB = TAIL + 832
KSLC_C, VSLC_C, VWIN_C = XH, XH + 4096, XR
QT = XR + SLOT
ATT = QT + SLOT
SBUF = ATT
KWIN_C = WH
PTB = KWIN_C + 4096

STAGES, _k, _ks = {}, 0, 0


def _stages(*stages):
    global _k, _ks
    for name, pairs, split in stages:
        STAGES[name] = (_k, pairs, _ks if split else None)
        _k += pairs
        _ks += pairs if split else 0


def _ffn_stages(f):
    return ((f"inA{f}", FTA // 2, True), (f"outA{f}", DT // 2, True),
            (f"inB{f}", FTB // 2, True), (f"outB{f}", DT // 2, True))


_stages(*_ffn_stages(0), ("v", 2, False), ("rk", 4, False), ("wo", 2, False), *_ffn_stages(1),
        ("kv", 3, False), *_ffn_stages(2), ("q", 2, True), ("bo", 2, True), *_ffn_stages(3))
COLS = {"inA": 2 * D, "inB": 2 * D, "outA": FTA * P, "outB": FTB * P, "q": 2 * D, "bo": 2 * D}


def cols_of(name):
    return COLS[name.rstrip("0123")]


def end_of(name):
    return STAGES[name][0] + STAGES[name][1]


C_ID, C_ONE, C_BLK, C_HSEL, C_RESET = 0, 128, 256, 384, 512
C_MP = C_RESET + TOK
C_MD = C_MP + 9 * 64
C_I = C_MD + 5 * 32
C_SEQ = C_I + 64
C_PAR = C_SEQ + 8
(Q_G00, Q_G01, Q_G02, Q_G10, Q_G11, Q_G12, Q_KVN, Q_FIN, Q_MU, Q_W0, Q_A0, Q_KK, Q_KA, Q_RK, Q_LNW,
 Q_LNB) = (0, 1, 2, 3, 4, 5, 6, 7, 8, 14, 15, 16, 17, 18, 19, 20)
NPAR = 22
C_ALL = C_PAR + NPAR * 8
M_STRICT, M_INCL, M_LOW, M_UP = 0, 1, 2, 3

T_D0, T_DC, T_DH, T_DD = 0, 512, 640, 640 + 1280
T_PT2 = T_DD + 1024
LEVELS_P, LEVELS_D = (2, 4, 8, 16, 32), (2,)
FILLS23 = (40, 19)


def head_of(i, par):
    return (2 * (i // 4) + par) * 4 + i % 4


SLOPES = [float(np.exp2(np.float32(-8.0 * (h + 1) / NH))) for h in range(NH)]


def constants():
    c = np.zeros((P, C_ALL), np.float32)
    c[:, C_ID:C_ID + P] = np.eye(P)
    c[:, C_ONE:C_ONE + P] = 1.0
    same = (np.arange(P)[:, None] // HD) == (np.arange(P)[None, :] // HD)
    c[:, C_BLK:C_BLK + P] = same
    hs = np.zeros((P, DT, NH), np.float32)
    for ft in range(DT):
        hs[np.arange(P), ft, 2 * ft + np.arange(P) // HD] = 1.0
    c[:, C_HSEL:C_HSEL + DT * NH] = hs.reshape(P, -1)
    reset = np.ones(TOK, np.float32)
    reset[0:SEQ:CH] = 0.0
    reset[SEQ::DEC_T] = 0.0
    c[:, C_RESET:C_RESET + TOK] = reset
    t, s = np.arange(CH)[:, None], np.arange(CH)[None, :]

    def level(m, t, s):
        return ((t // m) % 2 == 1) & (s // m == t // m - 1)

    mp = [(t < s), (t <= s), level(1, t, s)] + [level(m, s, t) for m in (1,) + LEVELS_P]
    for n, m in enumerate(mp):
        c[:, C_MP + n * CH:C_MP + (n + 1) * CH] = np.tile(m, (2, 1))
    n32 = np.arange(32)
    t, s = n32[:, None], n32[None, :]
    own = t // DEC_T == s // DEC_T
    md = [own & (t < s), own & (t <= s), level(1, t, s)] + [level(m, s, t) for m in (1,) + LEVELS_D]
    for n, m in enumerate(md):
        c[0:32, C_MD + n * 32:C_MD + (n + 1) * 32] = m
    c[:, C_I:C_I + CH] = np.tile(np.eye(CH), (2, 1))
    c[0:32, C_SEQ:C_SEQ + DEC_B] = n32[:, None] // DEC_T == np.arange(DEC_B)[None, :]
    expand = np.zeros((NH, DT, P), np.float32)
    for h in range(NH):
        expand[h, h // 2, (h % 2) * HD:(h % 2) * HD + HD] = 1.0
    p = np.arange(P)[:, None]
    d0 = np.arange(SEQ)[None, :] - 384 - p
    att = np.zeros((P, T_PT2), np.float32)
    att[:, T_D0:T_D0 + SEQ] = np.where(d0 <= 0, d0, NEG)
    dc = (16 * np.arange(NCMP)[None, None, :] + 31) - (P * np.arange(4)[None, :, None] + p[:, :, None])
    att[:, T_DC:T_DC + P] = np.where(dc <= 0, dc, NEG).reshape(P, P)
    j, h, tt = np.arange(P) // 64, (np.arange(P) % 64) // DEC_T, np.arange(P) % DEC_T
    slope = np.array(SLOPES, np.float32)[h][:, None]
    pos = (PAST + tt)[:, None]
    dd = np.zeros((P, 4, 192), np.float32)
    for u in range(4):
        b = (2 * u + j)[:, None]
        kb, kn = np.arange(P)[None, :] // 16, np.arange(P)[None, :] % 16
        dist = 16 * kn + 31 - pos
        dd[:, u, 0:P] = np.where((kb == b) & (dist <= 0), dist * slope, NEG)
        nb, nt = np.arange(32)[None, :] // DEC_T, np.arange(32)[None, :] % DEC_T
        dist = nt - tt[:, None]
        new = np.where((nb == b) & (dist <= 0), dist * slope, NEG)
        dd[:, u, 128:160] = new
        dd[:, u, 160:192] = new
    att[:, T_DD:T_DD + 768] = dd.reshape(P, 768)
    att[:, T_DD + 768:T_DD + 1024] = (np.arange(PAST)[None, :] - pos) * slope
    valid = (np.arange(P) >= 31).astype(np.float32)[:, None]
    return c, expand.reshape(NH, D), att, valid


class Steps:

    def __init__(self, engine, sem):
        self.engine, self.sem, self.n = engine, sem, 0

    def do(self, instruction):
        instruction.then_inc(self.sem, 1)
        self.n += 1
        return self.n

    def wait(self, n=None):
        self.engine.wait_ge(self.sem, self.n if n is None else n)


def program(nc, I, O):
    with ExitStack() as ctx:
        def sb(name, shape, dt=F32):
            return ctx.enter_context(nc.sbuf_tensor(name, shape, dt))

        def sem(name):
            return ctx.enter_context(nc.semaphore(name))

        base = -(-nc.sbuf_base // 32) * 32
        arena = sb("arena", [P, ARENA])
        raw = sb("raw", [P, 2, RAW])
        acc = sb("acc", [P, TOK])
        eps = sb("eps", [P, 2])

        def split_at(name, off, *shape):
            return nc.alloc_sbuf_tensor_at(name, [P, *shape], F32R, offset=base + 4 * off)

        xh, xl = split_at("xh", XH, DT, TOK), split_at("xl", XL, DT, TOK)
        hh, hl = split_at("hh", HH, FTA, TOK), split_at("hl", HL, FTA, TOK)
        wh, wl = split_at("wh", WH, 2, RAW), split_at("wl", WL, 2, RAW)
        const = sb("const", [P, C_ALL])
        sg = sb("sg", [P, 2, TOK])
        wc = sb("wc", [P, DT, 16])
        st = sb("st", [P, DT, HD])
        sm = sb("sm", [P, 2, 16])
        cbias = sb("cbias", [P, 4])
        ptab = sb("ptab", [1, DEC_B * NPG], I32)
        pst = ctx.enter_context(nc.psum_tensor("banks", [P, 8, 512], F32))

        def ar(off, *shape, p0=0, p1=P):
            n = 1
            for x in shape:
                n *= x
            v = arena[p0:p1, off:off + n]
            if len(shape) == 2:
                v = v.rearrange("p (a b) -> p a b", a=shape[0])
            elif len(shape) == 3:
                v = v.rearrange("p (a b c) -> p a b c", a=shape[0], b=shape[1])
            elif len(shape) == 4:
                v = v.rearrange("p (a b c d) -> p a b c d", a=shape[0], b=shape[1], c=shape[2])
            return v

        hT, xn = ar(H0, DT, TOK), ar(XN, DT, TOK)
        xr = ar(XR, DT, TOK)
        ident = const[:, C_ID:C_ID + P]
        ones = const[:, C_ONE:C_ONE + P]
        blk = const[:, C_BLK:C_BLK + P]
        hsel = const[:, C_HSEL:C_HSEL + DT * NH].rearrange("p (f h) -> p f h", f=DT)
        reset = const[:, C_RESET:C_RESET + TOK]

        def par(q, ft):
            return const[:, C_PAR + q * 8 + ft:C_PAR + q * 8 + ft + 1]

        def halves(ap):
            return ap.rearrange("p (h c) -> p h c", h=2)

        def bank2(b):
            return pst[:, b:b + 2, 0:HALF]

        xx, xs_w, xs_a, xs_g = ar(S_R, DT, TOK), ar(S_B, DT, TOK), ar(S_K, DT, TOK), ar(S_V, DT, TOK)
        xs_r, xs_k, xs_v = ar(S_XR, DT, TOK), ar(S_XK, DT, TOK), xx
        cumw, sigw, a_t = ar(S_A, DT, TOK), ar(S_B, DT, TOK), ar(S_K, DT, TOK)
        t_a, t_r, t_b, t_k, t_v = (ar(x, DT, TOK) for x in (S_A, S_R, S_B, S_K, S_V))
        t_ar = ar(S_A, 2, DT, TOK)
        w_w1, w_a1, w_g1 = ar(LORA, DT, 64), ar(LORA + 512, DT, 64), ar(LORA + 1024, DT, 160)
        w_w2, w_a2 = ar(LORA + 2304, D, p1=64), ar(LORA + 3328, D, p1=64)
        gs = ar(GS, 2, TOK)
        shift0 = ar(SHIFT0, DT, DEC_B)
        w_g2a, w_g2b = ar(G2, D), ar(G2 + 1024, D, p1=32)
        expand = ar(G2 + 1024, D, p0=32, p1=48)
        bc = ar(BC, TOK, p0=32, p1=48)
        gn_rows = ar(S_K, TOK, p0=32, p1=48)
        shifts = ar(BC + TOK, DT, 9)
        tmp = [ar(LORA + n * TOK, TOK) for n in range(8)]
        EP, EN, EX, KR0, KK_, SQ, KP, RR0 = tmp
        krs, rrs = (KR0, sg[:, 0, :]), (RR0, sg[:, 1, :])

        cb = [ar(CHB + n * 1024, 1024) for n in range(12)]
        V_, B_, K_, ABT, AKT, RBT, RKT, X_, XT, PP, AL, UU = cb
        um = [ar(CHB + 7 * 1024, 2, 2, 512, p1=32), ar(CHB + 9 * 1024, 2, 2, 512, p1=32)]
        s0T = ar(S_B, DT, DEC_B, HD)
        y0 = ar(S_K, DT, 2, 32)

        kslc, kwin = ar(KEYS, 2, TOK), ar(KEYS + 2 * TOK, 2, TOK)
        kvT = ar(KV, 12, TOK)
        cmpT = ar(CMPT, 4, 2, CMPTOK)
        cw1 = ar(CW1, 2, 16, P)
        chid = ar(CHID, 4, 2, 160)
        cpos, cw2, cred = ar(CSM, 2, 16), ar(CSM + 32, 2, HD), ar(CSM + 160, 2, P)
        ctmp = ar(CSM + 416, 16, P)
        kcmp = ar(TAIL, 2, 160)
        vcmp_p, vcmp_d = ar(TAIL + 320, 256, p1=32), ar(TAIL + 576, 256)
        v_slc, v_win, v_new = ar(VTOK, 4, 256), ar(VTOK + 1024, 4, 256), ar(VTOK + 2048, 2, 256, p1=32)
        kwin_c, kslc_c = ar(KWIN_C, DEC_B, 2, PAST), ar(KSLC_C, DEC_B * NPG, 2, PAGE)
        vslc_c, vwin_c = ar(VSLC_C, DEC_B * NPG, 256), ar(VWIN_C, DEC_B * NPG, 256)
        qT = oT = ar(QT, DT, TOK)
        sbuf = [ar(SBUF + n * 1056, 1056) for n in range(4)]
        pair_pt = [ar(PTB + n * 2048, 2048) for n in range(2)]
        ptb = [ar(PTB + n * 2048, 9, P) for n in range(2)]
        att = ar(ATAB, T_PT2)
        wgt = ar(ATT, DT, 48)
        gT = ar(ATT + 384, TOK, p1=48)
        gS = ar(ATAB + T_PT2, 48, p1=32)
        qbd = sg[:].rearrange("p a b -> p (a b)")[:, 0:1024]\
            .rearrange("p (x b r) -> p x b r", x=2, b=DEC_B)

        landed = [sem("slot0_landed"), sem("slot1_landed")]
        multiplied = [sem("slot0_multiplied"), sem("slot1_multiplied")]
        taken = [sem("set0_taken"), sem("set1_taken")]
        w_hi = [sem("slot0_high"), sem("slot1_high")]
        w_split = [sem("slot0_split"), sem("slot1_split")]
        gate_done = [sem("gate0_done"), sem("gate1_done")]
        hid_hi = [sem("hidden0_high"), sem("hidden1_high")]
        hid_done = [sem("hidden0_done"), sem("hidden1_done")]
        acc_step, xr_done, xh_done, xn_split = sem("acc_step"), sem("xr_done"), sem("xh_done"), sem("xn_split")
        oh_done, o_split, keys_kept, eps_set = sem("oh_done"), sem("o_split"), sem("keys_kept"), sem("eps_set")
        x_in = [sem("x0_in"), sem("x1_in")]
        const_in, lora_in = sem("const_in"), sem("lora_in")
        sq_done, sum_done, root_done, xn_done = (
            sem("sq_done"), sem("sum_done"), sem("root_done"), sem("xn_done"))
        xs_done, lora_mm, lora_act, lw_mm, lw_sig, lw_taken, cum_done = (
            sem("xs_done"), sem("lora_mm"), sem("lora_act"), sem("lw_mm"), sem("lw_sig"), sem("lw_taken"),
            sem("cum_done"))
        diff_done, exps_done, rk_copied, kksq_done, kksum_done, kkmax_done, kkroot_done, rk_done, bonus_mm = (
            sem("diff_done"), sem("exps_done"), sem("rk_copied"), sem("kksq_done"), sem("kksum_done"),
            sem("kkmax_done"), sem("kkroot_done"), sem("rk_done"), sem("bonus_mm"))
        temps_free, bonus_done, shifts_done, shift_out = (
            sem("temps_free"), sem("bonus_done"), sem("shifts_done"), sem("shift_out"))
        filled = [sem(f"buf{b}_filled") for b in range(4)]
        emptied = [sem(f"buf{b}_emptied") for b in range(4)]
        half_filled, half_copied = sem("even_heads_filled"), sem("even_heads_copied")
        pe_order = sem("pe_order")
        al_ready, xt_ready, st_ready = sem("al_ready"), sem("xt_ready"), sem("st_ready")
        s0_in, um_u_ready, um_v_ready, wkv_ready, wkv_out = (
            sem("s0_in"), sem("um_u_ready"), sem("um_v_ready"), sem("wkv_ready"), sem("wkv_out"))
        dve_step, act_step, pool_step = sem("dve_step"), sem("act_step"), sem("pool_step")
        gn_sq, gn_inverse = sem("gn_sq"), sem("gn_inverse")
        expand_in, chid_zero = sem("expand_in"), sem("chid_zero")
        rows_in, kv_out, cache_cmp_in, cw_in, cprod, cred_done = (
            sem("rows_in"), sem("kv_out"), sem("cache_cmp_in"), sem("cw_in"), sem("cprod"), sem("cred_done"))
        cmp_mm, cmp_ev, win_out = sem("cmp_mm"), sem("cmp_ev"), sem("win_out")
        table_in, caches_in, vwin_in, att_in = sem("table_in"), sem("caches_in"), sem("vwin_in"), sem("att_in")
        vt_mm, vt_ev = sem("vt_mm"), sem("vt_ev")
        gate_w_in, gate_mm, gate_sig, gate_tr, gates_done, gates_d_out, gates_d_in = (
            sem("gate_w_in"), sem("gate_mm"), sem("gate_sig"), sem("gate_tr"), sem("gates_done"),
            sem("gates_d_out"), sem("gates_d_in"))
        bias_ready, gates_s = sem("bias_ready"), sem("gates_s")
        score_mm, score_taken, negmax, exp_done, p_ready = (
            sem("score_mm"), sem("score_taken"), sem("negmax"), sem("exp_done"), sem("p_ready"))
        turned, turn_taken, o_mm, o_taken = sem("turned"), sem("turn_taken"), sem("o_mm"), sem("o_taken")
        qbd_zero, qbd_done = sem("qbd_zero"), sem("qbd_done")
        y_done, y_out = sem("y_done"), sem("y_out")

        g_p = sb("g_p", [P, 4, 48])
        g_d = sb("g_d", [P, 4, 3])
        block = ctx.enter_context(nc.Block())

        @block.sync
        def _(sp):
            def stream(name, src):
                k0, n, _ = STAGES[name]
                with sp.Fori(0, n) as i:
                    for s in range(2):
                        sp.wait_ge(multiplied[s], i + k0)
                        sp.dma_start(raw[:, s, :], src[bass.ds(2 * i + s, 1)].rearrange("o p c -> p (o c)"))\
                            .then_inc(landed[s], 16)

            def stream_split(name, src, c0=0):
                k0, n, ks = STAGES[name]
                cols = cols_of(name)
                with sp.Fori(0, n) as i:
                    for s in range(2):
                        sp.wait_ge(w_split[s], i + ks)
                        sp.dma_start(raw[:, s, 0:cols],
                                     src[bass.ds(2 * i + s, 1)].rearrange("o p c -> p (o c)")[:, c0:c0 + cols])\
                            .then_inc(landed[s], 16)

            def stream_ffn(f):
                stream_split(f"inA{f}", I["w_in"][f, 0:FTA])
                stream_split(f"outA{f}", I["w_out"][f])
                stream_split(f"inB{f}", I["w_in"][f, FTA:FT])
                stream_split(f"outB{f}", I["w_out"][f], FTA * P)

            def plain_done(name):
                for s in range(2):
                    sp.wait_ge(multiplied[s], end_of(name))

            for half in range(2):
                sp.dma_start(hT[:, 4 * half:4 * half + 4], I["x"][:, 4 * half:4 * half + 4])\
                    .then_inc(x_in[half], 16)
            stream_ffn(0)
            stream("v", I["w_v"])
            stream("rk", I["w_rk"])
            stream("wo", I["w_o"])
            plain_done("wo")
            stream_ffn(1)
            stream("kv", I["w_kv"])
            plain_done("kv")
            stream_ffn(2)
            stream_split("q", I["w_q"])
            stream_split("bo", I["w_bo"])
            stream_ffn(3)
            for ft in range(DT):
                sp.wait_ge(y_done, ft + 1)
                sp.dma_start(O["y"][:, ft], xn[:, ft]).then_inc(y_out, 16)
            sp.wait_ge(y_out, 16 * DT)
            sp.wait_ge(shift_out, 16)
            sp.wait_ge(wkv_out, 32)
            sp.wait_ge(kv_out, 16)
            sp.wait_ge(win_out, 16 * (4 + DEC_B))

        @block.tensor
        def _(pe):
            mm = pe.matmul

            def take(s, k):
                pe.wait_ge(landed[s], (k + 1) * 16)
                pe.wait_ge(taken[s], k)

            def take_split(s, k, ks):
                pe.wait_ge(w_split[s], ks + 1)
                pe.wait_ge(taken[s], k)

            def norm(n):
                pe.wait_ge(acc_step, EV * (n + 1))
                for half in range(2):
                    last = mm(pst[:, half, 0:HALF], ones, acc[:, half * HALF:(half + 1) * HALF],
                              start=True, stop=True)
                last.then_inc(sum_done, 1)

            def times(bank, s, tile, ah, al, start, stop):
                w = slice(tile * P, (tile + 1) * P)
                for wt, a, first, last in ((wh, ah, start, False), (wh, al, False, False), (wl, ah, False, stop)):
                    for half in range(2):
                        ins = mm(pst[:, bank + half, 0:HALF], wt[:, s, w], a[:, half * HALF:(half + 1) * HALF],
                                 start=first, stop=last)
                return ins

            def outputs2(s, ah, al, ready=None):
                for m in range(2):
                    for ft in range(DT):
                        if ready and m == 0:
                            ready(ft)
                        last = times(4 * s + 2 * m, s, m * DT + ft, ah[:, ft, :], al[:, ft, :],
                                     ft == 0, ft == DT - 1)
                last.then_inc(multiplied[s], 1)

            def split_stage(name, ready=None):
                k0, pairs, ks = STAGES[name]
                if ready:
                    for s in range(2):
                        take_split(s, k0, ks)
                        outputs2(s, xh, xl, ready if s == 0 else None)
                a = 1 if ready else 0
                with pe.Fori(a, pairs) as i:
                    for s in range(2):
                        take_split(s, i + k0, i + ks)
                        outputs2(s, xh, xl)

            def out_stage(name, tiles, hidden):
                k0, pairs, ks = STAGES[name]
                with pe.Fori(0, pairs) as i:
                    for s in range(2):
                        take_split(s, i + k0, i + ks)
                        for x in range(2):
                            pe.wait_ge(hid_done[x], hidden + tiles // 2 - 1)
                        for ft in range(tiles):
                            if ft >= tiles - 2:
                                pe.wait_ge(hid_done[ft % 2], hidden + tiles // 2)
                            last = times(4 * s, s, ft, hh[:, ft, :], hl[:, ft, :], ft == 0, ft == tiles - 1)
                        last.then_inc(multiplied[s], 1)

            def xn_ready(n):
                return lambda ft: pe.wait_ge(xn_split, DT * n + ft + 1)

            def ffn(f, n):
                split_stage(f"inA{f}", xn_ready(n))
                out_stage(f"outA{f}", FTA, f * FT // 2)
                split_stage(f"inB{f}")
                out_stage(f"outB{f}", FTB, f * FT // 2 + FTA // 2)

            def project(name, src, ready=None):
                k0, pairs, _ = STAGES[name]
                with pe.Fori(k0, k0 + pairs) as k:
                    for s in range(2):
                        take(s, k)
                        for m in range(2):
                            for ft in range(DT):
                                if ready and s == 0 and m == 0:
                                    ready(ft)
                                w = raw[:, s, (m * DT + ft) * P:(m * DT + ft + 1) * P]
                                for half in range(2):
                                    last = mm(pst[:, 4 * s + 2 * m + half, 0:HALF], w,
                                              src[:, ft, half * HALF:(half + 1) * HALF],
                                              start=(ft == 0), stop=(ft == DT - 1))
                        last.then_inc(multiplied[s], 1)

            fills = [0, 0, 0, 0]

            def fill(b):
                if fills[b]:
                    pe.wait_ge(emptied[b], fills[b])
                fills[b] += 1
                return pst[:, 2 * b:2 * b + 2, :]

            def got(b):
                pe.wait_ge(emptied[b], fills[b])

            pe.wait_ge(const_in, 32)
            norm(0)
            ffn(0, 0)
            norm(1)

            pe.wait_ge(lora_in, 16 * 8)
            for n, (x, w, m0, m) in enumerate(((xs_w, w_w1, 0, 64), (xs_a, w_a1, 0, 64), (xs_g, w_g1, 0, 128),
                                               (xs_g, w_g1, 128, 32))):
                if n:
                    pe.wait_ge(xs_done, DT + min(n, 2))
                for half in range(2):
                    for ft in range(DT):
                        if n == 0 and half == 0:
                            pe.wait_ge(xs_done, max(ft + 1, 6))
                        last = mm(pst[0:m, 2 * n + half, 0:HALF], w[:, ft, m0:m0 + m],
                                  x[:, ft, half * HALF:(half + 1) * HALF],
                                  start=(ft == 0), stop=(ft == DT - 1))
                last.then_inc(lora_mm, 1)
            pe.wait_ge(lora_act, 4)
            for ft in range(DT):
                e = ft % 2
                if ft >= 2:
                    pe.wait_ge(lw_sig, 2 * (ft - 1))
                for half in range(2):
                    mm(pst[:, 4 * e + half, 0:HALF], w_w2[:, ft * P:(ft + 1) * P],
                       sg[0:64, 0, half * HALF:(half + 1) * HALF], start=True, stop=True)
                for half in range(2):
                    last = mm(pst[:, 4 * e + 2 + half, 0:HALF], w_a2[:, ft * P:(ft + 1) * P],
                              sg[0:64, 1, half * HALF:(half + 1) * HALF], start=True, stop=True)
                last.then_inc(lw_mm, 1)
            pe.wait_ge(lw_sig, 2 * DT)
            pe.wait_ge(xs_done, DT + 5)
            project("v", xs_v)
            k0 = STAGES["rk"][0]

            def rk_squares(m):
                pe.wait_ge(kksq_done, m + 1)
                if m:
                    pe.wait_ge(kkmax_done, m)
                for half in range(2):
                    last = mm(pst[:, 4 + half, 0:HALF], blk, SQ[:, half * HALF:(half + 1) * HALF],
                              start=True, stop=True)
                last.then_inc(kksum_done, 1)

            def rk_bonus(m):
                pe.wait_ge(rk_done, m + 1)
                for half in range(2):
                    last = mm(pst[32:48, 6 + half, 0:HALF], hsel[:, m, :], SQ[:, half * HALF:(half + 1) * HALF],
                              start=(m == 0), stop=(m == DT - 1))
                last.then_inc(bonus_mm, 1)

            for m in range(DT):
                s, k = m % 2, k0 + m // 2
                pe.wait_ge(landed[s], (k + 1) * 16)
                pe.wait_ge(taken[1 - s], k + s)
                pe.wait_ge(taken[s], k)
                for w0, src in ((0, xs_r), (1, xs_k)):
                    for ft in range(DT):
                        w = raw[:, s, (w0 * DT + ft) * P:(w0 * DT + ft + 1) * P]
                        for half in range(2):
                            last = mm(pst[:, 2 * w0 + half, 0:HALF], w,
                                      src[:, ft, half * HALF:(half + 1) * HALF],
                                      start=(ft == 0), stop=(ft == DT - 1))
                        if m and w0 == 0 and ft == 2:
                            rk_squares(m - 1)
                last.then_inc(multiplied[s], 1)
                if m:
                    rk_bonus(m - 1)
            rk_squares(DT - 1)
            rk_bonus(DT - 1)
            pe.wait_ge(bonus_done, 1)
            pe.wait_ge(taken[0], k0 + 4)
            pe.wait_ge(taken[1], k0 + 4)
            pe.wait_ge(temps_free, DT)

            def cols(h, q, c):
                o = (h % 2) * 512 + (h // 2) * 64
                return slice(64 * q, 64 * q + c), slice(o, o + c)

            def wide(ap):
                return ap.rearrange("p b c -> p (b c)")

            def turn(src, u, b):
                buf = wide(fill(b))
                n = P if u < 4 else 32
                for ft in range(DT):
                    last = pe.transpose(buf[0:n, ft * P:(ft + 1) * P], src[:, ft, u * P:u * P + n], ident)
                last.then_inc(filled[b], 1)

            def tiles_in_turn(h0, nq):
                return [(h0, 0), (h0 + 1, 1), (h0 + 1, 0), (h0, 1)] if nq == 2 else [(h0, 0), (h0 + 1, 0)]

            def gram(b, lhs, rhs, u, c, nq):
                buf = wide(fill(b))
                for h0 in range(0, NH, 2):
                    for h, q in tiles_in_turn(h0, nq):
                        t0 = u * P + 64 * q
                        f = slice(64 * (h % 2), 64 * (h % 2) + 64)
                        r, co = cols(h, q, c)
                        last = mm(buf[r, co], lhs[f, h // 2, t0:t0 + c], rhs[f, h // 2, t0:t0 + c],
                                  start=True, stop=True)
                last.then_inc(filled[b], 1)

            def product(b, lhs, rhs, c, nq, signal=False, second=lambda: None):
                buf = wide(fill(b))
                for p in range(2):
                    if p:
                        second()
                    for h in range(p, NH, 2):
                        for q in range(nq):
                            r, co = cols(h, q, c)
                            last = mm(buf[r, co], lhs[r, co], rhs[r, co], start=True, stop=True)
                    if signal and p == 0:
                        last.then_inc(half_filled, 1)
                        halves_out[0] += 1
                last.then_inc(filled[b], 1)

            halves_out = [0]

            for u in range(5):
                c, nq, levels = (64, 2, LEVELS_P) if u < 4 else (32, 1, LEVELS_D)
                turn(t_v, u, 0)
                turn(t_b, u, 1)
                turn(t_k, u, 2)
                gram(3, t_b, t_a, u, c, nq)
                gram(0, t_a, t_b, u, c, nq)
                gram(1, t_k, t_a, u, c, nq)
                gram(2, t_b, t_r, u, c, nq)
                gram(3, t_k, t_r, u, c, nq)
                got(0)
                for n, _m in enumerate(levels):
                    lev = u * 5 + n
                    pe.wait_ge(al_ready, lev + 1)
                    product(0, AL, X_, c, nq, signal=True)
                    pe.wait_ge(xt_ready, u + 1)
                    if n:
                        got(2)
                    pe.wait_ge(half_copied, halves_out[0])
                    if n < len(levels) - 1:
                        product(1, XT, PP, c, nq, second=lambda: got(0))
                        product(2, PP, XT, c, nq)
                    else:
                        product(2, PP, XT, c, nq, second=lambda: got(0))
                    if n < len(levels) - 1:
                        got(1)
                got(1)
                got(2)
                got(3)
                if u < 4:
                    for q in range(2):
                        t0 = u * P + 64 * q
                        turns = 2 * u + q
                        buf = wide(fill(3))
                        for h in range(0, NH, 2):
                            for p in range(2):
                                r, co = cols(h + p, q, 64)
                                last = mm(buf[r, co], AKT[r, co], V_[r, (h + p) * 64:(h + p) * 64 + 64],
                                          start=(h == 0), stop=False, skip_group_check=True)
                        last.then_inc(pe_order, 1)
                        pe.wait_ge(pe_order, turns + 1)
                        pe.wait_ge(st_ready, turns + 1)
                        for p in range(2):
                            f = slice(64 * p, 64 * p + 64)
                            for h in range(p, NH, 2):
                                r, co = cols(h, q, 64)
                                last = mm(buf[r, co], t_a[f, h // 2, t0:t0 + 64], st[f, h // 2, :],
                                          start=False, stop=True, skip_group_check=True)
                        last.then_inc(filled[3], 1)
                        ybuf = wide(fill(1))
                        for h in range(0, NH, 2):
                            for p in range(2):
                                f = slice(64 * p, 64 * p + 64)
                                o = p * 512 + (h // 2) * 64
                                mm(ybuf[f, o:o + 64], st[f, h // 2, :], t_r[f, h // 2, t0:t0 + 64],
                                   start=(h == 0), stop=False, skip_group_check=True)
                        got(3)
                        buf = wide(fill(0))
                        for p in range(2):
                            for h in range(p, NH, 2):
                                r, co = cols(h, q, 64)
                                last = mm(buf[r, co], XT[r, co], PP[r, co], start=True, stop=True)
                            if p == 0:
                                last.then_inc(half_filled, 1)
                                halves_out[0] += 1
                        last.then_inc(filled[0], 1)
                        for p in range(2):
                            if p:
                                got(0)
                            else:
                                pe.wait_ge(half_copied, halves_out[0])
                            for h in range(p, NH, 2):
                                r, co = cols(h, q, 64)
                                f = slice(64 * p, 64 * p + 64)
                                o = p * 512 + (h // 2) * 64
                                mm(ybuf[f, o:o + 64], UU[r, co], RBT[r, co],
                                   start=False, stop=False, skip_group_check=True)
                                last = mm(ybuf[f, o:o + 64], V_[r, h * 64:h * 64 + 64], RKT[r, co],
                                          start=False, stop=True, skip_group_check=True)
                        last.then_inc(filled[1], 1)
                        buf = wide(fill(2))
                        for h in range(NH):
                            r, co = cols(h, q, 64)
                            f = slice(64 * (h % 2), 64 * (h % 2) + 64)
                            o = (h // 2) * 64
                            mm(buf[f, o:o + 64], B_[r, h * 64:h * 64 + 64], UU[r, co], start=True, stop=False)
                            last = mm(buf[f, o:o + 64], K_[r, h * 64:h * 64 + 64], V_[r, h * 64:h * 64 + 64],
                                      start=False, stop=True)
                        last.then_inc(filled[2], 1)
                else:
                    pe.wait_ge(s0_in, 16)
                    buf = wide(fill(3))
                    for h in range(NH):
                        r, co = cols(h, 0, 32)
                        o = (h % 2) * 512 + (h // 2) * 64
                        last = mm(buf[r, o:o + 64], AKT[r, co], V_[r, h * 64:h * 64 + 64], start=True, stop=True)
                    last.then_inc(filled[3], 1)
                    buf = fill(1).rearrange("p k (f x t) -> p k f x t", f=DT, x=2)
                    for b in range(DEC_B):
                        t0 = SEQ + DEC_T * b
                        for h in range(NH):
                            f = slice(64 * (h % 2), 64 * (h % 2) + 64)
                            last = mm(buf[f, h % 2, h // 2, :, 4 * b:4 * b + 4], s0T[f, h // 2, b, :],
                                      t_ar[f, :, h // 2, t0:t0 + DEC_T], start=True, stop=True)
                    last.then_inc(filled[1], 1)
                    got(1)
                    buf = wide(fill(0))
                    for ft in range(DT):
                        last = pe.transpose(buf[0:32, ft * P:(ft + 1) * P], y0[:, ft, 0, :], ident)
                    last.then_inc(filled[0], 1)
                    got(0)
                    buf = wide(fill(2))
                    for h in range(NH):
                        r, co = cols(h, 0, 32)
                        o = (h % 2) * 512 + (h // 2) * 64
                        last = mm(buf[r, o:o + 64], XT[r, co], PP[r, o:o + 64], start=True, stop=True)
                    last.then_inc(filled[2], 1)
                    got(2)
                    buf = wide(fill(1))
                    for h in range(NH):
                        r, co = cols(h, 0, 32)
                        o = (h % 2) * 512 + (h // 2) * 64
                        f = slice(64 * (h % 2), 64 * (h % 2) + 64)
                        mm(buf[f, o:o + 32], UU[r, o:o + 64], RBT[r, co], start=True, stop=False)
                        last = mm(buf[f, o:o + 32], V_[r, h * 64:h * 64 + 64], RKT[r, co], start=False, stop=True)
                    last.then_inc(filled[1], 1)
                    got(1)
                    for ft in range(DT):
                        buf = fill(ft % 2)
                        for half in range(2):
                            t = slice(half * HALF, (half + 1) * HALF)
                            last = mm(buf[:, half, 0:HALF], blk, t_r[:, ft, t], start=True, stop=True)
                        last.then_inc(filled[ft % 2], 1)
                        b = 2 + ft % 2
                        pe.wait_ge(um_u_ready, ft + 1)
                        pe.wait_ge(um_v_ready, ft + 1)
                        buf = fill(b)
                        for n, src in enumerate((B_, K_)):
                            for p in range(2):
                                h = 2 * ft + p
                                f = slice(64 * p, 64 * p + 64)
                                last = mm(buf[f, 0, :], src[0:32, h * 64:h * 64 + 64], um[ft % 2][:, p, n, :],
                                          start=(n == 0), stop=(n == 1), skip_group_check=True)
                        last.then_inc(filled[b], 1)
            pe.wait_ge(expand_in, 16)
            buf = fill(0)
            for half in range(2):
                for ft in range(DT):
                    if half == 0:
                        pe.wait_ge(gn_sq, ft + 1)
                    last = mm(buf[32:48, half, 0:HALF], hsel[:, ft, :], t_a[:, ft, half * HALF:(half + 1) * HALF],
                              start=(ft == 0), stop=(ft == DT - 1))
            last.then_inc(filled[0], 1)
            for step in ("bonus", "root", "gate"):
                for ft in range(DT):
                    b = (ft + 1) % 4
                    if step == "root" and ft == 0:
                        pe.wait_ge(gn_inverse, 1)
                    buf = fill(b)
                    for half in range(2):
                        t = slice(half * HALF, (half + 1) * HALF)
                        if step == "gate":
                            mm(buf[:, half, 0:HALF], w_g2a[:, ft * P:(ft + 1) * P], gs[:, 0, t],
                               start=True, stop=False)
                            last = mm(buf[:, half, 0:HALF], w_g2b[:, ft * P:(ft + 1) * P], gs[0:32, 1, t],
                                      start=False, stop=True)
                        else:
                            last = mm(buf[:, half, 0:HALF], expand[:, ft * P:(ft + 1) * P],
                                      (bc if step == "bonus" else gn_rows)[:, t], start=True, stop=True)
                    last.then_inc(filled[b], 1)

            def gated(ft):
                if ft == 0:
                    got(0)
                    got(1)
                pe.wait_ge(emptied[(ft + 1) % 4], fills[(ft + 1) % 4] - 1 + ft // 4)

            project("wo", t_r, gated)

            norm(2)
            ffn(1, 1)
            norm(3)
            pe.wait_ge(xn_done, DT + 1)
            project("kv", xn)

            for b in (0, 1):
                pe.wait_ge(taken[b], STAGES["kv"][0] + 3)
            pe.wait_ge(rows_in, 16 * 4)
            pe.wait_ge(cache_cmp_in, 16 * 2 * DEC_B * NPG)
            pe.wait_ge(cw_in, 16 * 3)
            pe.wait_ge(cred_done, 2)
            for kv in range(2):
                last = mm(pst[:, 4, kv:kv + 1], cred[:, kv, :], ones[:, 0:1], start=True, stop=True)
            last.then_inc(cmp_mm, 1)
            for kv in range(2):
                for s in range(16):
                    for p in range(2):
                        last = mm(pst[:, 2 * kv + p, 0:2 * NBLK], cw1[:, kv, s, :],
                                  cmpT[:, 2 * kv:2 * kv + 2, p, s:s + 16 * (NBLK - 1) + 1:16],
                                  start=(s == 0), stop=(s == 15))
                last.then_inc(cmp_mm, 1)
            pe.wait_ge(cmp_ev, 1 + 4)
            for p in range(2):
                f = slice(64 * p, 64 * p + 64)
                mm(pst[f, 5, 0:320], cw2[:, 0, :], chid[:, p, :, :], start=True, stop=True)
            for kvh in range(NKV):
                mm(pst[0:32, 6, kvh * 64:kvh * 64 + 64], chid[:, 2 + kvh % 2, kvh // 2, 0:32], cw2[:, 1, :],
                   start=True, stop=True)
                last = mm(pst[:, 7, kvh * 64:kvh * 64 + 64], chid[:, 2 + kvh % 2, kvh // 2, 32:160],
                          cw2[:, 1, :], start=True, stop=True)
            last.then_inc(cmp_mm, 1)
            for n, (src, tl) in enumerate([(8, t) for t in range(4)] + [(10, t) for t in range(4)]
                                          + [(8, 4), (10, 4)]):
                b = n % 4
                m = P if tl < 4 else 32
                if n >= 4:
                    pe.wait_ge(vt_ev, n - 3)
                for p in range(2):
                    last = pe.transpose(pst[0:m, b, p * P:(p + 1) * P], kvT[:, src + p, tl * P:tl * P + m],
                                        ident)
                last.then_inc(vt_mm, 1)
            pe.wait_ge(vt_ev, 10)
            pe.wait_ge(cmp_ev, 8)

            ffn(2, 2)
            norm(4)
            split_stage("q", xn_ready(3))
            pe.wait_ge(taken[0], STAGES["q"][0] + 2)
            pe.wait_ge(taken[1], STAGES["q"][0] + 2)
            pe.wait_ge(gate_w_in, 16)
            for half in range(2):
                for ft in range(DT):
                    last = mm(pst[0:48, half, 0:HALF], wgt[:, ft, :], xr[:, ft, half * HALF:(half + 1) * HALF],
                              start=(ft == 0), stop=(ft == DT - 1))
            last.then_inc(gate_mm, 1)
            pe.wait_ge(gate_sig, 1)
            for tl in range(5):
                m = P if tl < 4 else 32
                last = pe.transpose(pst[0:m, 2, tl * 48:tl * 48 + 48], gT[:, tl * P:tl * P + m],
                                    ident[0:48, 0:48])
            last.then_inc(gate_tr, 1)
            pe.wait_ge(gates_done, 1)

            n_turn = [0]

            def scores(e):
                i, p, qt = e // 8, e // 4 % 2, e % 4
                f = slice(64 * p, 64 * p + 64)
                nk = P * (qt + 1)
                q = qT[f, i, qt * P:(qt + 1) * P]
                if e >= 2:
                    pe.wait_ge(score_taken, 3 * (e - 1))
                mm(pst[:, 2 * (e % 2), 0:nk], q, kslc[f, i // 4, 0:nk], start=True, stop=True)
                mm(pst[:, 2 * (e % 2) + 1, 0:nk], q, kwin[f, i // 4, 0:nk], start=True, stop=True)
                if e >= 1:
                    pe.wait_ge(score_taken, 3 * e - 2)
                mm(pst[:, 4, 0:NCMP], q, kcmp[f, i // 4, 0:NCMP], start=True, stop=True).then_inc(score_mm, 1)

            def turn_group(blocks, bank, c0, free, groups=1):
                if free > 0:
                    pe.wait_ge(turn_taken, free)
                for x, (src, m) in enumerate(blocks):
                    last = pe.transpose(pst[0:m, bank, c0 + x * P:c0 + (x + 1) * P], src, ident)
                last.then_inc(turned, groups)

            def turn_probs(e):
                qt = e % 4
                s = sbuf[e % 4]
                pe.wait_ge(p_ready, e + 1)
                turn_group([(s[:, x * P:(x + 1) * P], P) for x in range(qt + 1)], 6, 0, 3 * e)
                window = [(s[:, 512 + x * P:512 + (x + 1) * P], P) for x in range(qt + 1)]
                if qt < 3:
                    turn_group(window + [(s[:, 1024:1024 + NCMP], NCMP)], 7, 0, 3 * e, 2)
                else:
                    turn_group(window, 7, 0, 3 * e)

            def turn_cmp(e):
                if e % 4 == 3:
                    turn_group([(sbuf[e % 4][:, 1024:1024 + NCMP], NCMP)], 6, 0, 3 * e + 1)

            def values(g):
                i, p, j = g // 4, g // 2 % 2, g % 2
                f = slice(64 * p, 64 * p + 64)
                kvh = 2 * (i // 4) + p
                pt = pair_pt[g % 2]
                pe.wait_ge(turn_taken, 6 * g + 6)
                if j == 0 and g >= 4:
                    pe.wait_ge(o_taken, g // 2 - 1)
                out = pst[f, 5, 2 * j * P:(2 * j + 2) * P]
                c = slice(kvh * 64, kvh * 64 + 64)
                for n, v in enumerate((v_slc, v_win)):
                    for x in range(2 * j + 1):
                        mm(out, v[:, x, c], pt[:, 896 * n + 256 * x:896 * n + 256 * x + 256],
                           start=(n == 0 and x == 0), stop=False, skip_group_check=True)
                    mm(out[:, P:2 * P], v[:, 2 * j + 1, c], pt[:, 896 * n + 768:896 * n + 896],
                       start=False, stop=False, skip_group_check=True)
                mm(out, vcmp_p[:, c], pt[0:NCMP, 1792:2048], start=False, stop=True, skip_group_check=True)\
                    .then_inc(o_mm, 1)

            E = 2 * DT * 4
            def sample_scores(u):
                if u == 0:
                    pe.wait_ge(qbd_done, 4)
                    pe.wait_ge(caches_in, 16 * (2 * DEC_B * NPG + 1))
                    pe.wait_ge(score_taken, 3 * (E - 1))
                else:
                    pe.wait_ge(score_taken, 3 * E + 2 * (u - 1))
                bank = 2 * (u % 2)
                for j in range(2):
                    b = 2 * u + j
                    r = slice(64 * j, 64 * j + 64)
                    for out, src in ((pst[r, bank, 0:128], lambda x: kcmp[:, x, 32:160]),
                                     (pst[r, bank, 128:160], lambda x: kslc[:, x, SEQ:TOK]),
                                     (pst[r, bank, 160:192], lambda x: kwin[:, x, SEQ:TOK]),
                                     (pst[r, bank + 1, 0:256].rearrange("p (g t) -> p g t", g=NPG),
                                      lambda x: kslc_c[:, 2 * b:2 * b + 2, x, :]),
                                     (pst[r, bank + 1, 256:512], lambda x: kwin_c[:, b, x, :])):
                        for x in range(2):
                            last = mm(out, qbd[:, x, b, :], src(x), start=(x == 0), stop=(x == 1))
                last.then_inc(score_mm, 1)

            def sample_turns(u):
                pe.wait_ge(p_ready, E + u + 1)
                s = sbuf[u]
                turn_group([(s[:, x * P:(x + 1) * P], P) for x in range(3)]
                           + [(s[:, 416:544], P)], 6, 0, 3 * E if u == 0 else 3 * E + 2 * u - 1)
                turn_group([(s[:, 544:672], P), (s[:, 384:416], 32), (s[:, 672:704], 32)], 7, 0, 3 * E + 2 * u)

            def sample_values(u):
                pe.wait_ge(turn_taken, 3 * E + 2 * u + 2)
                if u == 0:
                    pe.wait_ge(vwin_in, 16)
                    pe.wait_ge(score_taken, 3 * E)
                pt = ptb[u % 2]
                for x in range(2):
                    c = slice(x * P, (x + 1) * P)

                    def both(ap, x=x):
                        return ap.rearrange("p (j x r) -> p x j r", j=2, x=2)[:, x]

                    out = pst[:, 4, P * u:P * (u + 1)]
                    mm(both(out), vcmp_d[:, c], both(pt[:, 0, :]), start=True, stop=False, skip_group_check=True)
                    for j in range(2):
                        b, rows = 2 * u + j, slice(64 * j + 32 * x, 64 * j + 32 * x + 32)
                        for pg in range(NPG):
                            mm(out[:, rows], vslc_c[:, 2 * b + pg, c], pt[:, 1 + pg, rows],
                               start=False, stop=False, skip_group_check=True)
                            mm(out[:, rows], vwin_c[:, 2 * b + pg, c], pt[:, 3 + pg, rows],
                               start=False, stop=False, skip_group_check=True)
                    mm(both(out), v_new[:, 0, c], both(pt[0:32, 5, :]), start=False, stop=False,
                       skip_group_check=True)
                    last = mm(both(out), v_new[:, 1, c], both(pt[0:32, 6, :]), start=False, stop=True,
                              skip_group_check=True)
                last.then_inc(o_mm, 1)

            for e in range(E + 4):
                if 3 <= e <= E + 2:
                    turn_probs(e - 3)
                if e < E:
                    scores(e)
                if e == E:
                    sample_scores(0)
                if 3 <= e <= E + 2:
                    turn_cmp(e - 3)
                if e >= 5 and e % 2:
                    values((e - 5) // 2)
            for u in range(4):
                sample_turns(u)
                if u < 3:
                    sample_scores(u + 1)
                sample_values(u)
            split_stage("bo", lambda ft: pe.wait_ge(o_split, ft + 1))
            norm(5)
            ffn(3, 4)
            norm(6)

        @block.scalar
        def _(act):
            def split(name, i, s):
                k0, _, ks = STAGES[name]
                cols = cols_of(name)
                act.wait_ge(landed[s], (i + k0) * 16 + 16)
                act.wait_ge(multiplied[s], i + k0)
                act.activation(wh[:, s, 0:cols], raw[:, s, 0:cols], ACT.Copy).then_inc(w_hi[s], 1)

            def pipeline(name, finish, following):
                pairs = STAGES[name][1]
                with act.Fori(0, pairs - 1) as i:
                    split(name, i, 1)
                    finish(i, 0)
                    split(name, i + 1, 0)
                    finish(i, 1)
                split(name, pairs - 1, 1)
                finish(pairs - 1, 0)
                if following:
                    split(following, 0, 0)
                finish(pairs - 1, 1)

            def squares(name, n, tiles):
                k0 = STAGES[name][0]

                def finish(i, s):
                    act.wait_ge(taken[s], i + k0 + 1)
                    for m in range(tiles):
                        t = (2 * i + s) * tiles + m
                        x = m if tiles == 2 else s
                        act.wait_ge(acc_step, t + EV * n)
                        act.activation(sg[:, x, :], hT[:, bass.ds(t, 1), :].rearrange("p o c -> p (o c)"),
                                       ACT.Square).then_inc(sq_done, 1)
                return finish

            def norm(n, splits):
                act.wait_ge(sum_done, n + 1)
                act.activation(halves(sg[:, 0, :]), bank2(0), ACT.Sqrt, bias=eps[:, 0:1], scale=1.0 / D)\
                   .then_inc(root_done, 1)
                if splits is not None:
                    high_parts(splits)

            def high_parts(splits):
                for ft in range(DT):
                    act.wait_ge(xr_done, splits * DT + ft + 1)
                    act.activation(xh[:, ft, :], xr[:, ft, :], ACT.Copy).then_inc(xh_done, 1)

            def ffn(f, n, following=None):
                def hidden(name, before):
                    k0 = STAGES[name][0]

                    def finish(i, s):
                        act.wait_ge(multiplied[s], i + k0 + 1)
                        act.wait_ge(hid_done[s], i + before)
                        act.activation(halves(sg[:, s, :]), bank2(4 * s), ACT.Silu).then_inc(gate_done[s], 1)
                        act.wait_ge(taken[s], i + k0 + 1)
                        act.activation(hh[:, bass.ds(2 * i + s, 1), :].rearrange("p o c -> p (o c)"),
                                       sg[:, s, :], ACT.Copy).then_inc(hid_hi[s], 1)
                    return finish

                pipeline(f"inA{f}", hidden(f"inA{f}", f * FT // 2), f"outA{f}")
                pipeline(f"outA{f}", lambda i, s: None, f"inB{f}")
                pipeline(f"inB{f}", hidden(f"inB{f}", f * FT // 2 + FTA // 2), f"outB{f}")
                pipeline(f"outB{f}", squares(f"outB{f}", n, 1), following)

            def plain(name, finish):
                pairs = STAGES[name][1]
                with act.Fori(0, pairs) as i:
                    for s in range(2):
                        finish(i, s)

            seen = [0, 0, 0, 0]

            def empty(b):
                seen[b] += 1
                act.wait_ge(filled[b], seen[b])
                return pst[:, 2 * b:2 * b + 2, :]

            def skip(*bs):
                for b in bs:
                    seen[b] += 1

            act.wait_ge(const_in, 32)
            act.wait_ge(eps_set, 2)
            for ft in range(DT):
                if ft % 4 == 0:
                    act.wait_ge(x_in[ft // 4], 16)
                act.wait_ge(acc_step, ft)
                act.activation(sg[:, ft % 2, :], hT[:, ft, :], ACT.Square).then_inc(sq_done, 1)
            split("inA0", 0, 0)
            norm(0, 0)
            ffn(0, 1)
            norm(1, None)

            for n, (fn, out) in enumerate(((ACT.Tanh, sg[0:64, 0, :]), (ACT.Copy, sg[0:64, 1, :]),
                                           (ACT.Sigmoid, gs[:, 0, :]), (ACT.Sigmoid, gs[0:32, 1, :]))):
                m = out.shape[0]
                act.wait_ge(lora_mm, n + 1)
                if n == 0:
                    act.wait_ge(xn_done, DT)
                act.activation(halves(out), pst[0:m, 2 * n:2 * n + 2, 0:HALF], fn).then_inc(lora_act, 1)
            act.wait_ge(xs_done, DT + 5)
            for ft in range(DT):
                e = ft % 2
                act.wait_ge(lw_mm, ft + 1)
                act.activation(halves(sigw[:, ft, :]), bank2(4 * e), ACT.Sigmoid, bias=par(Q_W0, ft))\
                   .then_inc(lw_sig, 1)
                act.activation(halves(a_t[:, ft, :]), bank2(4 * e + 2), ACT.Sigmoid, bias=par(Q_A0, ft))\
                   .then_inc(lw_sig, 1)
            k0, pairs, _ = STAGES["v"]
            for n in range(2 * pairs):
                s = n % 2
                act.wait_ge(multiplied[s], k0 + n // 2 + 1)
                for m in range(2):
                    ins = act.activation(halves(t_v[:, 2 * n + m, :]), bank2(4 * s + 2 * m), ACT.Copy)
                ins.then_inc(taken[s], 1)
            k0 = STAGES["rk"][0]
            for m in range(DT):
                s = m % 2
                act.wait_ge(multiplied[s], k0 + m // 2 + 1)
                if m >= 2:
                    act.wait_ge(temps_free, m - 1)
                act.activation(halves(krs[s]), bank2(2), ACT.Copy)
                act.activation(halves(rrs[s]), bank2(0), ACT.Copy).then_inc(taken[s], 1)
                if m:
                    act.wait_ge(temps_free, m)
                act.wait_ge(cum_done, m + 1)
                act.activation(EP, cumw[:, m, :], ACT.Exp, scale=-DECAY)
                act.activation(EN, cumw[:, m, :], ACT.Exp, scale=DECAY)
                act.wait_ge(diff_done, m + 1)
                act.activation(EX, KP, ACT.Exp, scale=-DECAY).then_inc(exps_done, 1)
                act.wait_ge(kkmax_done, m + 1)
                act.activation(SQ, SQ, ACT.Sqrt).then_inc(kkroot_done, 1)
            act.wait_ge(bonus_mm, DT)
            act.activation(halves(bc), pst[32:48, 6:8, 0:HALF], ACT.Copy).then_inc(bonus_done, 1)
            act.wait_ge(temps_free, DT)

            def flat(ap):
                return ap.rearrange("p b c -> p (b c)")

            halves_in = [0]

            def copy_halves(dst, rows, c):
                halves_in[0] += 1
                act.wait_ge(half_filled, halves_in[0])
                rows = rows if isinstance(rows, slice) else slice(0, rows)
                for p in range(2):
                    if p:
                        empty(0)
                    out = dst[:, 512 * p:512 * p + 512].rearrange("p (a c) -> p a c", a=NH // 2)[:, :, 0:c]
                    src = pst[rows, p, :].rearrange("p (a c) -> p a c", a=NH // 2)[:, :, 0:c]
                    act.activation(out, src, ACT.Copy).then_inc(emptied[0] if p else half_copied, 1)

            for u in range(5):
                n = P if u < 4 else 32
                levels = LEVELS_P if u < 4 else LEVELS_D
                for b, dst in ((0, V_), (1, B_), (2, K_)):
                    act.activation(dst[0:n], flat(empty(b)[0:n]), ACT.Copy).then_inc(emptied[b], 1)
                skip(3, 0, 1, 2, 3)
                for x in range(len(levels)):
                    copy_halves(PP[0:n], n, 64 if u < 4 else 32)
                    skip(*((1, 2) if x < len(levels) - 1 else (2,)))
                if u < 4:
                    for q in range(2):
                        r = slice(64 * q, 64 * q + 64)
                        act.activation(PP[r], flat(empty(3)[r]), ACT.Copy).then_inc(emptied[3], 1)
                        copy_halves(UU[r], r, 64)
                        t0 = u * P + 64 * q
                        buf = empty(1)
                        for p in range(2):
                            f = slice(64 * p, 64 * p + 64)
                            ins = act.activation(t_r[f, :, t0:t0 + 64],
                                                 buf[f, p, :].rearrange("p (f t) -> p f t", f=DT), ACT.Copy)
                        ins.then_inc(emptied[1], 1)
                        skip(2)
                else:
                    act.activation(PP[0:32], flat(empty(3)[0:32]), ACT.Copy).then_inc(emptied[3], 1)
                    buf = empty(1)
                    for p in range(2):
                        f = slice(64 * p, 64 * p + 64)
                        ins = act.activation(y0[f].rearrange("p f x t -> p (f x t)"), buf[f, p, :], ACT.Copy)
                    ins.then_inc(emptied[1], 1)
                    skip(0)
                    act.activation(UU[0:32], flat(empty(2)[0:32]), ACT.Copy).then_inc(emptied[2], 1)
                    skip(1)
                    for ft in range(DT):
                        skip(2 + ft % 2)
            for ft in range(DT):
                skip(ft % 2)
                act.wait_ge(emptied[ft % 2], seen[ft % 2])
                act.activation(t_a[:, ft, :], t_r[:, ft, :], ACT.Square).then_inc(gn_sq, 1)
            act.activation(halves(gn_rows), empty(0)[32:48, :, 0:HALF], ACT.Sqrt, bias=eps[32:48, 1:2],
                           scale=1.0 / HD).then_inc(emptied[0], 1)

            plain("wo", squares("wo", 2, 2))
            split("inA1", 0, 0)
            norm(2, 1)
            ffn(1, 3)
            norm(3, None)

            k0, pairs, _ = STAGES["kv"]
            for n in range(2 * pairs):
                s = n % 2
                act.wait_ge(multiplied[s], k0 + n // 2 + 1)
                for m in range(2):
                    ins = act.activation(halves(kvT[:, 2 * n + m, :]), bank2(4 * s + 2 * m), ACT.Copy)
                ins.then_inc(taken[s], 1)
            act.wait_ge(cmp_mm, 1)
            act.activation(cbias[:, 0:2], pst[:, 4, 0:2], ACT.Copy).then_inc(cmp_ev, 1)
            act.wait_ge(cmp_ev, 1)
            act.wait_ge(chid_zero, 1)
            for kv in range(2):
                act.wait_ge(cmp_mm, 2 + kv)
                for p in range(2):
                    act.activation(chid[:, 2 * kv + p, :, 0:NBLK],
                                   pst[:, 2 * kv + p, 0:2 * NBLK].rearrange("p (x n) -> p x n", x=2),
                                   ACT.Gelu_apprx_tanh, bias=cbias[:, kv:kv + 1]).then_inc(cmp_ev, 1)
            act.wait_ge(cmp_mm, 4)
            act.activation(kcmp, pst[:, 5, 0:320].rearrange("p (x n) -> p x n", x=2), ACT.Copy).then_inc(cmp_ev, 1)
            act.activation(vcmp_p, pst[0:32, 6, 0:256], ACT.Copy).then_inc(cmp_ev, 1)
            act.activation(vcmp_d, pst[:, 7, 0:256], ACT.Copy).then_inc(cmp_ev, 1)
            act.wait_ge(cmp_mm, 4)
            for n in range(10):
                act.wait_ge(vt_mm, n + 1)
                b = n % 4
                if n < 8:
                    dst, m = (v_slc, v_win)[n // 4][:, n % 4, :], P
                else:
                    dst, m = v_new[:, n - 8, :], 32
                act.activation(dst, pst[0:m, b, 0:256], ACT.Copy).then_inc(vt_ev, 1)

            act.wait_ge(kv_out, 16)
            act.wait_ge(keys_kept, 1)
            split("inA2", 0, 0)
            high_parts(2)
            ffn(2, 4, "q")
            norm(4, 3)
            k0, pairs, _ = STAGES["q"]
            for n in range(2 * pairs):
                s = n % 2
                if n + 1 < 2 * pairs:
                    split("q", (n + 1) // 2, (n + 1) % 2)
                act.wait_ge(multiplied[s], k0 + n // 2 + 1)
                for m in range(2):
                    ins = act.activation(halves(qT[:, 2 * n + m, :]), bank2(4 * s + 2 * m), ACT.Copy,
                                         scale=HD ** -0.5)
                ins.then_inc(taken[s], 1)
            act.wait_ge(gate_mm, 1)
            act.activation(halves(gT), pst[0:48, 0:2, 0:HALF], ACT.Sigmoid).then_inc(gate_sig, 1)

            E = 2 * DT * 4
            turns = [0]

            def copy_turned(dst, m, n, b, c0=0):
                act.wait_ge(turned, turns[0] + 1)
                turns[0] += 1
                act.activation(dst, pst[0:m, b, c0:c0 + n * P].rearrange("p (x c) -> p x c", x=n), ACT.Copy)\
                   .then_inc(turn_taken, 1)

            def exps(e):
                qt, s, x = e % 4, sbuf[e % 4], e % 2
                nk = P * (qt + 1)
                act.wait_ge(negmax, e + 1)
                for n, c in enumerate((slice(1024, 1024 + NCMP), slice(0, nk), slice(512, 512 + nk))):
                    ins = act.activation(s[:, c], s[:, c], ACT.Exp, bias=sm[:, x, 4 + n:5 + n],
                                         accum_out=sm[:, x, 8 + n:9 + n])
                ins.then_inc(exp_done, 1)

            def copies(e):
                qt, g, q = e % 4, e // 2, e % 2
                pt = pair_pt[g % 2]
                if g >= 2 and q == 0:
                    act.wait_ge(o_mm, g - 1)
                both = qt + 1 - q
                for n, b in ((0, 6), (1, 7)):
                    act.wait_ge(turned, 3 * e + n + 1)
                    dst = pt[:, 896 * n:896 * n + 256 * both].rearrange("p (x q c) -> p x q c", q=2, c=P)[:, :, q]
                    ins = act.activation(dst, pst[:, b, 0:both * P].rearrange("p (x c) -> p x c", x=both), ACT.Copy)
                    if q:
                        ins = act.activation(pt[:, 896 * n + 768:896 * n + 896], pst[:, b, both * P:(both + 1) * P],
                                             ACT.Copy)
                    ins.then_inc(turn_taken, 1)
                turns[0] += 3
                if qt < 3:
                    copy_cmp(e, 7, (qt + 1) * P)

            def copy_cmp(e, b, c0):
                act.wait_ge(turned, 3 * e + 3)
                c = 1792 + e % 2 * P
                act.activation(pair_pt[e // 2 % 2][0:NCMP, c:c + P], pst[0:NCMP, b, c0:c0 + P], ACT.Copy)\
                   .then_inc(turn_taken, 1)

            for e in range(1, E + 3):
                if e >= 3:
                    copies(e - 3)
                if e <= E:
                    exps(e - 1)
                if e >= 3 and (e - 3) % 4 == 3:
                    copy_cmp(e - 3, 6, 0)
            for u in range(4):
                e = E + u
                s, x = sbuf[u], u % 2
                act.wait_ge(negmax, e + 1)
                for n, c in enumerate((slice(0, 128), slice(128, 416), slice(416, 704))):
                    ins = act.activation(s[:, c], s[:, c], ACT.Exp, bias=sm[:, x, 4 + n:5 + n],
                                         accum_out=sm[:, x, 8 + n:9 + n])
                ins.then_inc(exp_done, 1)
                pt = ptb[u % 2]
                act.wait_ge(o_mm, E // 2 + u - 1)
                copy_turned(pt[:, 0:4, :], P, 4, 6)
                act.wait_ge(turned, turns[0] + 1)
                turns[0] += 1
                act.activation(pt[:, 4, :], pst[:, 7, 0:P], ACT.Copy)
                act.activation(pt[0:32, 5:7, :], pst[0:32, 7, P:3 * P].rearrange("p (x c) -> p x c", x=2),
                               ACT.Copy).then_inc(turn_taken, 1)
            act.wait_ge(o_mm, E // 2 + 4)
            split("bo", 0, 0)
            act.wait_ge(o_taken, 20)
            for ft in range(DT):
                act.activation(xh[:, ft, :], oT[:, ft, :], ACT.Copy).then_inc(oh_done, 1)
            pipeline("bo", squares("bo", 5, 2), "inA3")
            norm(5, 4)
            ffn(3, 6)
            norm(6, None)

        @block.vector
        def _(dve):
            own = Steps(dve, dve_step)
            do = own.do

            def split(name, i, s):
                ks = STAGES[name][2]
                cols = cols_of(name)
                dve.wait_ge(w_hi[s], i + ks + 1)
                dve.tensor_tensor(wl[:, s, 0:cols], raw[:, s, 0:cols], wh[:, s, 0:cols].bitcast(F32), ALU.subtract)\
                   .then_inc(w_split[s], 1)

            def pipeline(name, finish, following):
                pairs = STAGES[name][1]
                with dve.Fori(0, pairs - 1) as i:
                    split(name, i, 1)
                    finish(i, 0)
                    split(name, i + 1, 0)
                    finish(i, 1)
                split(name, pairs - 1, 1)
                finish(pairs - 1, 0)
                if following:
                    split(following, 0, 0)
                finish(pairs - 1, 1)

            def clear(n):
                if n:
                    dve.wait_ge(sum_done, n)
                dve.memset(acc[:], 0.0).then_inc(acc_step, 1)

            def sum_square(n, t, x):
                dve.wait_ge(sq_done, t + (DT * n + 1))
                dve.wait_ge(acc_step, t + (EV * n + 1))
                dve.tensor_tensor(acc[:], acc[:], sg[:, x, :], ALU.add).then_inc(acc_step, 1)

            def inverse_root(n):
                dve.wait_ge(root_done, n + 1)
                do(dve.reciprocal(sg[:, 1, :], sg[:, 0, :]))
                own.wait()

            def norm(n, q, splits=None, last=False, again=False):
                if not again:
                    inverse_root(n)

                def low(ft):
                    dve.wait_ge(xh_done, splits * DT + ft + 1)
                    dve.tensor_tensor(xl[:, ft, :], xr[:, ft, :], xh[:, ft, :].bitcast(F32), ALU.subtract)\
                       .then_inc(xn_split, 1)

                dst = xn if splits is None else xr
                for ft in range(DT):
                    ins = dve.scalar_tensor_tensor(out=dst[:, ft, :], in0=hT[:, ft, :], scalar=par(q, ft),
                                                   in1=sg[:, 1, :], op0=ALU.mult, op1=ALU.mult)
                    if last:
                        ins.then_inc(y_done, 1)
                    elif splits is not None:
                        ins.then_inc(xr_done, 1)
                        if ft:
                            low(ft - 1)
                if splits is not None:
                    low(DT - 1)
                elif not last:
                    ins.then_inc(xn_done, 1)

            def ffn(f, n, following=None):
                def hidden(name, before):
                    def finish(i, s):
                        dve.wait_ge(gate_done[s], i + (before + 1))
                        dve.tensor_tensor(halves(sg[:, s, :]), halves(sg[:, s, :]), bank2(4 * s + 2), ALU.mult)\
                           .then_inc(taken[s], 1)
                        dve.wait_ge(hid_hi[s], i + (before + 1))
                        t = bass.ds(2 * i + s, 1)
                        dve.tensor_tensor(hl[:, t, :].rearrange("p o c -> p (o c)"), sg[:, s, :],
                                          hh[:, t, :].rearrange("p o c -> p (o c)").bitcast(F32), ALU.subtract)\
                           .then_inc(hid_done[s], 1)
                    return finish

                pipeline(f"inA{f}", hidden(f"inA{f}", f * FT // 2), f"outA{f}")
                pipeline(f"outA{f}", add(f"outA{f}", 1, 0.5), f"inB{f}")
                pipeline(f"inB{f}", hidden(f"inB{f}", f * FT // 2 + FTA // 2), f"outB{f}")
                clear(n)
                pipeline(f"outB{f}", add(f"outB{f}", 1, 0.5, n), following)

            def add(name, tiles, factor, n=None):
                k0 = STAGES[name][0]

                def finish(i, s):
                    dve.wait_ge(multiplied[s], i + (k0 + 1))
                    for m in range(tiles):
                        dst = hT[:, bass.ds((2 * i + s) * tiles + m, 1), :]\
                            .rearrange("p o (h c) -> p (o h) c", h=2)
                        ins = dve.scalar_tensor_tensor(out=dst, in0=bank2(4 * s + 2 * m), scalar=factor,
                                                       in1=dst, op0=ALU.mult, op1=ALU.add)
                    ins.then_inc(taken[s], 1)
                    if n is not None:
                        for m in range(tiles):
                            sum_square(n, (2 * i + s) * tiles + m, m if tiles == 2 else s)
                return finish

            seen = [0, 0, 0, 0]

            def empty(b):
                seen[b] += 1
                dve.wait_ge(filled[b], seen[b])
                return pst[:, 2 * b:2 * b + 2, :]

            def skip(*bs):
                for b in bs:
                    seen[b] += 1

            dve.wait_ge(const_in, 32)
            dve.memset(eps[:, 0:1], RMS_EPS).then_inc(eps_set, 1)
            dve.memset(eps[:, 1:2], GN_EPS).then_inc(eps_set, 1)
            clear(0)
            do(dve.tensor_scalar(const[:, C_PAR + 21 * 8:C_PAR + 22 * 8],
                                 const[:, C_PAR + Q_KA * 8:C_PAR + Q_KA * 8 + 8], -1.0, 1.0, ALU.mult, ALU.add))
            for ft in range(DT):
                sum_square(0, ft, ft % 2)
            split("inA0", 0, 0)
            norm(0, Q_G00, 0)
            ffn(0, 1)
            inverse_root(1)
            dve.wait_ge(lora_in, 16 * 8)
            for ft in range(DT):
                x, d = xn[:, ft, :], xx[:, ft, :]
                xs, ds = (v[:, SEQ:].rearrange("p (b t) -> p b t", t=DEC_T) for v in (x, d))
                dve.scalar_tensor_tensor(out=x, in0=hT[:, ft, :], scalar=par(Q_G01, ft), in1=sg[:, 1, :],
                                         op0=ALU.mult, op1=ALU.mult).then_inc(xn_done, 1)
                dve.wait_ge(xn_done, ft + 1)
                do(dve.tensor_tensor(d[:, 1:SEQ], x[:, 0:SEQ - 1], x[:, 1:SEQ], ALU.subtract))
                do(dve.tensor_scalar(d[:, 0:1], x[:, 0:1], -1.0, None, ALU.mult))
                do(dve.tensor_tensor(ds[:, :, 1:DEC_T], xs[:, :, 0:DEC_T - 1], xs[:, :, 1:DEC_T], ALU.subtract))
                do(dve.tensor_tensor(ds[:, :, 0], shift0[:, ft, :], xs[:, :, 0], ALU.subtract))
                own.wait()
                dve.scalar_tensor_tensor(out=xs_w[:, ft, :], in0=d, scalar=par(Q_MU + 3, ft), in1=x,
                                         op0=ALU.mult, op1=ALU.add).then_inc(xs_done, 1)
            dv = xn[:, :, SEQ:].rearrange("p f (b t) -> p f b t", t=DEC_T)
            do(dve.tensor_copy(shifts[:, :, 0:1], xn[:, :, SEQ - 1:SEQ]))
            dve.tensor_copy(shifts[:, :, 1:9], dv[:, :, :, DEC_T - 1]).then_inc(shifts_done, 1)
            for c, dst in ((4, xs_a), (5, xs_g), (0, xs_r), (1, xs_k), (2, xs_v)):
                for ft in range(DT):
                    ins = dve.scalar_tensor_tensor(out=dst[:, ft, :], in0=xx[:, ft, :], scalar=par(Q_MU + c, ft),
                                                   in1=xn[:, ft, :], op0=ALU.mult, op1=ALU.add)
                ins.then_inc(xs_done, 1)
            for ft in range(DT):
                dve.wait_ge(lw_sig, 2 * ft + 1)
                if ft == 0:
                    dve.wait_ge(xs_done, DT + 5)
                dve.tensor_tensor_scan(cumw[:, ft, :], reset, sigw[:, ft, :], 0.0, ALU.mult, ALU.add)\
                   .then_inc(cum_done, 1)
            dve.wait_ge(lora_act, 4)
            for m in range(DT):
                KR, RR = krs[m % 2], rrs[m % 2]
                if m:
                    dve.wait_ge(bonus_mm, m)
                dve.wait_ge(cum_done, m + 1)
                dve.wait_ge(lw_sig, 2 * m + 2)
                if m:
                    dve.wait_ge(temps_free, m)
                if m == 0:
                    dve.wait_ge(lw_sig, 2 * DT)
                dve.tensor_tensor(KP, cumw[:, m, :], sigw[:, m, :], ALU.subtract).then_inc(diff_done, 1)
                dve.wait_ge(taken[m % 2], STAGES["rk"][0] + m // 2 + 1)
                do(dve.tensor_scalar(KK_, KR, par(Q_KK, m), None, ALU.mult))
                own.wait()
                dve.tensor_tensor(SQ, KK_, KK_, ALU.mult).then_inc(kksq_done, 1)
                dve.wait_ge(kksum_done, m + 1)
                dve.tensor_scalar(halves(SQ), bank2(4), 1e-24, None, ALU.max).then_inc(kkmax_done, 1)
                dve.wait_ge(exps_done, m + 1)
                do(dve.tensor_scalar(KP, a_t[:, m, :], par(Q_KA, m), par(21, m), ALU.mult, ALU.add))
                do(dve.tensor_tensor(t_r[:, m, :], RR, EP, ALU.mult))
                own.wait()
                do(dve.tensor_tensor(KP, KP, KR, ALU.mult))
                do(dve.tensor_copy(wc[:, m, 0:8], EP[:, CH - 1:SEQ:CH]))
                do(dve.tensor_copy(wc[:, m, 8:16], EP[:, SEQ + DEC_T - 1:TOK:DEC_T]))
                dve.wait_ge(kkroot_done, m + 1)
                do(dve.reciprocal(SQ, SQ))
                own.wait()
                do(dve.tensor_tensor(KK_, KK_, SQ, ALU.mult))
                own.wait()
                do(dve.scalar_tensor_tensor(out=t_a[:, m, :], in0=KK_, scalar=-1.0, in1=EX,
                                            op0=ALU.mult, op1=ALU.mult))
                do(dve.tensor_tensor(KR, KK_, a_t[:, m, :], ALU.mult))
                dve.scalar_tensor_tensor(out=SQ, in0=RR, scalar=par(Q_RK, m), in1=KP,
                                         op0=ALU.mult, op1=ALU.mult).then_inc(rk_done, 1)
                own.wait()
                do(dve.tensor_tensor(t_b[:, m, :], KR, EN, ALU.mult))
                dve.tensor_tensor(t_k[:, m, :], KP, EN, ALU.mult).then_inc(temps_free, 1)
            dve.wait_ge(bonus_mm, DT)
            dve.wait_ge(temps_free, DT)

            def flat(ap):
                return ap.rearrange("p b c -> p (b c)")

            def by_head(ap, c):
                return ap.rearrange("p (a c) -> p a c", a=NH)[:, :, 0:c]

            st_ready_n = [1]
            dve.memset(st[:], 0.0).then_inc(st_ready, 1)
            for u in range(5):
                c, n, levels = (64, P, LEVELS_P) if u < 4 else (32, 32, LEVELS_D)

                def mask(x, n=n, c=c, u=u):
                    o = (C_MP if u < 4 else C_MD) + x * c
                    return const[0:n, o:o + c].unsqueeze(1).to_broadcast([n, NH, c])

                eye = const[0:n, C_I:C_I + c].unsqueeze(1).to_broadcast([n, NH, c])
                skip(0, 1, 2)

                def masked(dst, b, x, n=n, c=c):
                    return dve.tensor_tensor(by_head(dst[0:n], c), by_head(flat(empty(b)[0:n]), c), mask(x), ALU.mult)

                masked(ABT, 3, M_STRICT).then_inc(emptied[3], 1)
                do(masked(X_, 0, M_LOW))
                dve.wait_ge(emptied[3], seen[3])
                do(dve.tensor_tensor(by_head(XT[0:n], c), by_head(ABT[0:n], c), mask(M_UP), ALU.mult))
                own.wait()
                dve.tensor_tensor(by_head(X_[0:n], c), by_head(X_[0:n], c), eye, ALU.add).then_inc(emptied[0], 1)
                dve.tensor_tensor(by_head(XT[0:n], c), by_head(XT[0:n], c), eye, ALU.add).then_inc(xt_ready, 1)
                masked(AKT, 1, M_STRICT).then_inc(emptied[1], 1)
                masked(RBT, 2, M_INCL).then_inc(emptied[2], 1)
                masked(RKT, 3, M_INCL).then_inc(emptied[3], 1)
                dve.wait_ge(emptied[0], seen[0])
                dve.wait_ge(xt_ready, u + 1)
                for x in range(len(levels)):
                    skip(0)
                    if x < len(levels) - 1:
                        buf = by_head(flat(empty(1)[0:n]), c)
                        dve.tensor_tensor(by_head(X_[0:n], c), by_head(X_[0:n], c), buf, ALU.add)\
                           .then_inc(emptied[1], 1)
                    buf = by_head(flat(empty(2)[0:n]), c)
                    dve.tensor_tensor(by_head(XT[0:n], c), by_head(XT[0:n], c), buf, ALU.add)\
                       .then_inc(emptied[2], 1)
                    if x < len(levels) - 1:
                        dve.wait_ge(emptied[1], seen[1])
                        dve.wait_ge(emptied[2], seen[2])
                if u < 4:
                    for q in range(2):
                        skip(3, 1, 0)
                        buf = flat(empty(2))[:, 0:512].rearrange("p (f i) -> p f i", f=DT)
                        dve.wait_ge(st_ready, st_ready_n[0])
                        dve.tensor_tensor(st[:], st[:], buf, ALU.add).then_inc(emptied[2], 1)
                        dve.wait_ge(emptied[2], seen[2])
                        w = wc[:, :, 2 * u + q:2 * u + q + 1].to_broadcast([P, DT, HD])
                        dve.tensor_tensor(st[:], st[:], w, ALU.mult).then_inc(st_ready, 1)
                        st_ready_n[0] += 1
                else:
                    skip(3)
                    dve.wait_ge(emptied[3], seen[3])
                    skip(1)
                    buf = flat(empty(0)[0:32]).rearrange("p (f k i) -> p k f i", f=DT, k=2)
                    pp = PP[0:32].rearrange("p (k f i) -> p k f i", k=2, f=DT)
                    for k in range(2):
                        ins = dve.tensor_tensor(pp[:, k], pp[:, k], buf[:, k], ALU.add)
                    ins.then_inc(emptied[0], 1)
                    skip(2)

                    def build_v(ft):
                        if ft >= DT:
                            return
                        if ft >= 2:
                            dve.wait_ge(filled[2 + ft % 2], FILLS23[ft % 2] + ft // 2)
                        seq = const[0:32, C_SEQ:C_SEQ + DEC_B].unsqueeze(2).to_broadcast([32, DEC_B, HD])
                        for p in range(2):
                            h = 2 * ft + p
                            ins = dve.tensor_tensor(
                                um[ft % 2][:, p, 1, :].rearrange("p (b i) -> p b i", b=DEC_B),
                                V_[0:32, h * 64:h * 64 + 64].unsqueeze(1).to_broadcast([32, DEC_B, HD]), seq,
                                ALU.mult)
                        ins.then_inc(um_v_ready, 1)

                    dve.wait_ge(emptied[2], FILLS23[0])
                    build_v(0)
                    dve.wait_ge(emptied[1], seen[1])
                    buf = empty(1)
                    for p in range(2):
                        f = slice(64 * p, 64 * p + 64)
                        src = buf[f, p, :].rearrange("p (f t) -> p f t", f=DT)[:, :, 0:32]
                        ins = dve.tensor_tensor(t_r[f, :, SEQ:TOK], src, y0[f, :, 1, :], ALU.add)
                    ins.then_inc(emptied[1], 1)
                    for ft in range(DT):
                        buf = empty(ft % 2)[:, :, 0:HALF]
                        if ft == 0:
                            dve.wait_ge(emptied[1], seen[1] - 1)
                        dve.scalar_tensor_tensor(out=halves(t_r[:, ft, :]), in0=buf, scalar=-1.0 / HD,
                                                 in1=halves(t_r[:, ft, :]), op0=ALU.mult, op1=ALU.add)\
                           .then_inc(emptied[ft % 2], 1)
                        build_v(ft + 1)
                        b = 2 + ft % 2
                        buf = empty(b)[:, 0, :].rearrange("p (b i) -> p b i", b=DEC_B)
                        dve.tensor_tensor(s0T[:, ft], s0T[:, ft], buf, ALU.add).then_inc(emptied[b], 1)
                        dve.wait_ge(emptied[b], seen[b])
                        w = wc[:, ft, 8:16].unsqueeze(2).to_broadcast([P, DEC_B, HD])
                        dve.tensor_tensor(s0T[:, ft], s0T[:, ft], w, ALU.mult).then_inc(wkv_ready, 1)
            skip(0)
            dve.wait_ge(filled[0], seen[0])
            for ft in range(DT):
                b = (ft + 1) % 4
                if ft == 4:
                    dve.wait_ge(emptied[0], seen[0])
                    dve.reciprocal(gn_rows, gn_rows).then_inc(gn_inverse, 1)
                dve.tensor_tensor(halves(t_a[:, ft, :]), halves(t_v[:, ft, :]), empty(b)[:, :, 0:HALF], ALU.mult)\
                   .then_inc(emptied[b], 1)
            for ft in range(DT):
                b = (ft + 1) % 4
                dve.wait_ge(emptied[b], seen[b])
                do(dve.scalar_tensor_tensor(out=halves(t_r[:, ft, :]), in0=halves(t_r[:, ft, :]),
                                            scalar=par(Q_LNW, ft), in1=empty(b)[:, :, 0:HALF],
                                            op0=ALU.mult, op1=ALU.mult))
                own.wait()
                dve.scalar_tensor_tensor(out=t_r[:, ft, :], in0=t_r[:, ft, :], scalar=par(Q_LNB, ft),
                                         in1=t_a[:, ft, :], op0=ALU.add, op1=ALU.add)\
                   .then_inc(emptied[b], 1)
            root_seen = list(seen)
            for ft in range(DT):
                b = (ft + 1) % 4
                buf = empty(b)[:, :, 0:HALF]
                dve.wait_ge(emptied[b], root_seen[b] - 1 + ft // 4)
                dve.tensor_tensor(halves(t_r[:, ft, :]), halves(t_r[:, ft, :]), buf, ALU.mult)\
                   .then_inc(emptied[b], 1)
            clear(2)
            finish = add("wo", 2, 1.0, 2)
            with dve.Fori(0, STAGES["wo"][1]) as i:
                for s in range(2):
                    finish(i, s)
            split("inA1", 0, 0)
            dve.wait_ge(wkv_out, 32)
            norm(2, Q_G02, 1)
            ffn(1, 3)
            norm(3, Q_KVN)

            for kv in range(2):
                dve.wait_ge(cprod, kv + 1)
                dve.tensor_reduce(cred[:, kv, :], ctmp.rearrange("p s c -> p c s"), AX, ALU.add)\
                   .then_inc(cred_done, 1)
            dve.wait_ge(vt_ev, 10)
            dve.wait_ge(kv_out, 16)
            dve.tensor_copy(ar(KEYS, 4, TOK), kvT[:, 0:4, :]).then_inc(keys_kept, 1)
            dve.wait_ge(keys_kept, 1)
            split("inA2", 0, 0)
            norm(3, Q_G10, 2, again=True)
            ffn(2, 4, "q")
            norm(4, Q_G11, 3)
            pairs = STAGES["q"][1]
            for n in range(1, 2 * pairs):
                split("q", n // 2, n % 2)

            dve.wait_ge(gate_tr, 1)
            dve.tensor_copy(gS, pst[0:32, 2, 192:240]).then_inc(gates_s, 1)
            do(dve.tensor_copy(g_p[:], pst[:, 2, 0:192].rearrange("p (t c) -> p t c", t=4)))
            own.wait()
            g0 = g_p[:, 0, :].rearrange("p (h c) -> p h c", c=3)[:, :, 0]
            dve.wait_ge(att_in, 16)
            dve.tensor_scalar(g0, g0, cbias[:, 2:3], None, ALU.mult).then_inc(gates_done, 1)
            dve.wait_ge(gates_done, 1)
            dve.wait_ge(taken[0], STAGES["q"][0] + 2)
            dve.wait_ge(taken[1], STAGES["q"][0] + 2)
            dve.wait_ge(qbd_zero, 1)
            for x in range(2):
                for p in range(2):
                    f = slice(64 * p, 64 * p + 64)
                    src = qT[f, 4 * x:4 * x + 4, SEQ:TOK].rearrange("p g (b t) -> p g b t", t=DEC_T)
                    dst = qbd[f, x].rearrange("p b (x k g t) -> p x k g b t", x=2, k=2, g=4)[:, x, p]
                    for g in range(4):
                        ins = dve.tensor_copy(dst[:, g], src[:, g])
                    ins.then_inc(qbd_done, 1)

            E = 2 * DT * 4

            def bias_max(e):
                hh, qt, s, x = e // 4, e % 4, sbuf[e % 4], e % 2
                nk = P * (qt + 1)
                if qt == 0:
                    dve.wait_ge(bias_ready, hh + 1)
                dh = ar(ATAB + T_DH + 640 * (hh % 2), 640)
                dve.wait_ge(score_mm, e + 1)
                if e >= 4:
                    dve.wait_ge(turned, 3 * (e - 3))
                for n, (c, bank, c0, w, t) in enumerate((
                        (1024, 4, 0, NCMP, 512 + qt * NCMP), (0, 2 * (e % 2), 0, nk, (3 - qt) * P),
                        (512, 2 * (e % 2) + 1, 0, nk, (3 - qt) * P))):
                    dve.tensor_tensor_reduce(s[:, c:c + w], pst[:, bank, c0:c0 + w], dh[:, t:t + w], 1.0, -3e38,
                                             ALU.add, ALU.max, sm[:, x, n:n + 1]).then_inc(score_taken, 1)
                dve.wait_ge(score_taken, 3 * e + 3)
                dve.tensor_scalar(sm[:, x, 4:7], sm[:, x, 0:3], -1.0, None, ALU.mult).then_inc(negmax, 1)

            def scale(e):
                hh, qt, s, x = e // 4, e % 4, sbuf[e % 4], e % 2
                nk = P * (qt + 1)
                h = head_of(hh // 2, hh % 2)
                dve.wait_ge(exp_done, e + 1)
                do(dve.reciprocal(sm[:, x, 12:15], sm[:, x, 8:11]))
                own.wait()
                do(dve.tensor_tensor(sm[:, x, 8:11], sm[:, x, 12:15],
                                     g_p[:, qt, 3 * h:3 * h + 3], ALU.mult))
                own.wait()
                for n, c in ((1, slice(0, nk)), (2, slice(512, 512 + nk)), (0, slice(1024, 1024 + NCMP))):
                    ins = dve.tensor_scalar(s[:, c], s[:, c], sm[:, x, 8 + n:9 + n], None, ALU.mult)
                ins.then_inc(p_ready, 1)

            def take_out(hh):
                i, p = hh // 2, hh % 2
                f = slice(64 * p, 64 * p + 64)
                dve.wait_ge(o_mm, 2 * hh + 2)
                dve.tensor_copy(oT[f, i, 0:SEQ], pst[f, 5, :]).then_inc(o_taken, 1)

            for e in range(E + 1):
                if e < E:
                    bias_max(e)
                if e >= 1:
                    scale(e - 1)
                if e >= 9 and e % 4 == 1 and e < E:
                    take_out(e // 4 - 2)

            dve.wait_ge(gates_d_in, 16 * DEC_B)
            for u in range(4):
                e = E + u
                s, x, bank = sbuf[u], u % 2, 2 * (u % 2)
                dve.wait_ge(score_mm, e + 1)
                dve.wait_ge(turned, 3 * (e - 3))
                dve.wait_ge(p_ready, e)
                dd = att[:, T_DD + 192 * u:T_DD + 192 * u + 192]
                dc = att[:, T_DD + 768:T_DD + 1024]
                do(dve.tensor_tensor(s[:, 0:128], pst[:, bank, 0:128], dd[:, 0:128], ALU.add))
                do(dve.tensor_tensor(s[:, 384:416], pst[:, bank, 128:160], dd[:, 128:160], ALU.add))
                dve.tensor_tensor(s[:, 672:704], pst[:, bank, 160:192], dd[:, 160:192], ALU.add)\
                   .then_inc(score_taken, 1)
                do(dve.tensor_tensor(s[:, 128:384], pst[:, bank + 1, 0:256], dc, ALU.add))
                dve.tensor_tensor(s[:, 416:672], pst[:, bank + 1, 256:512], dc, ALU.add).then_inc(score_taken, 1)
                own.wait()
                dve.wait_ge(score_taken, 3 * E + 2 * u + 2)
                for n, c in enumerate((slice(0, 128), slice(128, 416), slice(416, 704))):
                    do(dve.tensor_reduce(sm[:, x, n:n + 1], s[:, c], AX, ALU.max))
                own.wait()
                dve.tensor_scalar(sm[:, x, 4:7], sm[:, x, 0:3], -1.0, None, ALU.mult).then_inc(negmax, 1)
                dve.wait_ge(exp_done, e + 1)
                do(dve.reciprocal(sm[:, x, 12:15], sm[:, x, 8:11]))
                own.wait()
                do(dve.tensor_tensor(sm[:, x, 8:11], sm[:, x, 12:15], g_d[:, u, :], ALU.mult))
                own.wait()
                for n, c in enumerate((slice(0, 128), slice(128, 416), slice(416, 704))):
                    ins = dve.tensor_scalar(s[:, c], s[:, c], sm[:, x, 8 + n:9 + n], None, ALU.mult)
                ins.then_inc(p_ready, 1)
                if u == 0:
                    take_out(NH - 2)
                    take_out(NH - 1)
            dve.wait_ge(o_mm, E // 2 + 4)
            for x in range(2):
                for p in range(2):
                    f = slice(64 * p, 64 * p + 64)
                    src = pst[f, 4, :].rearrange("p (b x k g t) -> p x k g b t", b=DEC_B, x=2, k=2, g=4)[:, x, p]
                    dst = oT[f, 4 * x:4 * x + 4, SEQ:TOK].rearrange("p g (b t) -> p g b t", t=DEC_T)
                    for g in range(4):
                        ins = dve.tensor_copy(dst[:, g], src[:, g])
                    ins.then_inc(o_taken, 1)
            split("bo", 0, 0)
            for ft in range(DT):
                dve.wait_ge(oh_done, ft + 1)
                dve.tensor_tensor(xl[:, ft, :], oT[:, ft, :], xh[:, ft, :].bitcast(F32), ALU.subtract)\
                   .then_inc(o_split, 1)
            clear(5)
            pipeline("bo", add("bo", 2, 1.0, 5), "inA3")
            norm(5, Q_G12, 4)
            ffn(3, 6)
            norm(6, Q_FIN, last=True)

        @block.gpsimd
        def _(pool):
            own = Steps(pool, pool_step)
            pool.dma_start(const[:, 0:C_PAR], I["const"]).then_inc(const_in, 16)
            pool.dma_start(const[:, C_PAR:C_PAR + 21 * 8], I["params"]).then_inc(const_in, 16)
            for dst, src in ((w_w1, "w1"), (w_a1, "a1"), (w_g1, "g1"), (w_w2, "w2"), (w_a2, "a2"),
                             (shift0, "shift0")):
                pool.dma_start(dst, I[src]).then_inc(lora_in, 16)
            pool.dma_start(w_g2a, I["g2"][0:P]).then_inc(lora_in, 16)
            pool.dma_start(w_g2b, I["g2"][P:160]).then_inc(lora_in, 16)
            pool.dma_start(expand, I["expand"]).then_inc(expand_in, 16)
            pool.dma_start(ptab[:], I["page_table"]).then_inc(table_in, 16)
            pool.dma_start(cbias[:, 2:3], I["valid"]).then_inc(att_in, 16)
            pool.dma_start(O["s_wink"][:, :, :, 0:PAST - DEC_T], I["win_k"][:, :, :, DEC_T:PAST])\
                .then_inc(win_out, 16)
            pool.dma_start(O["s_winv"][:, 0:PAST - DEC_T, :], I["win_v"][:, DEC_T:PAST, :]).then_inc(win_out, 16)
            pool.wait_ge(shifts_done, 1)
            pool.dma_start(O["shifts"], shifts).then_inc(shift_out, 16)

            for u in range(5):
                c, n, levels = (64, P, LEVELS_P) if u < 4 else (32, 32, LEVELS_D)
                if u == 4:
                    pool.wait_ge(filled[3], 4 * u + 2)
                    pool.dma_start(s0T, I["s_wkv"]).then_inc(s0_in, 16)
                for x in range(len(levels)):
                    pool.wait_ge(emptied[3], 4 * u + 1)
                    if u or x:
                        pool.wait_ge(filled[0], 9 * u + 2 + x if x else 9 * u - 2)
                    o = (C_MP if u < 4 else C_MD) + (M_UP + 1 + x) * c
                    m = const[0:n, o:o + c].unsqueeze(1).to_broadcast([n, NH, c])
                    al = AL[0:n].rearrange("p (a c) -> p a c", a=NH)[:, :, 0:c]
                    ab = ABT[0:n].rearrange("p (a c) -> p a c", a=NH)[:, :, 0:c]
                    pool.tensor_tensor(al, ab, m, ALU.mult).then_inc(al_ready, 1)
            pool.wait_ge(st_ready, 9)
            pool.dma_start(O["p_wkv"], st[:]).then_inc(wkv_out, 16)
            pool.wait_ge(emptied[2], FILLS23[0])
            seq = const[0:32, C_SEQ:C_SEQ + DEC_B].unsqueeze(2).to_broadcast([32, DEC_B, HD])
            for ft in range(DT):
                if ft >= 2:
                    pool.wait_ge(filled[2 + ft % 2], FILLS23[ft % 2] + ft // 2)
                for p in range(2):
                    o = p * 512 + ft * 64
                    ins = pool.tensor_tensor(um[ft % 2][:, p, 0, :].rearrange("p (b i) -> p b i", b=DEC_B),
                                             UU[0:32, o:o + 64].unsqueeze(1).to_broadcast([32, DEC_B, HD]), seq,
                                             ALU.mult)
                ins.then_inc(um_u_ready, 1)
            pool.wait_ge(wkv_ready, DT)
            pool.dma_start(O["s_wkv"], s0T).then_inc(wkv_out, 16)

            k = end_of("wo")
            pool.wait_ge(multiplied[0], k)
            pool.wait_ge(multiplied[1], k)
            pool.wait_ge(shift_out, 16)
            pool.dma_start(cw1, I["cw1"]).then_inc(cw_in, 16)
            k = end_of("outB1")
            pool.wait_ge(multiplied[0], k)
            pool.wait_ge(multiplied[1], k)
            pool.dma_start(cw2, I["cw2"]).then_inc(cw_in, 16)
            pool.dma_start(cpos, I["cpos"]).then_inc(cw_in, 16)
            pool.wait_ge(table_in, 16)
            with pool.Fori(0, DEC_B * NPG) as i:
                page = pool.value_load(ptab[0:1, bass.ds(i, 1)], min_val=0, max_val=I["pages"].shape[0] - 1)
                src = I["pages_c"][bass.ds(page, 1)].rearrange("o p (a t) -> p (o a) t", a=8)
                for half in range(2):
                    dst = cmpT[64 * half:64 * half + 64].rearrange("p a b c -> p (a b) c")
                    pool.dma_start(dst[:, :, bass.ds(i * PAGE + (SEQ - 16 * half), PAGE)], src)\
                        .then_inc(cache_cmp_in, 16)
            pool.wait_ge(cw_in, 48)
            for kv in range(2):
                if kv:
                    pool.wait_ge(cred_done, kv)
                pool.tensor_tensor(ctmp, cw1[:, kv], cpos[:, kv, :].unsqueeze(2).to_broadcast([P, 16, P]),
                                   ALU.mult).then_inc(cprod, 1)
            for x in range(2):
                pool.wait_ge(taken[x], STAGES["kv"][0] + 2)
            for p in range(2):
                for half in range(2):
                    pool.dma_start(cmpT[64 * half:64 * half + 64, :, p, 0:SEQ - 16 * half],
                                   kvT[64 * p:64 * p + 64, 4:8, 16 * half:SEQ]).then_inc(rows_in, 16)
            k = end_of("kv")
            pool.wait_ge(taken[0], k)
            pool.wait_ge(taken[1], k)
            pool.memset(chid[:, :, :, NBLK:NBLK + 1], 0.0).then_inc(chid_zero, 1)
            pool.dma_start(O["kv"], kvT).then_inc(kv_out, 16)
            pool.wait_ge(keys_kept, 1)
            for x in range(2):
                pool.dma_start(O["s_wink"][:, :, x, PAST - DEC_T:PAST].rearrange("b p t -> p b t"),
                               kwin[:, x, SEQ:TOK].rearrange("p (b t) -> p b t", t=DEC_T)).then_inc(win_out, 16)
            pool.wait_ge(vt_ev, 10)
            for b in range(DEC_B):
                pool.dma_start(O["s_winv"][b, PAST - DEC_T:PAST, :], v_new[DEC_T * b:DEC_T * b + DEC_T, 1, :])\
                    .then_inc(win_out, 16)
            pool.dma_start(att, I["att"]).then_inc(att_in, 16)
            k = end_of("outB2")
            pool.wait_ge(multiplied[0], k)
            pool.wait_ge(multiplied[1], k)
            pool.dma_start(wgt, I["w_gate"]).then_inc(gate_w_in, 16)
            pool.wait_ge(xn_split, DT * 4)
            pool.memset(sg[:].rearrange("p a b -> p (a b)")[:, 0:1024], 0.0).then_inc(qbd_zero, 1)
            pool.wait_ge(att_in, 32)

            def bias(hh):
                if hh >= 2:
                    pool.wait_ge(score_taken, 12 * (hh - 1))
                dst = ar(ATAB + T_DH + 640 * (hh % 2), 640)
                pool.tensor_scalar(dst, att[:, 0:640], SLOPES[head_of(hh // 2, hh % 2)], None, ALU.mult)\
                    .then_inc(bias_ready, 1)

            bias(0)
            bias(1)
            pool.wait_ge(gate_mm, 1)
            pool.dma_start(kwin_c, I["win_k"].rearrange("b p x t -> p b x t")).then_inc(caches_in, 16)
            for part in range(4):
                with pool.Fori(4 * part, 4 * part + 4) as i:
                    page = pool.value_load(ptab[0:1, bass.ds(i, 1)], min_val=0, max_val=I["pages"].shape[0] - 1)
                    pool.dma_start(kslc_c[:, bass.ds(i, 1)].rearrange("p o x t -> p (o x t)"),
                                   I["pages"][bass.ds(page, 1), :, 0:256].rearrange("o p c -> p (o c)"))\
                        .then_inc(caches_in, 16)
                    pool.dma_start(vslc_c[:, bass.ds(i, 1), :].rearrange("p o c -> p (o c)"),
                                   I["pages"][bass.ds(page, 1), :, 256:512].rearrange("o p c -> p (o c)"))\
                        .then_inc(caches_in, 16)
                bias(2 + part)
            pool.dma_start(vwin_c, I["win_v"].rearrange("b (g p) c -> p (b g) c", g=NPG)).then_inc(vwin_in, 16)
            pool.wait_ge(gates_s, 1)
            pool.dma_start(I["scratch"], gS).then_inc(gates_d_out, 16)
            pool.wait_ge(gates_d_out, 16)
            for b in range(DEC_B):
                pool.dma_start(g_d[64 * (b % 2):64 * (b % 2) + 64, b // 2, :],
                               I["scratch"].rearrange("(b t) (h c) -> b h t c", c=3, t=DEC_T)[b])\
                    .then_inc(gates_d_in, 16)
            for hh in range(6, NH):
                bias(hh)


def tiles_of(w, group):
    k, n = w.shape[-2:]
    lead = w.shape[:-2]
    x = w.reshape(*lead, k // P, P, n // P // group, group, P)
    d = len(lead)
    x = x.transpose(*range(d), d + 2, d + 1, d + 3, d + 0, d + 4)
    return np.ascontiguousarray(x).reshape(*lead, n // P // group, P, group * k)


def by_feature(v):
    return np.moveaxis(v.reshape(*v.shape[:-1], DT, P), -1, 0)


_OUTS = {"y": (P, DT, TOK), "shifts": (P, DT, 9), "p_wkv": (P, DT, HD), "s_wkv": (P, DT, DEC_B, HD),
         "kv": (P, 12, TOK), "s_wink": (DEC_B, P, 2, PAST), "s_winv": (DEC_B, PAST, 256)}


def kernel(**inputs):
    import concourse.bacc as bacc
    from concourse.bass_utils import run_bass_kernel_spmd

    a = {k: np.asarray(v) for k, v in inputs.items()}
    n_pool = a["cache_cs"].shape[0]
    head_order = [head_of(i, p) for i in range(DT) for p in range(2)]
    cols = np.concatenate([np.arange(h * HD, h * HD + HD) for h in head_order])
    const, expand, att, valid = constants()

    x = np.concatenate([a["x_prompt"].reshape(SEQ, D), a["x_sample"].reshape(DEC_B * DEC_T, D)])
    w_in = a["ffn_w_in"].reshape(4, DT, P, 2, FT, P).transpose(0, 4, 2, 3, 1, 5).reshape(4, FT, P, 2048)
    w_out = a["ffn_w_out"].reshape(4, FT, P, DT, P).transpose(0, 3, 2, 1, 4).reshape(4, DT, P, DFF)
    rkv = a["rw_w_rkv"][0]
    w_rk = rkv[:2].reshape(2, DT, P, DT, P).transpose(3, 2, 0, 1, 4).reshape(DT, P, 2048)
    kv_w = a["kv_w"].reshape(D, 6, 256)[:, [2, 4, 0, 1, 3, 5]].reshape(D, 1536)
    b_in = a["b_w_in"][0]
    cache = a["cache_cs"].reshape(n_pool, PAGE, 4, 2, P)
    pages = np.concatenate([
        cache[:, :, 2].transpose(0, 3, 2, 1).reshape(n_pool, P, 2 * PAGE),
        cache[:, :, 3].reshape(n_pool, PAGE, 256)], axis=2)
    pages_c = a["cache_cs"].reshape(n_pool, PAGE, 4, 2, 2, HD)[:, :, 0:2].transpose(0, 5, 2, 3, 4, 1)
    win = a["cache_win"].reshape(DEC_B, PAST, 2, 256)
    params = np.concatenate([a["norm_g"].reshape(6, D), a["kv_norm_g"][None], a["final_g"][None], a["rw_mu"][0],
                             a["rw_w0"], a["rw_a0"], a["rw_k_k"], a["rw_k_a"], a["rw_r_k"].reshape(1, D),
                             a["rw_lnx_w"], a["rw_lnx_b"]])
    arrays = {
        "x": by_feature(x).transpose(0, 2, 1),
        "w_in": w_in, "w_out": w_out, "w_rk": w_rk,
        "w_v": tiles_of(rkv[2], 2), "w_o": tiles_of(a["rw_w_o"][0], 2),
        "w_kv": tiles_of(kv_w, 2), "w_q": tiles_of(b_in[:, :D][:, cols], 2),
        "w_bo": tiles_of(a["b_w_o"][0][cols], 2),
        "w_gate": b_in[:, D:].reshape(DT, P, 48).transpose(1, 0, 2),
        "w1": a["rw_w1"][0].reshape(DT, P, 64).transpose(1, 0, 2),
        "a1": a["rw_a1"][0].reshape(DT, P, 64).transpose(1, 0, 2),
        "g1": a["rw_g1"][0].reshape(DT, P, 160).transpose(1, 0, 2),
        "w2": a["rw_w2"][0], "a2": a["rw_a2"][0], "g2": a["rw_g2"][0],
        "shift0": by_feature(a["state_shift"][0]).transpose(0, 2, 1),
        "s_wkv": a["state_wkv"][0].reshape(DEC_B, DT, 2, HD, HD).transpose(2, 4, 1, 0, 3).reshape(P, DT, DEC_B, HD),
        "const": const[:, :C_PAR], "params": by_feature(params).reshape(P, 21 * 8),
        "expand": expand, "att": att, "valid": valid,
        "pages": pages, "pages_c": pages_c.reshape(n_pool, HD, 8 * PAGE), "page_table": a["page_table"].reshape(1, DEC_B * NPG),
        "win_k": win[:, :, 0].reshape(DEC_B, PAST, 2, P).transpose(0, 3, 2, 1), "win_v": win[:, :, 1],
        "cw1": a["cmp_w1"].reshape(2, 2, 16, HD, P).transpose(1, 3, 0, 2, 4).reshape(P, 2, 16, P),
        "cw2": a["cmp_w2"].transpose(1, 0, 2), "cpos": a["cmp_pos"].reshape(2, 2, 16, HD).transpose(1, 3, 0, 2).reshape(P, 2, 16),
    }
    nc = bacc.Bacc("TRN2", target_bir_lowering=False, num_devices=1)
    in_map, I, O = {}, {}, {}
    for name, v in arrays.items():
        v = np.ascontiguousarray(v)
        in_map[f"in_{name}"] = v
        I[name] = nc.dram_tensor(f"in_{name}", v.shape, mybir.dt.from_np(v.dtype), kind="ExternalInput").ap()
    I["scratch"] = nc.dram_tensor("scratch", (DEC_B * DEC_T, 48), F32, kind="Internal").ap()
    for name, shape in _OUTS.items():
        O[name] = nc.dram_tensor(f"out_{name}", shape, F32, kind="ExternalOutput").ap()
    program(nc, I, O)
    r = run_bass_kernel_spmd(nc, [in_map], core_ids=[0]).results[0]
    r = {name: np.asarray(r[f"out_{name}"]) for name in _OUTS}

    y = r["y"].transpose(2, 1, 0).reshape(TOK, D)
    shifts = r["shifts"].transpose(2, 1, 0).reshape(9, D)
    p_wkv = r["p_wkv"].reshape(2, HD, DT, HD).transpose(2, 0, 3, 1).reshape(1, 1, NH, HD, HD)
    s_wkv = r["s_wkv"].reshape(2, HD, DT, DEC_B, HD).transpose(3, 2, 0, 4, 1).reshape(1, DEC_B, NH, HD, HD)
    kv = r["kv"].transpose(2, 1, 0).reshape(TOK, 6, NKV, HD)
    cs, win_new = kv[:, [2, 3, 0, 4]], kv[:, [1, 5]]
    s_win = np.stack([r["s_wink"].transpose(0, 3, 2, 1).reshape(DEC_B, PAST, NKV, HD),
                      r["s_winv"].reshape(DEC_B, PAST, NKV, HD)], axis=2)
    return (np.ascontiguousarray(y[:SEQ]).reshape(1, SEQ, D), np.ascontiguousarray(y[SEQ:]).reshape(DEC_B, DEC_T, D),
            shifts[0:1].reshape(1, 1, D), p_wkv, np.ascontiguousarray(cs[:SEQ])[None],
            np.ascontiguousarray(win_new[:SEQ])[None], shifts[1:].reshape(1, DEC_B, D), s_wkv,
            np.ascontiguousarray(cs[SEQ:]).reshape(DEC_B, DEC_T, 4, NKV, HD), s_win)
```
